# Optimizing a Trainium2 kernel written in Bass

```python
import math
import jax
import jax.numpy as jnp
from jax import lax
import numpy as np

D_MODEL = 1024
BATCH = 1
SEQ = 2048
DEPTH = 1
DEC_BATCH = 8
DEC_SEQ = 16
PAST_LEN = 1024

CHUNK = 64
N_BAND = 8
A_WIN = N_BAND * CHUNK
D_MIX = D_MODEL
GROUP_W = D_MIX // 4
H_A = 4
DH_A = GROUP_W // H_A
REL_CLIP = 128
H_B = 4
DH_B = GROUP_W // H_B
H_C = 4
P_C = GROUP_W // H_C
G_C = 2
N_C = 128
CONV_C = 4
XBC_W = GROUP_W + 2 * G_C * N_C
G_D = 4
DG_D = GROUP_W // G_D
SPAT = 128
D_FF = ((8 * D_MODEL // 3 + 127) // 128) * 128
CONV_F = 3
IN_SIZES = (GROUP_W, GROUP_W, GROUP_W, GROUP_W, GROUP_W, GROUP_W, GROUP_W, H_B, H_B, GROUP_W, XBC_W, H_C, GROUP_W, GROUP_W)
W_IN_COLS = sum(IN_SIZES)
EPS = 1e-6
NEG = -1e30

kernel_name = 'hybrid_chunk_streaming_encoder_step'

def _split_cols(a, sizes):
    out, start = [], 0
    for s in sizes:
        out.append(a[..., start:start + s])
        start += s
    return out

def _rmsnorm(x, g):
    xf = x.astype(jnp.float32)
    y = xf * lax.rsqrt(jnp.mean(jnp.square(xf), axis=-1, keepdims=True) + EPS)
    return (y * g.astype(jnp.float32)).astype(x.dtype)

def _layernorm(x, g):
    xf = x.astype(jnp.float32)
    mu = jnp.mean(xf, axis=-1, keepdims=True)
    var = jnp.mean(jnp.square(xf - mu), axis=-1, keepdims=True)
    return ((xf - mu) * lax.rsqrt(var + EPS) * g.astype(jnp.float32)).astype(x.dtype)

def _causal_dwconv(x, buf, w, b):
    t = x.shape[1]
    width = w.shape[0]
    xp = jnp.concatenate([buf.astype(x.dtype), x], axis=1)
    y = b + w[0] * xp[:, 0:t]
    for j in range(1, width):
        y = y + w[j] * xp[:, j:j + t]
    return y, xp[:, xp.shape[1] - (width - 1):]

def _to_chunks(a, nc, length):
    return jnp.moveaxis(a.reshape(a.shape[0], nc, length, *a.shape[2:]), 1, 0)

def _from_chunks(a):
    a = jnp.moveaxis(a, 0, 1)
    return a.reshape(a.shape[0], a.shape[1] * a.shape[2], *a.shape[3:])

def _band_attention(q, k, v, k_hist, v_hist, rel_bias):
    bsz, t, h, dh = q.shape
    p = k_hist.shape[1]
    nq = -(-t // CHUNK)
    tp = nq * CHUNK
    pad_new = ((0, 0), (0, tp - t), (0, 0), (0, 0))
    hist_pad = jnp.zeros((bsz, A_WIN - p, h, dh), q.dtype)
    k_all = jnp.concatenate([hist_pad, k_hist.astype(q.dtype), jnp.pad(k, pad_new)], axis=1)
    v_all = jnp.concatenate([hist_pad, v_hist.astype(q.dtype), jnp.pad(v, pad_new)], axis=1)
    slot = jnp.arange(A_WIN + tp)
    valid = (slot >= A_WIN - p) & (slot < A_WIN + t)
    qc = jnp.pad(q, pad_new).reshape(bsz, nq, CHUNK, h, dh)
    kc = k_all.reshape(bsz, nq + N_BAND, CHUNK, h, dh)
    vc = v_all.reshape(bsz, nq + N_BAND, CHUNK, h, dh)
    vm = valid.reshape(nq + N_BAND, CHUNK)
    k_band = jnp.concatenate([kc[:, j:j + nq] for j in range(N_BAND + 1)], axis=2)
    v_band = jnp.concatenate([vc[:, j:j + nq] for j in range(N_BAND + 1)], axis=2)
    m_band = jnp.concatenate([vm[j:j + nq] for j in range(N_BAND + 1)], axis=1)
    band = (N_BAND + 1) * CHUNK
    dist = A_WIN + jnp.arange(CHUNK)[:, None] - jnp.arange(band)[None, :]
    bias = rel_bias.astype(jnp.float32)[:, jnp.clip(dist, -REL_CLIP, REL_CLIP) + REL_CLIP]
    s = jnp.einsum('bnqhd,bnkhd->bnhqk', qc, k_band).astype(jnp.float32) * (dh ** -0.5) + bias
    s = jnp.where(m_band[None, :, None, None, :], s, NEG)
    pr = jax.nn.softmax(s, axis=-1).astype(v.dtype)
    o = jnp.einsum('bnhqk,bnkhd->bnqhd', pr, v_band)
    return o.reshape(bsz, tp, h * dh)[:, :t]

def _mlstm(q, k, v, ig, lf, c0, n0, m0):
    bsz, t, h, d = q.shape
    length = min(t, CHUNK)
    nc = t // length
    causal = jnp.tril(jnp.ones((length, length), dtype=bool))[None, :, :, None]

    def step(carry, inp):
        c, n, m = carry
        qc, kc, vc, ic, fc = inp
        b = jnp.cumsum(fc, axis=1)
        dmat = jnp.where(causal, b[:, :, None] - b[:, None] + ic[:, None], -jnp.inf)
        m_t = jnp.maximum(b + m[:, None], jnp.max(dmat, axis=2))
        wqk = jnp.exp(dmat - m_t[:, :, None]) * jnp.einsum('bthd,bshd->btsh', qc, kc)
        inter = jnp.exp(b + m[:, None] - m_t)
        num = inter[..., None] * jnp.einsum('bthd,bhde->bthe', qc, c) + jnp.einsum('btsh,bshe->bthe', wqk, vc)
        den = inter * jnp.einsum('bthd,bhd->bth', qc, n) + jnp.sum(wqk, axis=2)
        hout = num / jnp.maximum(jnp.abs(den), jnp.exp(-m_t))[..., None]
        m_last = m_t[:, -1]
        decay = jnp.exp(b[:, -1] + m - m_last)
        ws = jnp.exp(b[:, -1:] - b + ic - m_last[:, None])
        c = decay[..., None, None] * c + jnp.einsum('bsh,bshd,bshe->bhde', ws, kc, vc)
        n = decay[..., None] * n + jnp.einsum('bsh,bshd->bhd', ws, kc)
        return (c, n, m_last), hout

    f32 = jnp.float32
    inp = tuple(_to_chunks(a.astype(f32), nc, length) for a in (q, k, v, ig, lf))
    (c, n, m), hs = lax.scan(step, (c0.astype(f32), n0.astype(f32), m0.astype(f32)), inp)
    return _from_chunks(hs), c, n, m

def _ssd(x, dt, a, bm, cm, h0):
    t = x.shape[1]
    length = min(t, CHUNK)
    nc = t // length
    causal = jnp.tril(jnp.ones((length, length), dtype=bool))[None, :, :, None]

    def step(h, inp):
        xc, dtc, bc, cc = inp
        cs = jnp.cumsum(dtc * a, axis=1)
        dec = jnp.exp(jnp.where(causal, cs[:, :, None] - cs[:, None], -jnp.inf))
        cb = jnp.einsum('bthn,bshn->btsh', cc, bc)
        y = jnp.einsum('btsh,bshp->bthp', cb * dec * dtc[:, None], xc) + jnp.exp(cs)[..., None] * jnp.einsum('bthn,bhpn->bthp', cc, h)
        wl = jnp.exp(cs[:, -1:] - cs) * dtc
        h = jnp.exp(cs[:, -1])[..., None, None] * h + jnp.einsum('bsh,bshp,bshn->bhpn', wl, xc, bc)
        return h, y

    f32 = jnp.float32
    inp = tuple(_to_chunks(z.astype(f32), nc, length) for z in (x, dt, bm, cm))
    h, ys = lax.scan(step, h0.astype(f32), inp)
    return _from_chunks(ys), h

def _spatial_gate(u, v, w_s, b_s):
    bsz, t, _ = v.shape
    nk = -(-t // SPAT)
    tp = nk * SPAT
    vp = jnp.pad(v, ((0, 0), (0, tp - t), (0, 0))).reshape(bsz, nk, SPAT, G_D, DG_D)
    wm = w_s * jnp.tril(jnp.ones((SPAT, SPAT), w_s.dtype))
    f = jnp.einsum('gts,bnsgc->bntgc', wm, vp) + b_s.T[:, :, None]
    return u * f.reshape(bsz, tp, GROUP_W)[:, :t]

def _layer(x, c, k_hist, v_hist, b_c, b_n, b_m, c_ssm, c_conv, f_conv,
           w_ada, b_ada, g_mix, g_ffn, w_in, w_out, a_rel_bias,
           b_i_bias, b_f_bias, b_norm_g,
           c_conv_w, c_conv_b, c_dt_bias, c_a_log, c_d_skip, c_norm_g,
           d_norm_g, d_w_s, d_b_s,
           f_w_gate, f_w_up, f_conv_w, f_conv_b, f_w_down):
    bsz, t, _ = x.shape
    dt_x = x.dtype
    mod = jax.nn.silu(c) @ w_ada + b_ada
    sh1, sc1, gt1, sh2, sc2, gt2 = jnp.split(mod[:, None, :], 6, axis=-1)
    h = _rmsnorm(x, g_mix) * (1 + sc1) + sh1
    proj = h @ w_in
    qa, ka, va, qb, kb, vb, ob, ib, fb, zc, xbc, dtc, ud, vd = _split_cols(proj, IN_SIZES)

    qa = qa.reshape(bsz, t, H_A, DH_A)
    ka = ka.reshape(bsz, t, H_A, DH_A)
    va = va.reshape(bsz, t, H_A, DH_A)
    y_a = _band_attention(qa, ka, va, k_hist, v_hist, a_rel_bias).astype(dt_x)
    keep = min(A_WIN, t)
    new_k = ka[:, t - keep:]
    new_v = va[:, t - keep:]

    igate = ib.astype(jnp.float32) + b_i_bias
    logf = jax.nn.log_sigmoid(fb.astype(jnp.float32) + b_f_bias)
    hb, new_bc, new_bn, new_bm = _mlstm(qb.reshape(bsz, t, H_B, DH_B),
                                        kb.reshape(bsz, t, H_B, DH_B) * (DH_B ** -0.5),
                                        vb.reshape(bsz, t, H_B, DH_B), igate, logf, b_c, b_n, b_m)
    hb = _layernorm(hb, b_norm_g.reshape(H_B, DH_B)).reshape(bsz, t, GROUP_W)
    y_b = (jax.nn.sigmoid(ob) * hb).astype(dt_x)

    xbc, new_conv = _causal_dwconv(xbc, c_conv, c_conv_w, c_conv_b)
    xbc = jax.nn.silu(xbc)
    xs, bm, cm = _split_cols(xbc, (GROUP_W, G_C * N_C, G_C * N_C))
    rep = H_C // G_C
    bm = jnp.repeat(bm.reshape(bsz, t, G_C, N_C), rep, axis=2)
    cm = jnp.repeat(cm.reshape(bsz, t, G_C, N_C), rep, axis=2)
    dt = jax.nn.softplus(dtc.astype(jnp.float32) + c_dt_bias)
    a = -jnp.exp(c_a_log.astype(jnp.float32))
    xs = xs.reshape(bsz, t, H_C, P_C)
    yc, new_ssm = _ssd(xs, dt, a, bm, cm, c_ssm)
    yc = (yc + c_d_skip[:, None] * xs).reshape(bsz, t, GROUP_W)
    y_c = _rmsnorm((yc * jax.nn.silu(zc)).astype(dt_x), c_norm_g)

    ud = jax.nn.gelu(ud)
    vd = _layernorm(jax.nn.gelu(vd), d_norm_g)
    y_d = _spatial_gate(ud, vd, d_w_s, d_b_s).astype(dt_x)

    mix = jnp.concatenate([y_a, y_b, y_c, y_d], axis=-1) @ w_out
    x = x + gt1 * mix

    h2 = _rmsnorm(x, g_ffn) * (1 + sc2) + sh2
    g = h2 @ f_w_gate
    u = h2 @ f_w_up
    gconv, new_fconv = _causal_dwconv(g, f_conv, f_conv_w, f_conv_b)
    x = x + gt2 * ((jax.nn.silu(gconv) * u) @ f_w_down)
    return x, (new_k, new_v, new_bc, new_bn, new_bm, new_ssm, new_conv, new_fconv, vd)

def setup_inputs(seed: int = 0) -> dict:
    key = jax.random.key(seed)
    ks = iter(jax.random.split(key, 48))
    f32 = jnp.float32

    def nrm(shape, s=1.0):
        return s * jax.random.normal(next(ks), shape, f32)

    a_cache = min(A_WIN, PAST_LEN)
    dt0 = jnp.exp(jax.random.uniform(next(ks), (DEPTH, H_C), f32, math.log(1e-3), math.log(1e-1)))
    return {
        'x_prompt': nrm((BATCH, SEQ, D_MODEL)),
        'x_sample': nrm((DEC_BATCH, DEC_SEQ, D_MODEL)),
        'c_prompt': nrm((BATCH, D_MODEL)),
        'c_sample': nrm((DEC_BATCH, D_MODEL)),
        'cache_a_k': nrm((DEPTH, DEC_BATCH, a_cache, H_A, DH_A)),
        'cache_a_v': nrm((DEPTH, DEC_BATCH, a_cache, H_A, DH_A)),
        'state_b_c': nrm((DEPTH, DEC_BATCH, H_B, DH_B, DH_B), 0.1),
        'state_b_n': nrm((DEPTH, DEC_BATCH, H_B, DH_B), 0.1),
        'state_b_m': nrm((DEPTH, DEC_BATCH, H_B)),
        'state_c_ssm': nrm((DEPTH, DEC_BATCH, H_C, P_C, N_C), 0.1),
        'state_c_conv': nrm((DEPTH, DEC_BATCH, CONV_C - 1, XBC_W)),
        'state_ffn_conv': nrm((DEPTH, DEC_BATCH, CONV_F - 1, D_FF)),
        'w_ada': nrm((DEPTH, D_MODEL, 6 * D_MODEL), D_MODEL ** -0.5),
        'b_ada': nrm((DEPTH, 6 * D_MODEL), 0.02),
        'g_norm_mix': 1.0 + nrm((DEPTH, D_MODEL), 0.05),
        'g_norm_ffn': 1.0 + nrm((DEPTH, D_MODEL), 0.05),
        'w_in': nrm((DEPTH, D_MODEL, W_IN_COLS), D_MODEL ** -0.5),
        'w_out': nrm((DEPTH, D_MIX, D_MODEL), D_MIX ** -0.5),
        'a_rel_bias': nrm((DEPTH, H_A, 2 * REL_CLIP + 1), 0.1),
        'b_i_bias': nrm((DEPTH, H_B), 0.1),
        'b_f_bias': jnp.linspace(3.0, 6.0, H_B, dtype=f32)[None] + nrm((DEPTH, H_B), 0.1),
        'b_norm_g': 1.0 + nrm((DEPTH, GROUP_W), 0.05),
        'c_conv_w': nrm((DEPTH, CONV_C, XBC_W), CONV_C ** -0.5),
        'c_conv_b': nrm((DEPTH, XBC_W), 0.02),
        'c_dt_bias': dt0 + jnp.log(-jnp.expm1(-dt0)),
        'c_a_log': jnp.log(jax.random.uniform(next(ks), (DEPTH, H_C), f32, 1.0, 16.0)),
        'c_d_skip': 1.0 + nrm((DEPTH, H_C), 0.1),
        'c_norm_g': 1.0 + nrm((DEPTH, GROUP_W), 0.05),
        'd_norm_g': 1.0 + nrm((DEPTH, GROUP_W), 0.05),
        'd_w_s': nrm((DEPTH, G_D, SPAT, SPAT), 0.5 * SPAT ** -0.5),
        'd_b_s': 1.0 + nrm((DEPTH, G_D, SPAT), 0.1),
        'f_w_gate': nrm((DEPTH, D_MODEL, D_FF), D_MODEL ** -0.5),
        'f_w_up': nrm((DEPTH, D_MODEL, D_FF), D_MODEL ** -0.5),
        'f_conv_w': nrm((DEPTH, CONV_F, D_FF), CONV_F ** -0.5),
        'f_conv_b': nrm((DEPTH, D_FF), 0.02),
        'f_w_down': nrm((DEPTH, D_FF, D_MODEL), D_FF ** -0.5),
        'g_final': 1.0 + nrm((D_MODEL,), 0.05),
    }

def reference(x_prompt, x_sample, c_prompt, c_sample,
              cache_a_k, cache_a_v, state_b_c, state_b_n, state_b_m,
              state_c_ssm, state_c_conv, state_ffn_conv,
              w_ada, b_ada, g_norm_mix, g_norm_ffn, w_in, w_out, a_rel_bias,
              b_i_bias, b_f_bias, b_norm_g,
              c_conv_w, c_conv_b, c_dt_bias, c_a_log, c_d_skip, c_norm_g,
              d_norm_g, d_w_s, d_b_s,
              f_w_gate, f_w_up, f_conv_w, f_conv_b, f_w_down, g_final):
    f32 = jnp.float32
    bp = x_prompt.shape[0]
    xp = x_prompt
    xs = x_sample
    p_states = []
    s_states = []
    for l in range(DEPTH):
        params = (w_ada[l], b_ada[l], g_norm_mix[l], g_norm_ffn[l], w_in[l], w_out[l], a_rel_bias[l],
                  b_i_bias[l], b_f_bias[l], b_norm_g[l],
                  c_conv_w[l], c_conv_b[l], c_dt_bias[l], c_a_log[l], c_d_skip[l], c_norm_g[l],
                  d_norm_g[l], d_w_s[l], d_b_s[l],
                  f_w_gate[l], f_w_up[l], f_conv_w[l], f_conv_b[l], f_w_down[l])
        z_hist = jnp.zeros((bp, 0, H_A, DH_A), xp.dtype)
        xp, sp = _layer(xp, c_prompt, z_hist, z_hist,
                        jnp.zeros((bp, H_B, DH_B, DH_B), f32), jnp.zeros((bp, H_B, DH_B), f32),
                        jnp.zeros((bp, H_B), f32), jnp.zeros((bp, H_C, P_C, N_C), f32),
                        jnp.zeros((bp, CONV_C - 1, XBC_W), xp.dtype),
                        jnp.zeros((bp, CONV_F - 1, D_FF), xp.dtype), *params)
        xs, ss = _layer(xs, c_sample, cache_a_k[l], cache_a_v[l], state_b_c[l], state_b_n[l],
                        state_b_m[l], state_c_ssm[l], state_c_conv[l], state_ffn_conv[l], *params)
        p_states.append(sp)
        s_states.append(ss)
    y_prompt = _rmsnorm(xp, g_final)
    y_sample = _rmsnorm(xs, g_final)
    p_a_k = jnp.stack([s[0] for s in p_states])
    p_a_v = jnp.stack([s[1] for s in p_states])
    p_b_c = jnp.stack([s[2] for s in p_states])
    p_b_n = jnp.stack([s[3] for s in p_states])
    p_b_m = jnp.stack([s[4] for s in p_states])
    p_c_ssm = jnp.stack([s[5] for s in p_states])
    p_c_conv = jnp.stack([s[6] for s in p_states])
    p_ffn_conv = jnp.stack([s[7] for s in p_states])
    s_a_k = jnp.stack([s[0] for s in s_states])
    s_a_v = jnp.stack([s[1] for s in s_states])
    s_b_c = jnp.stack([s[2] for s in s_states])
    s_b_n = jnp.stack([s[3] for s in s_states])
    s_b_m = jnp.stack([s[4] for s in s_states])
    s_c_ssm = jnp.stack([s[5] for s in s_states])
    s_c_conv = jnp.stack([s[6] for s in s_states])
    s_ffn_conv = jnp.stack([s[7] for s in s_states])
    s_d_v = jnp.stack([s[8] for s in s_states])
    return (y_prompt, y_sample, p_a_k, p_a_v, p_b_c, p_b_n, p_b_m, p_c_ssm, p_c_conv, p_ffn_conv,
            s_a_k, s_a_v, s_b_c, s_b_n, s_b_m, s_c_ssm, s_c_conv, s_ffn_conv, s_d_v)


_drawn_inputs = setup_inputs


def setup_inputs(seed=0):
    import zlib

    import numpy as np

    out = dict(_drawn_inputs(seed))
    spreads = {}
    factors = {'a_rel_bias': 33.474,
     'b_norm_g': 7.425,
     'c_d_skip': 6.037,
     'c_norm_g': 3.989,
     'f_conv_b': 7.147,
     'cache_a_k': 3.604,
     'cache_a_v': 3.295,
     'd_b_s': 3.953}
    for name, (base, spread) in spreads.items():
        noise = np.random.default_rng([zlib.crc32(name.encode()), seed]).standard_normal(out[name].shape)
        drawn = base * np.exp(spread * noise) if base else spread * noise
        out[name] = jnp.asarray(drawn.astype(out[name].dtype))
    for name, factor in factors.items():
        out[name] = (out[name] * factor).astype(out[name].dtype)
    return out
```

```python
from contextlib import ExitStack

import concourse.bass as bass
from concourse import mybir

F32 = mybir.dt.float32
ALU = mybir.AluOpType
ACT = mybir.ActivationFunctionType
AX = mybir.AxisListType.X

P = 128
D = 1024
KD = D // P
SEQ = 2048
NT = SEQ // P
NB, TS = 8, 16
GW = 256
H, DH = 4, 64
NSTATE = 128
XW = 768
KX = XW // P
WIN = 3340
X0 = 2056
PW = WIN - XW
FF = 2816
KF = FF // P
EPS = 1e-6
NEG = -1e30
HIST = 512
BAND = HIST + P
NPAST = HIST // P

QA, KA, VA, QB, KB, VB, OB, IB, FB, ZC, DT, UD, VD = (
    0, 256, 512, 768, 1024, 1280, 1536, 1792, 1796, 1800, 2056, 2060, 2316)


def spread(ap, axis, n):
    shape = list(ap.shape)
    shape.insert(axis, n)
    return ap.unsqueeze(axis).to_broadcast(shape)


class Steps:

    def __init__(self, engine, sem):
        self.engine, self.sem, self.base, self.count, self.per_tile = engine, sem, 0, 0, None
        self.last = None

    def tile(self, i):
        if self.per_tile is None and self.count:
            self.per_tile = self.count
        if self.per_tile is not None:
            self.base = i * self.per_tile
        self.count = 0

    def __call__(self, instruction):
        self.count += 1
        instruction.then_inc(self.sem, 1)
        self.last = (self.sem, self.base + self.count)

    def on(self, engine):
        self.engine = engine
        return self

    def settle(self):
        self.engine.wait_ge(*self.last)


class Tile:

    def __init__(self, pair, parity):
        self.pair, self.parity = pair, parity
        self.i = pair * 2 + parity
        self.first = isinstance(pair, int) and self.i == 0
        self.done = self.i + 1

    def nth(self, k, per):
        return self.i * per + (k + 1)


def new_pools(nc, ctx):
    def sb(name, shape, dt=F32):
        return ctx.enter_context(nc.sbuf_tensor(name, list(shape), dt))

    def ps(name, shape, dt=F32):
        return ctx.enter_context(nc.psum_tensor(name, list(shape), dt))

    return sb, ps


def make_constants(nc, sb, sem):
    c = {
        "ident": sb("ident", [P, P]),
        "ones": sb("ones", [P, P]),
        "tri": sb("tri", [P, P]),
        "tri_s": sb("tri_s", [P, P]),
        "pick": sb("pick", [H, H, P]),
        "stream": sb("stream", [P, NB]),
        "to_prompt": sb("to_prompt", [9, P]),
        "to_sample": sb("to_sample", [9, P]),
        "minus_half": sb("minus_half", [P, H]),
        "zeros": sb("zeros", [P, KX * 3]),
        "per_width": sb("per_width", [P, H + 2]),
        "eps": sb("eps", [P, H]),
    }
    made, cut = sem("const_made"), sem("const_cut")

    def program(pool):
        g = nc.gpsimd
        for name in ("ident", "pick", "to_prompt", "to_sample", "zeros"):
            g.memset(c[name][:], 0.0).then_inc(made, 1)
        for name in ("ones", "tri", "tri_s", "stream"):
            g.memset(c[name][:], 1.0).then_inc(made, 1)
        g.memset(c["minus_half"][:], -0.5).then_inc(made, 1)
        g.memset(c["eps"][:], EPS).then_inc(made, 1)
        g.memset(c["per_width"][:, 0:H], 1.0 / DH).then_inc(made, 1)
        g.memset(c["per_width"][:, H:H + 1], 1.0 / GW).then_inc(made, 1)
        g.memset(c["per_width"][:, H + 1:H + 2], 1.0 / D).then_inc(made, 1)
        pool.wait_ge(made, 14)
        n = 0

        def cut_out(ap, pattern, op, fill, base, rows):
            nonlocal n
            g.affine_select(out=ap, in_=ap, pattern=pattern, compare_op=op, fill=fill, base=base,
                            channel_multiplier=rows).then_inc(cut, 1)
            n += 1
            return n

        cut_out(c["ident"][:], [[-1, P]], ALU.not_equal, 1.0, 0, 1)
        cut_out(c["pick"][:], [[-1, H], [0, P]], ALU.not_equal, 1.0, 0, 1)
        cut_out(c["to_prompt"][:], [[0, P]], ALU.not_equal, 1.0, 0, 1)
        ts = c["to_sample"][:].rearrange("k (b t) -> k b t", b=NB)
        cut_out(ts, [[-1, NB], [0, TS]], ALU.not_equal, 1.0, -1, 1)
        cut_out(c["tri"][:], [[1, P]], ALU.is_ge, 0.0, 0, -1)
        cut_out(c["tri_s"][:], [[1, P]], ALU.is_ge, 0.0, 0, -1)
        cut_out(c["stream"][:], [[-TS, NB]], ALU.is_ge, 0.0, 0, 1)
        pool.wait_ge(cut, n)
        t3 = c["tri_s"][:].rearrange("p (b t) -> p b t", b=NB)
        cut_out(t3, [[-TS, NB], [0, TS]], ALU.is_ge, 0.0, 0, 1)
        cut_out(c["stream"][:], [[TS, NB]], ALU.is_ge, 0.0, TS - 1, -1)
        pool.wait_ge(cut, n)

    return c, program


def modulation(nc, sem, A, S, c, const_program, keep, w_in_sb):
    with ExitStack() as ctx:
        sb, ps = new_pools(nc, ctx)
        NS = 1 + NB
        NG = 6 * D // 512
        cond, cond_e, cond_r = sb("cond", [NS, D]), sb("cond_e", [NS, D]), sb("cond_r", [NS, D])
        cond_t = sb("cond_t", [P, KD, NS])
        w = [sb(f"w_ada{j}", [P, KD, 512]) for j in range(2)]
        bias, mod = sb("b_ada", [NS, 2, 512]), sb("mod", [NS, 6 * D])
        g_col = sb("g_col", [P, 2, KD])
        keep["ffn_gate"] = sb("ffn_gate", [P, 2, D])
        cond_ps = ps("cond_ps", [P, 512])
        mod_ps = ps("mod_ps", [P, 2, 512])
        col_ps = ps("col_ps", [P, 512])
        gate_ps = ps("gate_ps", [P, 4, 512])
        s_in, s_g = sem("mod_inputs"), sem("mod_gains")
        s_w = [sem(f"w_ada_loaded{j}") for j in range(2)]
        s_e, s_c, s_ct, s_ctc = sem("cond_exp"), sem("cond_silu"), sem("cond_turned"), sem("cond_kept")
        s_m, s_mk, s_col, s_gate, s_colk, s_gatek = (
            sem("mod_group"), sem("mod_kept"), sem("mod_cols"), sem("gate_rows"), sem("cols_kept"), sem("gates_kept"))
        s_v = sem("mod_dve")
        s_win, s_gout = sem("w_in_loaded"), sem("ffn_gate_stored")
        w_view = A["w_ada"][0].rearrange("(k p) n -> p k n", p=P)

        block = ctx.enter_context(nc.Block())

        @block.gpsimd
        def _(pool):
            const_program(pool)

        @block.sync
        def _(sp):
            sp.dma_start(cond[0:1, :], A["c_prompt"]).then_inc(s_in, 16)
            sp.dma_start(cond[1:NS, :], A["c_sample"]).then_inc(s_in, 16)
            for j in range(NG):
                if j >= 2:
                    sp.wait_ge(s_m, j - 1)
                    sp.wait_ge(s_mk, j - 1)
                sp.dma_start(bias[:, j % 2, :], A["b_ada"][0, j * 512:(j + 1) * 512].partition_broadcast(NS)
                             ).then_inc(s_w[j % 2], 16)
                sp.dma_start(w[j % 2][:], w_view[:, :, j * 512:(j + 1) * 512]).then_inc(s_w[j % 2], 16)
            w_in = A["w_in"][0].rearrange("(k p) n -> k p n", p=P)
            for k in range(KD):
                sp.dma_start(w_in_sb[:, k * WIN:(k + 1) * WIN], w_in[k]).then_inc(s_win, 16)
            sp.wait_ge(s_gatek, 8)
            sp.dma_start(S["ffn_gate"], keep["ffn_gate"][:]).then_inc(s_gout, 16)
            sp.wait_ge(s_gout, 16)

        @block.scalar
        def _(act):
            act.dma_start(g_col[:, 0, :], A["g_norm_mix"][0].rearrange("(k p) -> p k", p=P),
                          allow_slow_non_contiguous=True).then_inc(s_g, 16)
            act.dma_start(g_col[:, 1, :], A["g_norm_ffn"][0].rearrange("(k p) -> p k", p=P),
                          allow_slow_non_contiguous=True).then_inc(s_g, 16)
            act.wait_ge(s_in, 32)
            nc.scalar.activation(cond_e[:], cond[:], ACT.Silu).then_inc(s_e, 1)

        @block.vector
        def _(dve):
            dve.wait_ge(s_ct, 1)
            nc.vector.tensor_copy(cond_t[:], cond_ps[:, 0:KD * NS].rearrange("p (k s) -> p k s", k=KD)
                                  ).then_inc(s_ctc, 1)
            for j in range(NG):
                dve.wait_ge(s_m, j + 1)
                nc.vector.tensor_tensor(mod[:, j * 512:(j + 1) * 512], mod_ps[0:NS, j % 2, :],
                                        bias[:, j % 2, :], ALU.add).then_inc(s_mk, 1)
            dve.wait_ge(s_col, 1)
            dve.wait_ge(s_g, 32)
            cols = col_ps[:, 0:4 * KD * NS].rearrange("p (a k s) -> p a k s", a=4, k=KD)
            for a, norm in enumerate(("mix", "ffn")):
                nc.vector.tensor_copy(keep[norm + "_shift"][:], cols[:, 2 * a]).then_inc(s_colk, 1)
                nc.vector.tensor_scalar(keep[norm + "_scale"][:], cols[:, 2 * a + 1], 1.0, None, ALU.add
                                        ).then_inc(s_v, 1)
                dve.wait_ge(s_v, 2 * a + 1)
                nc.vector.tensor_tensor(keep[norm + "_scale"][:], keep[norm + "_scale"][:],
                                        spread(g_col[:, a, :], 2, NS), ALU.mult).then_inc(s_v, 1)
            n = 0
            for gate in ("mix_gate", "ffn_gate"):
                for who in range(2):
                    for half in range(2):
                        n += 1
                        dve.wait_ge(s_gate, n)
                        nc.vector.tensor_copy(keep[gate][:, who, half * 512:(half + 1) * 512],
                                              gate_ps[:, (n - 1) % 4, :]).then_inc(s_gatek, 1)
            dve.wait_ge(s_gatek, n)
            dve.wait_ge(s_colk, 2)
            dve.wait_ge(s_v, 4)

        @block.tensor
        def _(pe):
            t = nc.tensor
            pe.wait_ge(s_e, 1)
            pe.wait_ge(sem.constants_cut, 9)
            for k in range(KD):
                last = t.transpose(cond_ps[:, k * NS:(k + 1) * NS], cond_e[:, k * P:(k + 1) * P], c["ident"][0:NS, 0:NS])
            last.then_inc(s_ct, 1)
            pe.wait_ge(s_ctc, 1)
            for j in range(NG):
                pe.wait_ge(s_w[j % 2], 32 * (j // 2 + 1))
                if j >= 2:
                    pe.wait_ge(s_mk, j - 1)
                for k in range(KD):
                    last = t.matmul(mod_ps[0:NS, j % 2, :], cond_t[:, k, :], w[j % 2][:, k, :],
                                    start=(k == 0), stop=(k == KD - 1))
                last.then_inc(s_m, 1)
            pe.wait_ge(s_mk, NG)
            at = 0
            for piece in (0, 1, 3, 4):
                for k in range(KD):
                    last = t.transpose(col_ps[:, at:at + NS], mod[:, piece * D + k * P:piece * D + (k + 1) * P],
                                       c["ident"][0:NS, 0:NS])
                    at += NS
            last.then_inc(s_col, 1)
            n = 0
            for piece in (2, 5):
                for who in ("to_prompt", "to_sample"):
                    for half in range(2):
                        if n >= 4:
                            pe.wait_ge(s_gatek, n - 3)
                        at = piece * D + half * 512
                        t.matmul(gate_ps[:, n % 4, :], c[who][:], mod[:, at:at + 512], start=True, stop=True
                                 ).then_inc(s_gate, 1)
                        n += 1


def projection(nc, sem, A, S, c, keep, w_in_sb):
    with ExitStack() as ctx:
        sb, ps = new_pools(nc, ctx)
        x = [sb(f"x{j}", [P, D]) for j in range(2)]
        xn = [sb(f"xn{j}", [P, D]) for j in range(2)]
        squares = sb("squares", [P, D])
        ht = [sb(f"ht{j}", [P, KD, P]) for j in range(2)]
        out = [sb(f"proj_out{j}", [P, PW]) for j in range(2)]
        xout = [sb(f"xbc_out{j}", [P, KX, P]) for j in range(2)]
        ss, mean, rstd = sb("ss", [P, 2]), sb("mean", [P, 2]), sb("rstd", [P, 2])
        turned = ps("turned", [P, KD, P])
        unit = ps("unit", [P, 4, 512])
        s_x = [sem(f"x_loaded{j}") for j in range(2)]
        s_ss, s_mean, s_rstd, s_xn = sem("p1_squares"), sem("p1_mean"), sem("p1_rstd"), sem("p1_normed")
        s_t, s_ht, s_u, s_uk = sem("p1_turned"), sem("p1_ht"), sem("p1_unit"), sem("p1_unit_kept")
        s_o = [sem(f"p1_stored{j}") for j in range(2)]
        s_win, s_z = sem["w_in_loaded"], sem("p1_zero_columns")
        s_tmp = sem("p1_mod_products")

        groups = [(0, 1, 512, 0, 0), (512, 1, 512, 0, 512), (1024, 1, 384, 0, 1024), (1408, 1, 392, 0, 1408),
                  (1800, 2, 256, 1024, 1800), (3080, 1, 260, 0, 2312)]
        NU = len(groups) + 2

        def w_group(k, g):
            start, blocks, width, stride, _ = groups[g]
            at = k * WIN + start
            if blocks == 1:
                return w_in_sb[:, at:at + width]
            return w_in_sb[:, at:at + blocks * stride].rearrange("p (a n) -> p a n", a=blocks)[:, :, 0:width]

        block = ctx.enter_context(nc.Block())

        @block.sync
        def _(sp):
            xp = A["x_prompt"][0]
            xsamp = A["x_sample"].rearrange("b t d -> (b t) d")
            sp.dma_start(S["xbc"][:, :, 0:3], c["zeros"][:].rearrange("p (k j) -> p k j", k=KX)).then_inc(s_z, 16)
            sp.dma_start(x[0][:], xp[0:P, :]).then_inc(s_x[0], 16)
            sp.dma_start(x[1][:], xp[P:2 * P, :]).then_inc(s_x[1], 16)

            def store(t, sample=False):
                j = t.parity
                sp.wait_ge(s_uk, t.nth(NU - 1, NU))
                if sample:
                    sp.dma_start(S["proj"][SEQ:SEQ + P, :], out[j][:]).then_inc(s_o[j], 16)
                    sp.dma_start(S["xbc_s"][:, :, :], xout[j][:]).then_inc(s_o[j], 16)
                else:
                    sp.dma_start(S["proj"][bass.ds(t.i * P, P), :], out[j][:]).then_inc(s_o[j], 16)
                    sp.dma_start(S["xbc"][:, :, bass.ds(t.i * P + 3, P)], xout[j][:]).then_inc(s_o[j], 16)

            def both(pair, last=False):
                for j in range(2):
                    t = Tile(pair, j)
                    if last and j == 1:
                        store(t)
                        continue
                    sp.wait_ge(s_xn, t.nth(0, 1))
                    if last:
                        sp.dma_start(x[0][:], xsamp).then_inc(s_x[0], 16)
                    else:
                        sp.dma_start(x[j][:], xp[bass.ds(t.i * P + 2 * P, P), :]).then_inc(s_x[j], 16)
                    store(t)

            both(0)
            with sp.Fori(1, NT // 2 - 1) as pair:
                both(pair)
            both(NT // 2 - 1, last=True)
            store(Tile(NT // 2, 0), sample=True)
            sp.wait_ge(s_z, 16)
            sp.wait_ge(s_o[0], 32 * (NT // 2 + 1))
            sp.wait_ge(s_o[1], 32 * (NT // 2))

        @block.scalar
        def _(act):
            def squares_of(t):
                j = t.parity
                act.wait_ge(s_x[j], t.pair * 16 + 16)
                if not t.first:
                    act.wait_ge(s_ss, t.i * 1)
                nc.scalar.activation(squares[:], x[j][:], ACT.Square, accum_out=ss[:, j:j + 1]).then_inc(s_ss, 1)

            def keep_units(t, first_pair):
                j = t.parity
                if not first_pair:
                    act.wait_ge(s_o[j], t.pair * 32)
                for u in range(NU):
                    act.wait_ge(s_u, t.nth(u, NU))
                    if u < len(groups):
                        width, to = groups[u][1] * groups[u][2], groups[u][4]
                        nc.scalar.activation(out[j][:, to:to + width], unit[:, u % 4, 0:width], ACT.Copy
                                             ).then_inc(s_uk, 1)
                    else:
                        v = u - len(groups)
                        nc.scalar.activation(xout[j][:, 3 * v:3 * v + 3, :],
                                             unit[:, u % 4, 0:3 * P].rearrange("p (k t) -> p k t", k=3), ACT.Copy
                                             ).then_inc(s_uk, 1)

            def tiles(pair, first_pair=False, more=True):
                squares_of(Tile(pair, 1))
                keep_units(Tile(pair, 0), first_pair)
                if more:
                    squares_of(Tile(pair + 1, 0))
                keep_units(Tile(pair, 1), first_pair)

            squares_of(Tile(0, 0))
            tiles(0, first_pair=True)
            with act.Fori(1, NT // 2) as pair:
                tiles(pair)
            keep_units(Tile(NT // 2, 0), False)

        @block.gpsimd
        def _(pool):
            def rstd_of(t):
                j = t.parity
                pool.wait_ge(s_ss, t.done)
                nc.gpsimd.tensor_tensor(mean[:, j:j + 1], ss[:, j:j + 1], c["per_width"][:, H + 1:H + 2], ALU.mult
                                        ).then_inc(s_mean, 1)
                pool.wait_ge(s_mean, t.nth(0, 2))
                nc.gpsimd.tensor_tensor(mean[:, j:j + 1], mean[:, j:j + 1], c["eps"][:, 0:1], ALU.add
                                        ).then_inc(s_mean, 1)
                pool.wait_ge(s_mean, t.nth(1, 2))
                nc.gpsimd.tensor_tensor(rstd[:, j:j + 1], mean[:, j:j + 1], c["minus_half"][:, 0:1], ALU.pow
                                        ).then_inc(s_rstd, 1)

            rstd_of(Tile(0, 0))
            rstd_of(Tile(0, 1))
            with pool.Fori(1, NT // 2) as pair:
                rstd_of(Tile(pair, 0))
                rstd_of(Tile(pair, 1))
            rstd_of(Tile(NT // 2, 0))

        @block.vector
        def _(dve):
            def normalise(t):
                j = t.parity
                if not t.first:
                    pass
                dve.wait_ge(s_rstd, t.done)
                nc.vector.tensor_scalar(xn[j][:], x[j][:], rstd[:, j:j + 1], None, ALU.mult).then_inc(s_xn, 1)

            def keep_ht(t, sample=False, wait_used=True):
                j = t.parity
                dve.wait_ge(s_t, t.done)
                if wait_used:
                    dve.wait_ge(s_u, (t.i - 1) * NU)
                for k in range(KD):
                    if not sample:
                        ins = nc.vector.tensor_scalar(ht[j][:, k, :], turned[:, k, :], keep["mix_scale"][:, k, 0:1],
                                                      keep["mix_shift"][:, k, 0:1], ALU.mult, ALU.add)
                        if k == KD - 1:
                            ins.then_inc(s_ht, 1)
                    else:
                        wide = [P, NB, TS]
                        v = ht[j][:, k, :].rearrange("p (b t) -> p b t", b=NB)
                        nc.vector.tensor_tensor(v, turned[:, k, :].rearrange("p (b t) -> p b t", b=NB),
                                                keep["mix_scale"][:, k, 1:].unsqueeze(2).to_broadcast(wide),
                                                ALU.mult).then_inc(s_tmp, 1)
                        dve.wait_ge(s_tmp, k + 1)
                        ins = nc.vector.tensor_tensor(v, v, keep["mix_shift"][:, k, 1:].unsqueeze(2).to_broadcast(wide),
                                                      ALU.add)
                        if k == KD - 1:
                            ins.then_inc(s_ht, 1)

            def tile(t, first_use, sample=False):
                normalise(t)
                keep_ht(t, sample, not first_use)

            tile(Tile(0, 0), True)
            tile(Tile(0, 1), True)
            with dve.Fori(1, NT // 2) as pair:
                tile(Tile(pair, 0), False)
                tile(Tile(pair, 1), False)
            tile(Tile(NT // 2, 0), False, sample=True)

        @block.tensor
        def _(pe):
            def turn(t):
                j = t.parity
                pe.wait_ge(s_xn, t.done)
                if not t.first:
                    pe.wait_ge(s_ht, t.i * 1)
                for k in range(KD):
                    last = nc.tensor.transpose(turned[:, k, :], xn[j][:, k * P:(k + 1) * P], c["ident"][:])
                last.then_inc(s_t, 1)

            def project(t):
                j = t.parity
                pe.wait_ge(s_ht, t.done)
                for u in range(NU):
                    if not (t.first and u < 4):
                        pe.wait_ge(s_uk, t.i * NU + (u - 3))
                    if u < len(groups):
                        width, blocks = groups[u][2], groups[u][1]
                        dst = unit[:, u % 4, 0:width * blocks]
                        if blocks > 1:
                            dst = dst.rearrange("p (a n) -> p a n", a=blocks)
                        for k in range(KD):
                            last = nc.tensor.matmul(dst, ht[j][:, k, :], w_group(k, u), start=(k == 0),
                                                    stop=(k == KD - 1))
                    else:
                        for v in range(3):
                            col = X0 + (3 * (u - len(groups)) + v) * P
                            for k in range(KD):
                                last = nc.tensor.matmul(unit[:, u % 4, v * P:(v + 1) * P],
                                                        w_in_sb[:, k * WIN + col:k * WIN + col + P], ht[j][:, k, :],
                                                        start=(k == 0), stop=(k == KD - 1))
                    last.then_inc(s_u, 1)

            turn(Tile(0, 0))
            pe.wait_ge(s_win, 16 * KD)

            def tiles(pair):
                turn(Tile(pair, 1))
                project(Tile(pair, 0))
                turn(Tile(pair + 1, 0))
                project(Tile(pair, 1))

            tiles(0)
            with pe.Fori(1, NT // 2) as pair:
                tiles(pair)
            project(Tile(NT // 2, 0))


def rel_bias_rows(nc, sem, A, S):
    with ExitStack() as ctx:
        sb, _ = new_pools(nc, ctx)
        rev, ext = sb("rel_rev", [H, 257]), sb("rel_ext", [H, 768])
        s_in, s_e, s_row, s_rel = sem("rel_in"), sem("rel_extended"), sem("rel_row_stored"), sem("rel_stored")
        block = ctx.enter_context(nc.Block())

        @block.sync
        def _(sp):
            sp.dma_start(rev[:], A["a_rel_bias_reversed"][0]).then_inc(s_in, 16)
            sp.wait_ge(s_e, 2)
            sp.dma_start(S["rel_row"], ext[:]).then_inc(s_row, 16)
            sp.wait_ge(s_row, 16)
            for h in range(H):
                sp.dma_start(S["rel"][h], S["rel_row"][h].partition_broadcast(P)).then_inc(s_rel, 16)
            sp.wait_ge(s_rel, 16 * H)

        @block.vector
        def _(dve):
            dve.wait_ge(s_in, 16)
            nc.vector.tensor_copy(ext[:, 0:512], rev[:, 0:1].to_broadcast([H, 512])).then_inc(s_e, 1)
            dve.wait_ge(s_e, 1)
            nc.vector.tensor_copy(ext[:, 511:768], rev[:, 0:257]).then_inc(s_e, 1)


def rel_tile(S, rows, cols):
    flat = S["rel"].rearrange("h q u -> h (q u)")[:, 127:127 + P * 767]
    return flat.rearrange("h (q j) -> q h j", j=767)[rows, :, cols]


def sample_attention(nc, sem, A, S, c, ya_keep):
    with ExitStack() as ctx:
        sb, ps = new_pools(nc, ctx)
        pt = sb("sa_proj", [P, 768])
        k_in, v_in = sb("k_in", [P, NB, NPAST, GW]), sb("v_in", [P, NB, NPAST, GW])
        k_t = sb("k_t", [P, 2, NB, HIST])
        k_new = sb("k_new", [P, 2, P])
        band = sb("band_s", [P, H, BAND])
        q_z = sb("q_z", [P, H, P])
        q_m = [sb(f"q_m{j}", [P, NB, P]) for j in range(2)]
        stream_row = sb("stream_row", [P, NB, P])
        score, prob = sb("score_s", [P, BAND]), sb("prob_s", [P, BAND])
        prob_t = sb("prob_t_s", [P, BAND])
        wide, own = sb("wide_s", [P, NB, DH]), sb("own_s", [P, DH])
        nmax, total, inv = sb("nmax_s", [P, H]), sb("total_s", [P, H]), sb("inv_s", [P, H])
        turn_ps = ps("sa_turn", [P, 2, 512])
        s_ps = ps("sa_score", [P, 1024])
        p_ps = ps("sa_prob_t", [P, 1024])
        o_ps, n_ps = ps("sa_out", [P, 512]), ps("sa_new", [P, 512])
        s_in, s_k, s_v, s_band = sem("sa_proj_loaded"), sem("sa_k_loaded"), sem("sa_v_loaded"), sem("sa_band_loaded")
        s_neg, s_row, s_z = sem("sa_band_masked"), sem("sa_stream_row"), sem("sa_q_zero")
        s_qt, s_q, s_kt, s_kk = sem("sa_qk_turned"), sem("sa_qk_kept"), sem("sa_k_turned"), sem("sa_k_kept")
        s_qm, s_s, s_mx, s_p, s_pt, s_ptk, s_o, s_dve = (
            sem("sa_q_masked"), sem("sa_scores"), sem("sa_max"), sem("sa_probs"), sem("sa_probs_turned"),
            sem("sa_probs_kept"), sem("sa_out_done"), sem("sa_dve"))
        s_used = sem("sa_out_used")
        block = ctx.enter_context(nc.Block())

        @block.sync
        def _(sp):
            sp.dma_start(pt[:], S["proj"][SEQ:SEQ + P, 0:768]).then_inc(s_in, 16)
            for b in range(NB):
                sp.dma_start(k_in[:, b], A["cache_a_k"][0, b].rearrange("(n p) h d -> p n (h d)", p=P)).then_inc(s_k, 16)
            for b in range(NB):
                sp.dma_start(v_in[:, b], A["cache_a_v"][0, b].rearrange("(n p) h d -> p n (h d)", p=P)).then_inc(s_v, 16)
            sp.wait_ge(s_neg, 1)
            for b in range(NB):
                rows = slice(b * TS, (b + 1) * TS)
                sp.dma_start(band[rows, :, 0:HIST], rel_tile(S, slice(0, TS), slice(0, HIST))).then_inc(s_band, 16)
                sp.dma_start(band[rows, :, HIST + b * TS:HIST + (b + 1) * TS],
                             rel_tile(S, slice(0, TS), slice(HIST, HIST + TS))).then_inc(s_band, 16)

        @block.gpsimd
        def _(pool):
            nc.gpsimd.memset(band[:], NEG).then_inc(s_neg, 1)
            nc.gpsimd.memset(q_z[:], 0.0).then_inc(s_z, 1)
            nc.gpsimd.memset(stream_row[:], 0.0).then_inc(s_row, 1)
            pool.wait_ge(s_row, 1)
            sr = stream_row[:].rearrange("p n (b t) -> p n b t", b=NB)
            nc.gpsimd.affine_select(out=sr, in_=sr, pattern=[[1, NB], [-1, NB], [0, TS]], compare_op=ALU.not_equal,
                                    fill=1.0, base=0, channel_multiplier=0).then_inc(s_row, 1)

        @block.tensor
        def _(pe):
            t = nc.tensor
            pe.wait_ge(s_in, 16)
            for a in range(4):
                last = t.transpose(turn_ps[:, 0, a * P:(a + 1) * P], pt[:, a * P:(a + 1) * P], c["ident"][:])
            last.then_inc(s_qt, 1)
            n = 0
            pe.wait_ge(s_k, 16 * NB)
            for b in range(NB):
                for pair in range(2):
                    n += 1
                    if n >= 2:
                        pe.wait_ge(s_kk, n - 2) if n > 2 else None
                    if n == 2:
                        pe.wait_ge(s_q, 3)
                    for m in range(NPAST):
                        last = t.transpose(turn_ps[:, n % 2, m * P:(m + 1) * P], k_in[:, b, m, pair * P:(pair + 1) * P],
                                           c["ident"][:])
                    last.then_inc(s_kt, 1)
            pe.wait_ge(s_kk, 2 * NB)
            pe.wait_ge(s_v, 16 * NB)
            for h in range(H):
                pe.wait_ge(s_qm, h + 1)
                if h:
                    pe.wait_ge(s_mx, h)
                for b in range(NB):
                    t.matmul(s_ps[:, 0:HIST], q_m[h % 2][:, b, :], k_t[:, h // 2, b, :], start=(b == 0),
                             stop=(b == NB - 1))
                t.matmul(s_ps[:, HIST:BAND], q_z[:, h, :], k_new[:, h // 2, :], start=True, stop=True).then_inc(s_s, 1)
                pe.wait_ge(s_p, h + 1)
                for m in range(NPAST + 1):
                    last = t.transpose(p_ps[:, m * P:(m + 1) * P], prob[:, m * P:(m + 1) * P], c["ident"][:])
                last.then_inc(s_pt, 1)
                pe.wait_ge(s_ptk, h + 1)
                if h:
                    pe.wait_ge(s_used, h)
                for m in range(NPAST):
                    t.matmul(o_ps[:].rearrange("p (b d) -> p b d", b=NB), prob_t[:, m * P:(m + 1) * P],
                             v_in[:, :, m, h * DH:(h + 1) * DH], start=(m == 0), stop=(m == NPAST - 1))
                t.matmul(n_ps[:, 0:DH], prob_t[:, HIST:BAND], pt[:, VA + h * DH:VA + (h + 1) * DH], start=True,
                         stop=True).then_inc(s_o, 1)

        @block.scalar
        def _(act):
            for n in range(1, 2 * NB + 1):
                b, pair = (n - 1) // 2, (n - 1) % 2
                act.wait_ge(s_kt, n)
                nc.scalar.activation(k_t[:, pair, b, :], turn_ps[:, n % 2, :], ACT.Copy).then_inc(s_kk, 1)
            for h in range(H):
                act.wait_ge(s_mx, h + 1)
                if h:
                    act.wait_ge(s_pt, h)
                nc.scalar.activation(prob[:], score[:], ACT.Exp, bias=nmax[:, h:h + 1], accum_out=total[:, h:h + 1]
                                     ).then_inc(s_p, 1)
                act.wait_ge(s_pt, h + 1)
                if h:
                    act.wait_ge(s_o, h)
                nc.scalar.activation(prob_t[:], p_ps[:, 0:BAND], ACT.Copy).then_inc(s_ptk, 1)

        @block.vector
        def _(dve):
            v = nc.vector
            step = Steps(dve, s_dve)
            dve.wait_ge(s_qt, 1)
            dve.wait_ge(s_z, 1)
            qk = turn_ps[:, 0, :].rearrange("p (a t) -> p a t", a=4)
            v.tensor_copy(q_z[0:64, 0:4:2, :], qk[0:64, 0:2, :]).then_inc(s_q, 1)
            v.tensor_copy(q_z[64:128, 1:4:2, :], qk[64:128, 0:2, :]).then_inc(s_q, 1)
            v.tensor_copy(k_new[:], qk[:, 2:4, :]).then_inc(s_q, 1)
            dve.wait_ge(s_q, 3)
            dve.wait_ge(s_row, 2)
            dve.wait_ge(s_band, 32 * NB)

            def mask_q(h):
                if h >= 2:
                    dve.wait_ge(s_s, h - 1)
                v.tensor_tensor(q_m[h % 2][:], spread(q_z[:, h, :], 1, NB), stream_row[:], ALU.mult).then_inc(s_qm, 1)

            mask_q(0)
            for h in range(H):
                if h + 1 < H:
                    mask_q(h + 1)
                dve.wait_ge(s_s, h + 1)
                if h:
                    dve.wait_ge(s_p, h)
                step(v.scalar_tensor_tensor(score[:], s_ps[:, 0:BAND], DH ** -0.5, band[:, h, :], ALU.mult, ALU.add))
                step.settle()
                v.tensor_reduce(nmax[:, h:h + 1], score[:], AX, ALU.max, negate=True).then_inc(s_mx, 1)
                dve.wait_ge(s_p, h + 1)
                step(v.reciprocal(inv[:, h:h + 1], total[:, h:h + 1]))
                dve.wait_ge(s_o, h + 1)
                step(v.tensor_tensor(wide[:], o_ps[:].rearrange("p (b d) -> p b d", b=NB), spread(c["stream"][:], 2, DH),
                                     ALU.mult))
                step.settle()
                step(v.tensor_reduce(own[:], wide[:].rearrange("p b d -> p d b"), AX, ALU.add))
                step.settle()
                v.tensor_tensor(own[:], own[:], n_ps[:, 0:DH], ALU.add).then_inc(s_used, 1)
                dve.wait_ge(s_used, h + 1)
                step(v.tensor_scalar(ya_keep[:, h * DH:(h + 1) * DH], own[:], inv[:, h:h + 1], None, ALU.mult))
            step.settle()


ROWS = 8
R_INTER, R_FLOOR, R_WB, R_CS, R_WC, R_A, R_NCS, R_DT = range(ROWS)


def mixers(nc, sem, A, O, S, c, keep, ya_sample):
    with ExitStack() as ctx:
        sb, ps = new_pools(nc, ctx)
        w_out = sb("w_out", [P, KD, D])
        taps_c = sb("taps_c", [P, 5, KX])
        gb, gc, gd = sb("gb", [P, GW]), sb("gc", [P, GW]), sb("gd", [P, GW])
        skip = sb("skip", [P, H])
        row_par = sb("row_par", [H, 8])
        ws_t = sb("ws_t", [P, H, P])
        bs = sb("bs", [P, H])
        pt = [sb(f"pt{j}", [P, PW]) for j in range(2)]
        xt = [sb(f"xt{j}", [P, KX * NB * (TS + 3)]) for j in range(2)]
        xr = sb("xr", [P, D])
        acc, xc = sb("acc", [P, KX, P]), sb("xc", [P, KX, P])
        uv, sz = sb("uv", [P, 2 * GW]), sb("sz", [P, GW])
        stats, mv, rs_d = sb("stats", [P, 6]), sb("mv", [P, 2]), sb("rs_d", [P, 1])
        vn, fd = sb("vn", [P, GW]), sb("fd", [P, GW])
        u_in, soft = sb("u_in", [H, 2, P]), sb("soft", [H, 2, P])
        sp_ = sb("sp_", [H, 2, P])
        ig, nb, la, mx = sb("ig", [H, P]), sb("nb", [H, P]), sb("la", [H, P]), sb("mx", [H, P])
        row, arg, bc = sb("row", [H, ROWS, P]), sb("arg", [H, 5, P]), sb("bc", [H, 2, P])
        col = sb("col", [P, ROWS, H])
        qkb = sb("qkb", [DH, 2 * H, P])
        dec_arg = sb("dec_arg", [P, 2 * H, P])
        wt, gt = sb("wt", [P, H, P]), sb("gt", [P, H, P])
        ws_in = wt
        v1, v1w = sb("v1", [P, H, DH + 1]), sb("v1w", [P, H, DH + 1])
        xs_b = sb("xs_b", [P, 2 * GW])
        xdt, xwl, xsk = sb("xdt", [P, H, DH]), sb("xwl", [P, H, DH]), sb("xsk", [P, H, DH])
        to = sb("to", [P, GW])
        nums, den = sb("nums", [P, H, DH + 1]), sb("den", [P, H])
        hb, sq, sums = sb("hb", [P, H, DH]), sb("sq", [P, H, DH]), sb("sums", [P, H])
        ssb, rsb_m, rsb = sb("ssb", [P, H]), sb("rsb_m", [P, H]), sb("rsb", [P, H])
        yz, ssc, rsc_m, rsc = sb("yz", [P, GW]), sb("ssc", [P, 1]), sb("rsc_m", [P, 1]), sb("rsc", [P, 1])
        y = sb("y_mix", [P, D])
        yt = sb("yt", [P, KD, P])
        prod = sb("prod2", [P, D])
        ss2, rs2_m, rs2 = sb("ss2", [P, 1]), sb("rs2_m", [P, 1]), sb("rs2", [P, 1])
        big = [ps(f"big{j}", [P, 1024]) for j in range(2)]
        turn = ps("turn", [P, 1024])
        out_ps, row_ps = ps("out_ps", [P, 512]), ps("row_ps", [P, 512])

        names = """rows_turned qk_turned scores_done cols_turned pv_done bcast_done qkb_turned cb_done qk_done
            xsb_turned nums_done ys_done state_ps_done f_done y_turned out_done h2_turned
            load_done0 load_done1 tile_stored
            gelu_done tap0_done softplus_done xc_done rows_exp prob_done prob_kept gate_tanh qkb_kept dec_exp xsb_kept
            sq_c_done yt_kept sq2_done xn2_done h2_kept
            v1_copied v1w_done xd_done rstd_d_done dec_masked rstd_b_done rstd_c_done rstd_2_done xwl_done skip_done
            qk_kept rows_in conv_done max_done args_done rows_done cols_kept var_done vn_done ya_done dec_ready
            w_done g_done yb_centred yz_done x2_done y_ready states_done probs_turned
            dve_step act_step pool_step params_loaded w_out_loaded spatial_turned alog_exp setup_dve
            vall_loaded xres_loaded""".split()
        E = {n: sem("m_" + n) for n in names}
        s_load = [E["load_done0"], E["load_done1"]]
        s_final, s_final2, s_ones = sem("m_final_stored"), sem("m_sample_stored"), sem("m_ones")
        N_PARAMS = 16
        steps_of = {}

        def engines(scope):
            sample = scope["sample"]
            band, k_t, v_all = scope.get("band"), scope.get("k_t"), scope.get("v_all")
            q_z, score, prob_t = (scope.get(n) for n in ("q_z", "score", "prob_t"))
            prob = score
            nmax, total, inv = (scope.get(n) for n in ("nmax", "total", "inv"))
            cst, hst, m0 = scope["cst"], scope["hst"], scope["m0"]
            mask = scope["mask"]
            batch = NB if sample else 1

            def x_view(t, j):
                flat = xt[t.parity]
                if sample:
                    return flat[:, 0:KX * NB * (TS + 3)].rearrange("p (k b t) -> p k b t", k=KX, b=NB)[:, :, :, j:j + TS]
                return flat[:, 0:KX * (P + 3)].rearrange("p (k t) -> p k t", k=KX)[:, :, j:j + P]

            def chan(ap, k):
                a = ap[:, k, :]
                return a.rearrange("p (b t) -> p b t", b=NB) if sample else a

            def blocks(i):
                return (i + 1) if isinstance(i, int) and i < NPAST else NPAST + 1

            def start_tile(engine, t):
                if not t.first:
                    engine.wait_ge(E["h2_kept"], t.i * 1)

            def tensor_tile(pe, t):
                T, j, i = nc.tensor, t.parity, t.i
                p = pt[j]
                pe.wait_ge(s_load[j], t.pair * 32 + 32)
                start_tile(pe, t)
                for n, at in enumerate((IB, FB, DT)):
                    last = T.transpose(row_ps[0:H, n * P:(n + 1) * P], p[:, at:at + H], c["ident"][:])
                last.then_inc(E["rows_turned"], 1)
                if not sample:
                    for a in range(4):
                        last = T.transpose(turn[:, a * P:(a + 1) * P], p[:, a * P:(a + 1) * P], c["ident"][:])
                    last.then_inc(E["qk_turned"], 1)
                    nk = blocks(i)
                    first_key = (i - (nk - 1)) * P

                    def scores(h):
                        n1 = min(nk * P, 512)
                        if h >= 2:
                            pe.wait_ge(E["max_done"], t.nth(h - 2, H))
                        ins = T.matmul(big[h % 2][:, 0:n1], q_z[:, h, :], k_t[:, h // 2, bass.ds(first_key, n1)],
                                       start=True, stop=True)
                        if nk > 4:
                            ins = T.matmul(big[h % 2][:, 512:640], q_z[:, h, :],
                                           k_t[:, h // 2, bass.ds(first_key + 512, P)], start=True, stop=True)
                        ins.then_inc(E["scores_done"], 1)

                    pe.wait_ge(E["qk_kept"], t.nth(2, 3))
                    scores(0)
                    scores(1)
                pe.wait_ge(E["rows_done"], t.done)
                for r in range(ROWS):
                    last = T.matmul(row_ps[:, 384 + r * H:384 + (r + 1) * H], row[:, r, :], c["ident"][0:H, 0:H],
                                    start=True, stop=True)
                last.then_inc(E["cols_turned"], 1)
                if not sample:
                    for h in range(H):
                        pe.wait_ge(E["prob_done"], t.nth(h, H))
                        if h:
                            pe.wait_ge(E["prob_kept"], t.nth(h - 1, H))
                        for m in range(nk):
                            last = T.transpose(turn[:, m * P:(m + 1) * P], prob[h % 2][:, m * P:(m + 1) * P], c["ident"][:])
                        last.then_inc(E["probs_turned"], 1)
                        if h + 2 < H:
                            scores(h + 2)
                        pe.wait_ge(E["prob_kept"], t.nth(h, H))
                        pe.wait_ge(E["vall_loaded"], 16)
                        for m in range(nk):
                            if isinstance(i, int):
                                v = v_all[:, i - (nk - 1) + m, h * DH:(h + 1) * DH]
                            else:
                                v = v_all[:, bass.ds(i + (m - (nk - 1)), 1), h * DH:(h + 1) * DH].rearrange("p o d -> p (o d)")
                            last = T.matmul(out_ps[:, h * DH:(h + 1) * DH], prob_t[h % 2][:, m * P:(m + 1) * P], v,
                                            start=(m == 0), stop=(m == nk - 1))
                        last.then_inc(E["pv_done"], 1)
                pe.wait_ge(E["args_done"], t.done)
                for r in range(2):
                    for h in range(H):
                        T.matmul(big[0][:, r * 512 + h * P:r * 512 + (h + 1) * P], c["pick"][:, h, :], bc[:, r, :],
                                 start=True, stop=True)
                for n, (r, rows) in enumerate(((R_INTER, DH), (R_CS, P))):
                    for h in range(H):
                        at = 768 + (n * H + h) * batch
                        last_cols = row[:, r, TS - 1:P:TS] if sample else row[:, r, P - 1:P]
                        last = T.matmul(big[1][0:rows, at:at + batch], c["pick"][:, h, 0:rows], last_cols, start=True,
                                        stop=True)
                last.then_inc(E["bcast_done"], 1)
                if not sample:
                    pe.wait_ge(E["prob_kept"], t.nth(H - 1, H))
                for n, at in enumerate((QB, KB)):
                    for h in range(H):
                        last = T.matmul(turn[0:DH, (n * H + h) * P:(n * H + h + 1) * P],
                                        p[:, at + h * DH:at + (h + 1) * DH], c["ident"][:], start=True, stop=True)
                last.then_inc(E["qkb_turned"], 1)
                pe.wait_ge(E["xc_done"], t.done)
                for g in range(2):
                    last = T.matmul(big[1][:, 512 + g * P:512 + (g + 1) * P], xc[:, 2 + g, :], xc[:, 4 + g, :],
                                    start=True, stop=True)
                last.then_inc(E["cb_done"], 1)
                pe.wait_ge(E["qkb_kept"], t.done)
                for h in range(H):
                    last = T.matmul(big[1][:, h * P:(h + 1) * P], qkb[:, H + h, :], qkb[:, h, :], start=True, stop=True)
                last.then_inc(E["qk_done"], 1)
                for k in range(4):
                    last = T.transpose(turn[:, k * P:(k + 1) * P], xc[:, k, :], c["ident"][:])
                last.then_inc(E["xsb_turned"], 1)
                pe.wait_ge(E["w_done"], t.done)
                pe.wait_ge(E["v1_copied"], t.done)
                if not sample:
                    pe.wait_ge(E["ya_done"], t.done)
                W1 = DH + 1
                for h in range(H):
                    T.matmul(out_ps[:, h * W1:(h + 1) * W1], wt[:, h, :], v1[:, h, :], start=True, stop=True)
                if not sample:
                    for h in range(H):
                        last = T.matmul(row_ps[:, h * W1:(h + 1) * W1], qkb[:, h, :], cst[:, h, :], start=True, stop=True)
                    last.then_inc(E["nums_done"], 1)
                else:
                    for h in range(H):
                        if h:
                            pe.wait_ge(scope["n2_used"], h)
                        for half in range(2):
                            last = T.matmul(big[0][:, half * 512:half * 512 + 4 * W1].rearrange("p (b e) -> p b e", b=4),
                                            qkb[:, h, :], cst[:, h, 4 * half:4 * half + 4, :], start=True, stop=True)
                        last.then_inc(scope["n2_done"], 1)
                pe.wait_ge(E["g_done"], t.done)
                pe.wait_ge(E["xd_done"], t.done)
                pe.wait_ge(E["xsb_kept"], t.done)
                for h in range(H):
                    last = T.matmul(turn[:, 512 + h * DH:512 + (h + 1) * DH], gt[:, h, :], xdt[:, h, :], start=True,
                                    stop=True)
                if not sample:
                    for h in range(H):
                        last = T.matmul(turn[:, 768 + h * DH:768 + (h + 1) * DH], xc[:, 4 + h // 2, :], hst[:, h, :],
                                        start=True, stop=True)
                    last.then_inc(E["ys_done"], 1)
                    pe.wait_ge(E["v1w_done"], t.done)
                    pe.wait_ge(E["xwl_done"], t.done)
                    for h in range(H):
                        T.matmul(big[0][0:DH, h * W1:(h + 1) * W1], p[:, KB + h * DH:KB + (h + 1) * DH], v1w[:, h, :],
                                 start=True, stop=True)
                    for h in range(H):
                        last = T.matmul(big[0][:, 512 + h * DH:512 + (h + 1) * DH], xs_b[:, GW + h // 2 * P:GW + (h // 2 + 1) * P],
                                        xwl[:, h, :], start=True, stop=True)
                    last.then_inc(E["state_ps_done"], 1)
                else:
                    last.then_inc(E["ys_done"], 1)
                    for h in range(H):
                        pe.wait_ge(scope["n2_used"], H + h)
                        T.matmul(big[0][:, 0:512].rearrange("p (b e) -> p b e", b=NB), xc[:, 4 + h // 2, :],
                                 hst[:, h, :, :], start=True, stop=True).then_inc(scope["n2_done"], 1)
                    for h in range(H):
                        pe.wait_ge(scope["n2_used"], 2 * H + h)
                        pe.wait_ge(scope["vws_done"], h + 1)
                        for half in range(2):
                            last = T.matmul(big[0][0:DH, half * 512:half * 512 + 4 * W1], p[:, KB + h * DH:KB + (h + 1) * DH],
                                            scope["vws"][h % 2][:, 4 * half * W1:(4 * half + 4) * W1], start=True, stop=True)
                        last.then_inc(scope["n2_done"], 1)
                    for h in range(H):
                        pe.wait_ge(scope["n2_used"], 3 * H + h)
                        pe.wait_ge(scope["vws_done"], H + h + 1)
                        T.matmul(big[0][:, 0:512], xs_b[:, GW + h // 2 * P:GW + (h // 2 + 1) * P],
                                 scope["vws"][h % 2][:, 0:512], start=True, stop=True).then_inc(scope["n2_done"], 1)
                pe.wait_ge(E["vn_done"], t.done)
                for g in range(H):
                    last = T.matmul(big[1][:, g * DH:(g + 1) * DH], scope["ws_t"][:, g, :], vn[:, g * DH:(g + 1) * DH],
                                    start=True, stop=True)
                last.then_inc(E["f_done"], 1)
                pe.wait_ge(E["y_ready"], t.done)
                for k in range(KD):
                    last = T.transpose(turn[:, k * P:(k + 1) * P], y[:, k * P:(k + 1) * P], c["ident"][:])
                last.then_inc(E["y_turned"], 1)
                pe.wait_ge(E["w_out_loaded"], 16)
                pe.wait_ge(E["yt_kept"], t.done)
                if sample:
                    pe.wait_ge(scope["n2_used"], 4 * H)
                else:
                    pe.wait_ge(E["states_done"], t.done)
                for half in range(2):
                    for k in range(KD):
                        last = T.matmul(big[0][:, half * 512:(half + 1) * 512], yt[:, k, :],
                                        w_out[:, k, half * 512:(half + 1) * 512], start=(k == 0), stop=(k == KD - 1))
                last.then_inc(E["out_done"], 1)
                pe.wait_ge(E["xn2_done"], t.done)
                for k in range(KD):
                    last = T.transpose(big[1][:, k * P:(k + 1) * P], prod[:, k * P:(k + 1) * P], c["ident"][:])
                last.then_inc(E["h2_turned"], 1)

            def scalar_tile(act, t, step):
                a, j, i = nc.scalar, t.parity, t.i
                p = pt[j]
                act.wait_ge(s_load[j], t.pair * 32 + 32)
                start_tile(act, t)
                step.tile(i)
                step(a.activation(uv[:], p[:, UD:UD + 2 * GW], ACT.Gelu_apprx_tanh))
                a.activation(sz[:], p[:, ZC:ZC + GW], ACT.Silu).then_inc(E["gelu_done"], 1)
                if sample:
                    act.wait_ge(scope["xt_loaded"], 16 * scope["xt_dmas"])
                for k in range(KX):
                    ins = a.activation(chan(acc, k), x_view(t, 0)[:, k], ACT.Identity, scale=taps_c[:, 0, k:k + 1],
                                       bias=taps_c[:, 4, k:k + 1])
                ins.then_inc(E["tap0_done"], 1)
                act.wait_ge(E["rows_in"], t.done)
                step(a.activation(soft[:], u_in[:], ACT.Abs))
                step.settle()
                step(a.activation(soft[:], soft[:], ACT.Exp, scale=-1.0))
                step.settle()
                a.activation(soft[:], soft[:], ACT.Ln, bias=1.0).then_inc(E["softplus_done"], 1)
                act.wait_ge(E["conv_done"], t.done)
                a.activation(xc[:], acc[:], ACT.Silu).then_inc(E["xc_done"], 1)
                act.wait_ge(E["args_done"], t.done)
                a.activation(row[:, 0:5, :], arg[:], ACT.Exp).then_inc(E["rows_exp"], 1)
                a.activation(to[:], p[:, OB:OB + GW], ACT.Tanh, scale=0.5).then_inc(E["gate_tanh"], 1)
                if not sample:
                    w = blocks(i) * P

                    def probs(h):
                        act.wait_ge(E["max_done"], t.nth(h, H))
                        a.activation(prob[h % 2][:, 0:w], score[h % 2][:, 0:w], ACT.Exp, bias=nmax[:, h:h + 1],
                                     accum_out=total[:, h:h + 1]).then_inc(E["prob_done"], 1)

                    probs(0)
                    probs(1)
                    for h in range(H):
                        act.wait_ge(E["probs_turned"], t.nth(h, H))
                        if h >= 2:
                            act.wait_ge(E["pv_done"], t.nth(h - 2, H))
                        a.activation(prob_t[h % 2][:, 0:w], turn[:, 0:w], ACT.Copy).then_inc(E["prob_kept"], 1)
                        if h + 2 < H:
                            probs(h + 2)
                act.wait_ge(E["qkb_turned"], t.done)
                a.activation(qkb[:], turn[0:DH, :].rearrange("p (a t) -> p a t", a=2 * H), ACT.Copy
                             ).then_inc(E["qkb_kept"], 1)
                act.wait_ge(E["dec_ready"], t.done)
                a.activation(dec_arg[:], dec_arg[:], ACT.Exp).then_inc(E["dec_exp"], 1)
                act.wait_ge(E["xsb_turned"], t.done)
                a.activation(xs_b[:], turn[:, 0:512], ACT.Copy).then_inc(E["xsb_kept"], 1)
                act.wait_ge(E["yz_done"], t.done)
                a.activation(xdt[:].rearrange("p h d -> p (h d)"), yz[:], ACT.Square, accum_out=ssc[:]).then_inc(E["sq_c_done"], 1)
                act.wait_ge(E["y_turned"], t.done)
                if not t.first:
                    act.wait_ge(E["tile_stored"], t.i * 32)
                a.activation(yt[:], turn[:].rearrange("p (k t) -> p k t", k=KD), ACT.Copy).then_inc(E["yt_kept"], 1)
                act.wait_ge(E["x2_done"], t.done)
                act.wait_ge(E["sq_c_done"], t.done)
                a.activation(turn[:], xr[:], ACT.Square, accum_out=ss2[:]).then_inc(E["sq2_done"], 1)
                act.wait_ge(E["rstd_2_done"], t.done)
                a.activation(prod[:], xr[:], ACT.Copy, scale=rs2[:, 0:1]).then_inc(E["xn2_done"], 1)
                act.wait_ge(E["h2_turned"], t.done)
                for k in range(KD):
                    if not sample:
                        ins = a.activation(yt[:, k, :], big[1][:, k * P:(k + 1) * P], ACT.Identity,
                                           scale=keep["ffn_scale"][:, k, 0:1], bias=keep["ffn_shift"][:, k, 0:1])
                    else:
                        for b in range(NB):
                            ins = a.activation(yt[:, k, b * TS:(b + 1) * TS], big[1][:, k * P + b * TS:k * P + (b + 1) * TS],
                                               ACT.Identity, scale=keep["ffn_scale"][:, k, 1 + b:2 + b],
                                               bias=keep["ffn_shift"][:, k, 1 + b:2 + b])
                ins.then_inc(E["h2_kept"], 1)

            def pool_tile(pool, t, step):
                g, j = nc.gpsimd, t.parity
                p = pt[j]
                pool.wait_ge(s_load[j], t.pair * 32 + 32)
                start_tile(pool, t)
                step.tile(t.i)

                def rstd(out, mid, square_sum, at, width, signal):
                    step(g.tensor_tensor(mid, square_sum, c["per_width"][:, at:at + width], ALU.mult))
                    step.settle()
                    step(g.tensor_tensor(mid, mid, c["eps"][:, 0:width], ALU.add))
                    step.settle()
                    g.tensor_tensor(out, mid, c["minus_half"][:, 0:width], ALU.pow).then_inc(E[signal], 1)

                g.tensor_tensor(v1[:, :, 0:DH], p[:, VB:VB + GW].rearrange("p (h d) -> p h d", h=H),
                                c["ones"][:, 0:1].unsqueeze(2).to_broadcast([P, H, DH]), ALU.mult
                                ).then_inc(E["v1_copied"], 1)
                pool.wait_ge(E["var_done"], t.done)
                step(g.tensor_tensor(rsc_m[:], mv[:, 1:2], c["eps"][:, 0:1], ALU.add))
                step.settle()
                g.tensor_tensor(rs_d[:], rsc_m[:], c["minus_half"][:, 0:1], ALU.pow).then_inc(E["rstd_d_done"], 1)
                pool.wait_ge(E["cols_kept"], t.done)
                pool.wait_ge(E["v1_copied"], t.done)
                g.tensor_tensor(v1w[:], v1[:], spread(col[:, R_WB, :], 2, DH + 1), ALU.mult).then_inc(E["v1w_done"], 1)
                pool.wait_ge(E["dec_exp"], t.done)
                g.tensor_tensor(dec_arg[:], dec_arg[:], spread(mask[:], 1, 2 * H), ALU.mult).then_inc(E["dec_masked"], 1)
                pool.wait_ge(E["xsb_kept"], t.done)
                xs = xs_b[:, 0:GW].rearrange("p (h d) -> p h d", h=H)
                g.tensor_tensor(xdt[:], xs, spread(col[:, R_DT, :], 2, DH), ALU.mult).then_inc(E["xd_done"], 1)
                g.tensor_tensor(xwl[:], xs, spread(col[:, R_WC, :], 2, DH), ALU.mult).then_inc(E["xwl_done"], 1)
                g.tensor_tensor(xsk[:], xs, spread(skip[:], 2, DH), ALU.mult).then_inc(E["skip_done"], 1)
                pool.wait_ge(E["yb_centred"], t.done)
                rstd(rsb[:], rsb_m[:], ssb[:], 0, H, "rstd_b_done")
                pool.wait_ge(E["sq_c_done"], t.done)
                rstd(rsc[:], rsc_m[:], ssc[:], H, 1, "rstd_c_done")
                pool.wait_ge(E["sq2_done"], t.done)
                rstd(rs2[:], rs2_m[:], ss2[:], H + 1, 1, "rstd_2_done")

            def vector_tile(dve, t, step):
                v, j, i = nc.vector, t.parity, t.i
                p = pt[j]
                dve.wait_ge(s_load[j], t.pair * 32 + 32)
                start_tile(dve, t)
                step.tile(i)
                dve.wait_ge(E["rows_turned"], t.done)
                step(v.tensor_scalar(u_in[:, 0, :], row_ps[0:H, P:2 * P], row_par[:, 1:2], -1.0, ALU.add, ALU.mult))
                step(v.tensor_scalar(ig[:], row_ps[0:H, 0:P], row_par[:, 0:1], None, ALU.add))
                v.tensor_scalar(u_in[:, 1, :], row_ps[0:H, 2 * P:3 * P], row_par[:, 2:3], None, ALU.add
                                ).then_inc(E["rows_in"], 1)
                if not sample:
                    dve.wait_ge(E["qk_turned"], t.done)
                    qk = turn[:, 0:512].rearrange("p (a t) -> p a t", a=4)
                    v.tensor_copy(q_z[0:64, 0:4:2, :], qk[0:64, 0:2, :]).then_inc(E["qk_kept"], 1)
                    v.tensor_copy(q_z[64:128, 1:4:2, :], qk[64:128, 0:2, :]).then_inc(E["qk_kept"], 1)
                    v.tensor_copy(k_t[:, :, bass.ds(i * P, P)], qk[:, 2:4, :]).then_inc(E["qk_kept"], 1)
                dve.wait_ge(E["tap0_done"], t.done)
                for tap in range(1, 4):
                    for k in range(KX):
                        ins = v.scalar_tensor_tensor(chan(acc, k), x_view(t, tap)[:, k], taps_c[:, tap, k:k + 1],
                                                     chan(acc, k), ALU.mult, ALU.add)
                    if tap < 3:
                        step(ins)
                        step.settle()
                ins.then_inc(E["conv_done"], 1)

                def scores(h):
                    w = blocks(i) * P
                    dve.wait_ge(E["scores_done"], t.nth(h, H))
                    if h >= 2:
                        dve.wait_ge(E["probs_turned"], t.nth(h - 2, H))
                    step(v.scalar_tensor_tensor(score[h % 2][:, 0:w], big[h % 2][:, 0:w], DH ** -0.5,
                                                band[:, h, BAND - w:BAND], ALU.mult, ALU.add))
                    step.settle()
                    v.tensor_reduce(nmax[:, h:h + 1], score[h % 2][:, 0:w], AX, ALU.max, negate=True
                                    ).then_inc(E["max_done"], 1)

                if not sample:
                    scores(0)
                    scores(1)
                dve.wait_ge(E["softplus_done"], t.done)
                step(v.scalar_tensor_tensor(sp_[:], u_in[:], 0.0, soft[:], ALU.max, ALU.add))
                step.settle()
                step(v.tensor_scalar(la[:], sp_[:, 1, :], row_par[:, 4:5], None, ALU.mult))
                step(v.tensor_copy(row[:, R_DT, :], sp_[:, 1, :]))
                segments = [(b * TS, (b + 1) * TS) for b in range(NB)] if sample else [(0, P)]
                for lo, hi in segments:
                    ins = v.tensor_tensor_scan(nb[:, lo:hi], c["ones"][0:H, lo:hi], sp_[:, 0, lo:hi], 0.0, ALU.mult, ALU.add)
                step(ins)
                step.settle()
                for lo, hi in segments:
                    ins = v.tensor_tensor_scan(arg[:, 3, lo:hi], c["ones"][0:H, lo:hi], la[:, lo:hi], 0.0, ALU.mult, ALU.add)
                step(v.tensor_tensor(row[:, R_A, :], ig[:], nb[:], ALU.add))
                step.settle()
                for n, (lo, hi) in enumerate(segments):
                    ins = v.tensor_tensor_scan(mx[:, lo:hi], row[:, R_A, lo:hi], row[:, R_A, lo:hi], m0[:, n:n + 1],
                                               ALU.max, ALU.max)
                step(v.tensor_copy(bc[:, 1, :], arg[:, 3, :]))
                step.settle()
                step(v.tensor_scalar(row[:, R_NCS, :], arg[:, 3, :], -1.0, None, ALU.mult))
                step(v.tensor_tensor(arg[:, 1, :], nb[:], mx[:], ALU.subtract))
                step(v.tensor_scalar(bc[:, 0, :], mx[:], -1.0, None, ALU.mult))
                if not sample:
                    step(v.tensor_scalar(arg[:, 0, :], mx[:], m0[:, 0:1], -1.0, ALU.subtract, ALU.mult))
                    step(v.tensor_scalar(arg[:, 2, :], row[:, R_A, :], mx[:, P - 1:P], None, ALU.subtract))
                    step(v.tensor_scalar(arg[:, 4, :], arg[:, 3, :], arg[:, 3, P - 1:P], -1.0, ALU.subtract, ALU.mult))
                    step.settle()
                    v.tensor_tensor(m0[:], mx[:, P - 1:P], nb[:, P - 1:P], ALU.subtract).then_inc(E["args_done"], 1)
                else:
                    def streams(ap):
                        return ap.rearrange("h (b t) -> h b t", b=NB)

                    step(v.tensor_tensor(streams(arg[:, 0, :]), spread(m0[:], 2, TS), streams(mx[:]), ALU.subtract))
                    step(v.tensor_tensor(streams(arg[:, 2, :]), streams(row[:, R_A, :]), spread(mx[:, TS - 1:P:TS], 2, TS),
                                         ALU.subtract))
                    step(v.tensor_tensor(streams(arg[:, 4, :]), spread(arg[:, 3, TS - 1:P:TS], 2, TS),
                                         streams(arg[:, 3, :]), ALU.subtract))
                    step.settle()
                    v.tensor_tensor(m0[:], mx[:, TS - 1:P:TS], nb[:, TS - 1:P:TS], ALU.subtract).then_inc(E["args_done"], 1)
                dve.wait_ge(E["gelu_done"], t.done)
                step(v.bn_stats(stats[:], uv[:, GW:2 * GW]))
                step.settle()
                dve.wait_ge(E["rows_exp"], t.done)
                v.tensor_tensor(row[:, R_WC, :], row[:, R_WC, :], row[:, R_DT, :], ALU.mult).then_inc(E["rows_done"], 1)
                v.bn_aggr(mv[:], stats[:]).then_inc(E["var_done"], 1)
                if not sample:
                    scores(2)
                    scores(3)
                dve.wait_ge(E["cols_turned"], t.done)
                v.tensor_copy(col[:], row_ps[:, 384:384 + ROWS * H].rearrange("p (r h) -> p r h", r=ROWS)
                              ).then_inc(E["cols_kept"], 1)
                dve.wait_ge(E["rstd_d_done"], t.done)
                step(v.tensor_scalar(vn[:], uv[:, GW:2 * GW], mv[:, 0:1], rs_d[:, 0:1], ALU.subtract, ALU.mult))
                step.settle()
                v.tensor_tensor(vn[:], vn[:], gd[:], ALU.mult).then_inc(E["vn_done"], 1)
                if not sample:
                    dve.wait_ge(E["pv_done"], t.nth(H - 1, H))
                    step(v.reciprocal(inv[:], total[:]))
                    step.settle()
                    v.tensor_tensor(y[:, 0:GW].rearrange("p (h d) -> p h d", h=H),
                                    out_ps[:, 0:GW].rearrange("p (h d) -> p h d", h=H), spread(inv[:], 2, DH), ALU.mult
                                    ).then_inc(E["ya_done"], 1)
                else:
                    step(v.tensor_copy(y[:, 0:GW], ya_sample[:]))
                dve.wait_ge(E["bcast_done"], t.done)
                dve.wait_ge(E["cols_kept"], t.done)
                for n, r in enumerate((R_A, R_NCS)):
                    for h in range(H):
                        at = n * 512 + h * P
                        ins = v.tensor_scalar(dec_arg[:, n * H + h, :], big[0][:, at:at + P], col[:, r, h:h + 1], 0.0,
                                              ALU.add, ALU.min)
                ins.then_inc(E["dec_ready"], 1)
                dve.wait_ge(E["dec_masked"], t.done)
                dve.wait_ge(E["qk_done"], t.done)
                v.scalar_tensor_tensor(wt[:], big[1][:, 0:512].rearrange("p (h t) -> p h t", h=H), DH ** -0.5,
                                       dec_arg[:, 0:H, :], ALU.mult, ALU.mult).then_inc(E["w_done"], 1)
                for grp in range(2):
                    ins = v.tensor_tensor(gt[:, 2 * grp:2 * grp + 2, :], spread(big[1][:, 512 + grp * P:512 + (grp + 1) * P], 1, 2),
                                          dec_arg[:, H + 2 * grp:H + 2 * grp + 2, :], ALU.mult)
                ins.then_inc(E["g_done"], 1)
                y4 = y[:].rearrange("p (g h d) -> p g h d", g=4, h=H)
                W1 = DH + 1
                if not sample:
                    dve.wait_ge(E["nums_done"], t.done)
                    step(v.tensor_tensor(nums[:], row_ps[:, 0:H * W1].rearrange("p (h e) -> p h e", h=H),
                                         spread(col[:, R_INTER, :], 2, W1), ALU.mult))
                else:
                    for h in range(H):
                        dve.wait_ge(scope["n2_done"], h + 1)
                        wide = scope["wide"]
                        for half in range(2):
                            ins = v.tensor_tensor(wide[:, 4 * half:4 * half + 4, :],
                                                  big[0][:, half * 512:half * 512 + 4 * W1].rearrange("p (b e) -> p b e", b=4),
                                                  spread(c["stream"][:, 4 * half:4 * half + 4], 2, W1), ALU.mult)
                        ins.then_inc(scope["n2_used"], 1)
                        dve.wait_ge(scope["n2_used"], h + 1)
                        step(v.tensor_reduce(nums[:, h, :], wide[:].rearrange("p b e -> p e b"), AX, ALU.add))
                        step.settle()
                    step(v.tensor_tensor(nums[:], nums[:], spread(col[:, R_INTER, :], 2, W1), ALU.mult))
                step.settle()
                step(v.tensor_tensor(nums[:], nums[:], out_ps[:, 0:H * W1].rearrange("p (h e) -> p h e", h=H), ALU.add))
                step.settle()
                dn = nums[:, :, DH]
                step(v.scalar_tensor_tensor(den[:], dn, -1.0, dn, ALU.mult, ALU.max))
                step.settle()
                step(v.tensor_tensor(den[:], den[:], col[:, R_FLOOR, :], ALU.max))
                step.settle()
                step(v.reciprocal(den[:], den[:]))
                step.settle()
                step(v.tensor_tensor(hb[:], nums[:, :, 0:DH], spread(den[:], 2, DH), ALU.mult))
                step.settle()
                step(v.tensor_reduce(sums[:], hb[:], AX, ALU.add))
                step.settle()
                step(v.tensor_scalar(sums[:], sums[:], 1.0 / DH, None, ALU.mult))
                step.settle()
                step(v.tensor_tensor(hb[:], hb[:], spread(sums[:], 2, DH), ALU.subtract))
                step.settle()
                step(v.tensor_tensor(sq[:], hb[:], hb[:], ALU.mult))
                step.settle()
                v.tensor_reduce(ssb[:], sq[:], AX, ALU.add).then_inc(E["yb_centred"], 1)
                dve.wait_ge(E["ys_done"], t.done)
                yz3 = yz[:].rearrange("p (h d) -> p h d", h=H)
                if not sample:
                    step(v.tensor_tensor(yz3, turn[:, 768:1024].rearrange("p (h d) -> p h d", h=H),
                                         spread(col[:, R_CS, :], 2, DH), ALU.mult))
                else:
                    wide = scope["wide"]
                    for h in range(H):
                        dve.wait_ge(scope["n2_done"], H + h + 1)
                        v.tensor_tensor(wide[:, :, 0:DH], big[0][:, 0:512].rearrange("p (b e) -> p b e", b=NB),
                                        spread(c["stream"][:], 2, DH), ALU.mult).then_inc(scope["n2_used"], 1)
                        dve.wait_ge(scope["n2_used"], H + h + 1)
                        step(v.tensor_reduce(yz3[:, h, :], wide[:, :, 0:DH].rearrange("p b e -> p e b"), AX, ALU.add))
                        step.settle()
                    step(v.tensor_tensor(yz3, yz3, spread(col[:, R_CS, :], 2, DH), ALU.mult))
                step.settle()
                step(v.tensor_tensor(yz[:], yz[:], turn[:, 512:768], ALU.add))
                dve.wait_ge(E["skip_done"], t.done)
                step.settle()
                step(v.tensor_tensor(yz3, yz3, xsk[:], ALU.add))
                step.settle()
                v.tensor_tensor(yz[:], yz[:], sz[:], ALU.mult).then_inc(E["yz_done"], 1)
                dve.wait_ge(E["rstd_b_done"], t.done)
                step(v.tensor_tensor(hb[:], hb[:], spread(rsb[:], 2, DH), ALU.mult))
                dve.wait_ge(E["gate_tanh"], t.done)
                step.settle()
                step(v.scalar_tensor_tensor(sq[:].rearrange("p h d -> p (h d)"), to[:], 1.0,
                                            hb[:].rearrange("p h d -> p (h d)"), ALU.add, ALU.mult))
                step.settle()
                step(v.tensor_tensor(y[:, GW:2 * GW], sq[:].rearrange("p h d -> p (h d)"), gb[:], ALU.mult))
                if not sample:
                    dve.wait_ge(E["state_ps_done"], t.done)
                    step(v.tensor_tensor(cst[:], cst[:], spread(big[1][0:DH, 768:768 + H], 2, W1), ALU.mult))
                    step(v.tensor_tensor(hst[:], hst[:], spread(big[1][:, 768 + H:768 + 2 * H], 2, DH), ALU.mult))
                    step.settle()
                    step(v.scalar_tensor_tensor(cst[:], big[0][0:DH, 0:H * W1].rearrange("p (h e) -> p h e", h=H),
                                                DH ** -0.5, cst[:], ALU.mult, ALU.add))
                    v.tensor_tensor(hst[:], hst[:], big[0][:, 512:768].rearrange("p (h e) -> p h e", h=H), ALU.add
                                    ).then_inc(E["states_done"], 1)
                else:
                    vws = scope["vws"]

                    def weigh(n):
                        h = n % H
                        if n >= 2:
                            dve.wait_ge(scope["n2_done"], 2 * H + n - 1)
                        if n < H:
                            dst = vws[n % 2][:, 0:NB * W1].rearrange("p (b e) -> p b e", b=NB)
                            v.tensor_tensor(dst, spread(v1w[:, h, :], 1, NB), spread(c["stream"][:], 2, W1), ALU.mult
                                            ).then_inc(scope["vws_done"], 1)
                        else:
                            dst = vws[n % 2][:, 0:NB * DH].rearrange("p (b e) -> p b e", b=NB)
                            v.tensor_tensor(dst, spread(xwl[:, h, :], 1, NB), spread(c["stream"][:], 2, DH), ALU.mult
                                            ).then_inc(scope["vws_done"], 1)

                    dve.wait_ge(E["v1w_done"], t.done)
                    dve.wait_ge(E["xwl_done"], t.done)
                    weigh(0)
                    weigh(1)
                    for n in range(2 * H):
                        h = n % H
                        if n < H:
                            dec = spread(big[1][0:DH, 768 + h * NB:768 + (h + 1) * NB], 2, W1)
                            step(v.tensor_tensor(cst[:, h], cst[:, h], dec, ALU.mult))
                            dve.wait_ge(scope["n2_done"], 2 * H + n + 1)
                            step.settle()
                            for half in range(2):
                                b4 = slice(4 * half, 4 * half + 4)
                                ins = v.scalar_tensor_tensor(
                                    cst[:, h, b4, :],
                                    big[0][0:DH, half * 512:half * 512 + 4 * W1].rearrange("p (b e) -> p b e", b=4),
                                    DH ** -0.5, cst[:, h, b4, :], ALU.mult, ALU.add)
                            ins.then_inc(scope["n2_used"], 1)
                        else:
                            dec = spread(big[1][:, 768 + (H + h) * NB:768 + (H + h + 1) * NB], 2, DH)
                            step(v.tensor_tensor(hst[:, h], hst[:, h], dec, ALU.mult))
                            dve.wait_ge(scope["n2_done"], 2 * H + n + 1)
                            step.settle()
                            v.tensor_tensor(hst[:, h], hst[:, h], big[0][:, 0:512].rearrange("p (b e) -> p b e", b=NB),
                                            ALU.add).then_inc(scope["n2_used"], 1)
                        if n + 2 < 2 * H:
                            weigh(n + 2)
                dve.wait_ge(E["f_done"], t.done)
                step(v.tensor_tensor(fd[:].rearrange("p (h d) -> p h d", h=H), big[1][:, 0:GW].rearrange("p (h d) -> p h d", h=H),
                                     spread(scope["bs"][:], 2, DH), ALU.add))
                step.settle()
                step(v.tensor_tensor(y[:, 3 * GW:4 * GW], fd[:], uv[:, 0:GW], ALU.mult))
                dve.wait_ge(E["rstd_c_done"], t.done)
                step.settle()
                v.scalar_tensor_tensor(y[:, 2 * GW:3 * GW], yz[:], rsc[:, 0:1], gc[:], ALU.mult, ALU.mult
                                       ).then_inc(E["y_ready"], 1)
                dve.wait_ge(E["out_done"], t.done)
                dve.wait_ge(E["xres_loaded"], t.i * 16 + 16)
                step(v.tensor_tensor(prod[:], big[0][:], keep["mix_gate"][:, 1 if sample else 0, :], ALU.mult))
                step.settle()
                v.tensor_tensor(xr[:], xr[:], prod[:], ALU.add).then_inc(E["x2_done"], 1)

            return tensor_tile, scalar_tile, pool_tile, vector_tile

        with ExitStack() as pctx:
            psb, _ = new_pools(nc, pctx)
            scope = {
                "sample": False, "mask": c["tri"], "ws_t": ws_t, "bs": bs,
                "band": psb("band", [P, H, BAND]), "k_t": psb("k_t_p", [P, 2, SEQ]), "v_all": psb("v_all", [P, NT, GW]),
                "q_z": psb("q_z_p", [P, H, P]), "score": [psb(f"score{n}", [P, BAND]) for n in range(2)],
                "prob_t": [psb(f"prob_t{n}", [P, BAND]) for n in range(2)],
                "nmax": psb("nmax", [P, H]), "total": psb("total", [P, H]), "inv": psb("inv", [P, H]),
                "cst": psb("cst", [DH, H, DH + 1]), "hst": psb("hst", [P, H, DH]), "m0": psb("m0", [H, 1]),
            }
            band, cst, hst, m0 = (scope[n] for n in ("band", "cst", "hst", "m0"))
            ssm_out = prod[0:DH, 0:512]
            tensor_tile, scalar_tile, pool_tile, vector_tile = engines(scope)
            block = pctx.enter_context(nc.Block())

            @block.sync
            def _(sp):
                def load_in(i, j):
                    sp.dma_start(pt[j][:], S["proj"][bass.ds(i * P, P), :]).then_inc(s_load[j], 16)
                    sp.dma_start(xt[j][:, 0:KX * (P + 3)].rearrange("p (k t) -> p k t", k=KX),
                                 S["xbc"][:, :, bass.ds(i * P, P + 3)]).then_inc(s_load[j], 16)

                def load_x(i):
                    sp.dma_start(xr[:], A["x_prompt"][0, bass.ds(i * P, P), :]).then_inc(E["xres_loaded"], 16)

                params = [(row_par[:, n:n + 1], A[name].rearrange("a h -> h a"))
                          for n, name in enumerate(("b_i_bias", "b_f_bias", "c_dt_bias", "c_a_log"))]
                params += [(skip[:], A["c_d_skip"][0].partition_broadcast(P)),
                           (gb[:], A["b_norm_g"][0].partition_broadcast(P)),
                           (gc[:], A["c_norm_g"][0].partition_broadcast(P)),
                           (gd[:], A["d_norm_g"][0].partition_broadcast(P)),
                           (bs[:], A["d_b_s"][0].rearrange("g t -> t g")),
                           (taps_c[:, 4, :], A["c_conv_b"][0].rearrange("(k p) -> p k", p=P)),
                           (ws_in[:], A["d_w_s"][0].rearrange("g t s -> t g s")),
                           (band[:], rel_tile(S, slice(0, P), slice(0, BAND)))]
                params += [(taps_c[:, n, :], A["c_conv_w"][0, n].rearrange("(k p) -> p k", p=P)) for n in range(4)]
                for dst, src in params:
                    sp.dma_start(dst, src, allow_slow_non_contiguous=True).then_inc(E["params_loaded"], 16)
                assert len(params) == N_PARAMS
                load_in(0, 0)
                load_in(1, 1)
                sp.dma_start(scope["v_all"][:], S["proj"][0:SEQ, VA:VA + GW].rearrange("(n p) d -> p n d", p=P)
                             ).then_inc(E["vall_loaded"], 16)
                load_x(0)
                sp.dma_start(w_out[:], A["w_out"][0].rearrange("(k p) n -> p k n", p=P)).then_inc(E["w_out_loaded"], 16)

                def tile(t, more=2):
                    sp.wait_ge(E["h2_kept"], t.nth(0, 1))
                    sp.dma_start(S["x2"][bass.ds(t.i * P, P), :], xr[:]).then_inc(E["tile_stored"], 16)
                    sp.dma_start(S["h2t"][:, :, bass.ds(t.i * P, P)], yt[:]).then_inc(E["tile_stored"], 16)
                    if more > 1:
                        load_in(t.i + 2, t.parity)
                    sp.wait_ge(E["tile_stored"], t.i * 32 + 32)
                    if more:
                        load_x(t.i + 1)

                for i in range(NPAST):
                    tile(Tile(i // 2, i % 2))
                with sp.Fori(NPAST // 2, NT // 2 - 1) as pair:
                    tile(Tile(pair, 0))
                    tile(Tile(pair, 1))
                tile(Tile(NT // 2 - 1, 0), more=1)
                tile(Tile(NT // 2 - 1, 1), more=0)
                sp.wait_ge(E["setup_dve"], 9)
                copies = [(O["p_c_ssm"][0, 0].rearrange("h p n -> p h n"), ssm_out.rearrange("p (h n) -> p h n", h=H)),
                          (O["p_b_c"][0, 0].rearrange("h d e -> d h e"), cst[:, :, 0:DH]),
                          (O["p_b_n"][0, 0].rearrange("h d -> d h"), cst[:, :, DH]),
                          (O["p_b_m"][0].rearrange("a h -> h a"), m0[:]),
                          (O["p_a_k"][0, 0].rearrange("t h d -> t (h d)"), S["proj"][SEQ - HIST:SEQ, KA:KA + GW]),
                          (O["p_a_v"][0, 0].rearrange("t h d -> t (h d)"), S["proj"][SEQ - HIST:SEQ, VA:VA + GW]),
                          (O["s_a_k"][0].rearrange("b t h d -> (b t) (h d)"), S["proj"][SEQ:SEQ + P, KA:KA + GW]),
                          (O["s_a_v"][0].rearrange("b t h d -> (b t) (h d)"), S["proj"][SEQ:SEQ + P, VA:VA + GW])]
                for n in range(3):
                    copies.append((O["p_c_conv"][0, 0, n].rearrange("(k p) -> p k", p=P), S["xbc"][:, :, SEQ + n]))
                for dst, src in copies:
                    sp.dma_start(dst, src, allow_slow_non_contiguous=True).then_inc(s_final, 16)
                sp.wait_ge(s_final, 16 * len(copies))

            @block.tensor
            def _(pe):
                pe.wait_ge(E["params_loaded"], 16 * N_PARAMS)
                for g in range(H):
                    last = nc.tensor.transpose(turn[:, g * P:(g + 1) * P], ws_in[:, g, :], c["ident"][:])
                last.then_inc(E["spatial_turned"], 1)
                pe.wait_ge(E["setup_dve"], 7)
                for i in range(NPAST):
                    tensor_tile(pe, Tile(i // 2, i % 2))
                with pe.Fori(NPAST // 2, NT // 2) as pair:
                    tensor_tile(pe, Tile(pair, 0))
                    tensor_tile(pe, Tile(pair, 1))
                pe.wait_ge(E["states_done"], NT)
                pe.wait_ge(E["xn2_done"], NT)
                for h in range(H):
                    last = nc.tensor.transpose(turn[0:DH, h * P:(h + 1) * P], hst[:, h, :], c["ident"][:])
                last.then_inc(E["spatial_turned"], 1)

            @block.scalar
            def _(act):
                step = Steps(act, E["act_step"])
                act.wait_ge(E["params_loaded"], 16 * N_PARAMS)
                nc.scalar.activation(row_par[:, 4:5], row_par[:, 3:4], ACT.Exp).then_inc(E["alog_exp"], 1)
                for i in range(NPAST):
                    scalar_tile(act, Tile(i // 2, i % 2), step)
                with act.Fori(NPAST // 2, NT // 2) as pair:
                    scalar_tile(act, Tile(pair, 0), step)
                    scalar_tile(act, Tile(pair, 1), step)
                steps_of["act"] = step

            @block.gpsimd
            def _(pool):
                step = Steps(pool, E["pool_step"])
                nc.gpsimd.memset(v1[:, :, DH:DH + 1], 1.0).then_inc(s_ones, 1)
                nc.gpsimd.memset(scope["q_z"][:], 0.0).then_inc(s_ones, 1)
                pool.wait_ge(s_ones, 2)
                pool.wait_ge(E["params_loaded"], 16 * N_PARAMS)
                for i in range(NPAST):
                    pool_tile(pool, Tile(i // 2, i % 2), step)
                with pool.Fori(NPAST // 2, NT // 2) as pair:
                    pool_tile(pool, Tile(pair, 0), step)
                    pool_tile(pool, Tile(pair, 1), step)
                steps_of["pool"] = step

            @block.vector
            def _(dve):
                step = Steps(dve, E["dve_step"])
                v, ready = nc.vector, E["setup_dve"]
                dve.wait_ge(E["params_loaded"], 16 * N_PARAMS)
                v.memset(cst[:], 0.0).then_inc(ready, 1)
                v.memset(hst[:], 0.0).then_inc(ready, 1)
                v.memset(m0[:], 0.0).then_inc(ready, 1)
                v.memset(band[0:64, :, BAND - 64:BAND], NEG).then_inc(ready, 1)
                v.memset(band[64:128, :, 0:64], NEG).then_inc(ready, 1)
                v.tensor_scalar(gb[:], gb[:], 0.5, None, ALU.mult).then_inc(ready, 1)
                dve.wait_ge(E["spatial_turned"], 1)
                v.tensor_tensor(ws_t[:], turn[:, 0:512].rearrange("p (g t) -> p g t", g=H), spread(c["tri"][:], 1, H),
                                ALU.mult).then_inc(ready, 1)
                dve.wait_ge(E["alog_exp"], 1)
                v.tensor_scalar(row_par[:, 4:5], row_par[:, 4:5], -1.0, None, ALU.mult).then_inc(ready, 1)
                dve.wait_ge(ready, 8)
                dve.wait_ge(s_ones, 2)
                for i in range(NPAST):
                    vector_tile(dve, Tile(i // 2, i % 2), step)
                with dve.Fori(NPAST // 2, NT // 2) as pair:
                    vector_tile(dve, Tile(pair, 0), step)
                    vector_tile(dve, Tile(pair, 1), step)
                dve.wait_ge(E["spatial_turned"], 2)
                v.tensor_copy(ssm_out, turn[0:DH, 0:512]).then_inc(ready, 1)
                steps_of["dve"] = step

        with ExitStack() as sctx:
            ssb_, _ = new_pools(nc, sctx)
            W1 = DH + 1
            scope = {
                "sample": True, "mask": c["tri_s"], "ws_t": ssb_("ws_t_s", [P, H, P]), "bs": ssb_("bs_s", [P, H]),
                "cst": ssb_("cst_s", [DH, H, NB, W1]), "hst": ssb_("hst_s", [P, H, NB, DH]), "m0": ssb_("m0_s", [H, NB]),
                "wide": ssb_("wide_m", [P, NB, W1]), "vws": [ssb_(f"vws{n}", [P, NB * W1]) for n in range(2)],
                "n2_done": sem("ms_wide_done"), "n2_used": sem("ms_wide_used"), "vws_done": sem("ms_vws_done"),
                "xt_loaded": sem("ms_xt_loaded"), "xt_dmas": KX * (NB + 1),
            }
            cst, hst, m0 = scope["cst"], scope["hst"], scope["m0"]
            ssm = ssb_("ssm_rows", [DH, NB * H, P])
            ws16, ws_wide = ssb_("ws16", [P, H, TS]), ssb_("ws_wide", [P, H, P])
            s_in, s_ssm, s_t, s_k, s_wide = (sem("ms_in"), sem("ms_ssm_loaded"), sem("ms_turned"), sem("ms_kept"),
                                             sem("ms_spatial_spread"))
            tensor_tile, scalar_tile, pool_tile, vector_tile = engines(scope)
            t16 = Tile(NT // 2, 0)
            block = sctx.enter_context(nc.Block())

            @block.sync
            def _(sp):
                for b in range(NB):
                    rows = slice(b * TS, (b + 1) * TS)
                    sp.dma_start(ws16[rows], A["d_w_s"][0, :, 0:TS, 0:TS].rearrange("g t s -> t g s")).then_inc(s_in, 16)
                    sp.dma_start(scope["bs"][rows], A["d_b_s"][0, :, 0:TS].rearrange("g t -> t g"),
                                 allow_slow_non_contiguous=True).then_inc(s_in, 16)
                sp.dma_start(ssm[:], A["state_c_ssm"][0].rearrange("b h p n -> p (b h) n")).then_inc(s_ssm, 16)
                for b in range(NB):
                    sp.dma_start(cst[:, :, b, 0:DH], A["state_b_c"][0, b].rearrange("h d e -> d h e")).then_inc(s_in, 16)
                    sp.dma_start(cst[:, :, b, DH], A["state_b_n"][0, b].rearrange("h d -> d h"),
                                 allow_slow_non_contiguous=True).then_inc(s_in, 16)
                sp.dma_start(m0[:], A["state_b_m"][0].rearrange("b h -> h b"), allow_slow_non_contiguous=True
                             ).then_inc(s_in, 16)
                for half in range(2):
                    sp.dma_start(pt[0][:, half * PW // 2:(half + 1) * PW // 2],
                                 S["proj"][SEQ:SEQ + P, half * PW // 2:(half + 1) * PW // 2]).then_inc(s_load[0], 16)
                sp.dma_start(xr[:], A["x_sample"].rearrange("b t d -> (b t) d")).then_inc(E["xres_loaded"], 16)
                for k in range(KX):
                    view = xt[0][:].rearrange("p (k b t) -> p k b t", k=KX, b=NB)[:, k]
                    sp.dma_start(view[:, :, 3:], S["xbc_s"][:, k, :].rearrange("p (b t) -> p b t", b=NB)
                                 ).then_inc(scope["xt_loaded"], 16)
                    for b in range(NB):
                        sp.dma_start(view[:, b, 0:3], A["state_c_conv"][0, b, :, k * P:(k + 1) * P].rearrange("j p -> p j"),
                                     allow_slow_non_contiguous=True).then_inc(scope["xt_loaded"], 16)
                sp.wait_ge(E["h2_kept"], NT + 1)
                out = [(S["h2t"][:, :, SEQ:SEQ + P], yt[:]), (S["x2"][SEQ:SEQ + P, :], xr[:]),
                       (O["s_d_v"][0].rearrange("b t d -> (b t) d"), vn[:]),
                       (O["s_b_m"][0].rearrange("b h -> h b"), m0[:])]
                for b in range(NB):
                    out.append((O["s_b_c"][0, b].rearrange("h d e -> d h e"), cst[:, :, b, 0:DH]))
                    out.append((O["s_b_n"][0, b].rearrange("h d -> d h"), cst[:, :, b, DH]))
                    for n in range(3):
                        out.append((O["s_c_conv"][0, b, n].rearrange("(k p) -> p k", p=P),
                                    S["xbc_s"][:, :, b * TS + TS - 3 + n]))
                for dst, src in out:
                    sp.dma_start(dst, src, allow_slow_non_contiguous=True).then_inc(s_final2, 16)
                sp.wait_ge(s_k, 5 + NB)
                sp.dma_start(O["s_c_ssm"][0].rearrange("b h p n -> p (b h) n"), ssm[:]).then_inc(s_final2, 16)
                sp.wait_ge(s_final2, 16 * (len(out) + 1))

            @block.tensor
            def _(pe):
                pe.wait_ge(s_ssm, 16)
                for h in range(H):
                    if h >= 2:
                        pe.wait_ge(s_k, h - 1)
                    for b in range(NB):
                        last = nc.tensor.transpose(big[h % 2][:, b * DH:(b + 1) * DH], ssm[:, b * H + h, :],
                                                   c["ident"][0:DH, 0:DH])
                    last.then_inc(s_t, 1)
                pe.wait_ge(s_wide, 1)
                for g in range(H):
                    last = nc.tensor.transpose(turn[:, g * P:(g + 1) * P], ws_wide[:, g, :], c["ident"][:])
                last.then_inc(s_t, 1)
                pe.wait_ge(s_k, 5)
                pe.wait_ge(s_in, 16 * (4 * NB + 1))
                tensor_tile(pe, t16)
                for b in range(NB):
                    if b >= 2:
                        pe.wait_ge(s_k, 5 + b - 1)
                    for h in range(H):
                        last = nc.tensor.transpose(turn[0:DH, b % 2 * 512 + h * P:b % 2 * 512 + (h + 1) * P],
                                                   hst[:, h, b, :], c["ident"][:])
                    last.then_inc(s_t, 1)

            @block.scalar
            def _(act):
                scalar_tile(act, t16, steps_of["act"].on(act))

            @block.gpsimd
            def _(pool):
                pool_tile(pool, t16, steps_of["pool"].on(pool))

            @block.vector
            def _(dve):
                v = nc.vector
                for h in range(H):
                    dve.wait_ge(s_t, h + 1)
                    v.tensor_copy(hst[:, h], big[h % 2][:, 0:512].rearrange("p (b d) -> p b d", b=NB)).then_inc(s_k, 1)
                dve.wait_ge(s_in, 16 * (4 * NB + 1))
                v.tensor_copy(ws_wide[:].rearrange("p g (b s) -> p g b s", b=NB), spread(ws16[:], 2, NB)
                              ).then_inc(s_wide, 1)
                dve.wait_ge(s_t, 5)
                v.tensor_tensor(scope["ws_t"][:], turn[:, 0:512].rearrange("p (g t) -> p g t", g=H),
                                spread(c["tri_s"][:], 1, H), ALU.mult).then_inc(s_k, 1)
                dve.wait_ge(s_k, 5)
                vector_tile(dve, t16, steps_of["dve"].on(dve))
                for b in range(NB):
                    dve.wait_ge(s_t, 6 + b)
                    v.tensor_copy(ssm[:, b * H:(b + 1) * H, :],
                                  turn[0:DH, b % 2 * 512:b % 2 * 512 + 512].rearrange("p (h n) -> p h n", h=H)
                                  ).then_inc(s_k, 1)


def feed_forward(nc, sem, A, O, S, c, keep):
    with ExitStack() as ctx:
        sb, ps = new_pools(nc, ctx)
        spans = [(0, 768, [(0, 384), (384, 384)]), (768, 768, [(0, 384), (384, 384)]),
                 (1536, 512, [(0, 512), (512, 128)])]
        NSP, MAXT = len(spans), 768
        NCH = 2
        h2 = sb("h2", [P, KD, MAXT])
        mid = sb("mid", [P, KF, MAXT])
        down = sb("down", [P, KD, MAXT])
        w_up = [sb(f"w_gu{j}", [P, 2, KD, P]) for j in range(2)]
        w_dn = [sb(f"w_dn{j}", [P, KF, P]) for j in range(2)]
        g_buf, g_s = sb("g_buf", [P, 2 + MAXT]), sb("g_s", [P, NB, 2 + TS])
        conv, gate_on = sb("conv", [P, MAXT]), sb("gate_on", [P, MAXT])
        taps, tap = sb("taps", [P, KF, 4]), sb("tap", [P, 4])
        tail = sb("tail", [P, KF, 18])
        hist = sb("hist", [P, KF, 16])
        xr = [sb(f"xr{j}", [P, D]) for j in range(2)]
        ffn_gate = sb("ffn_gate_in", [P, 2, D])
        y, prod = sb("y", [P, D]), sb("prod", [P, D])
        g_fin = sb("g_fin", [P, D])
        ss, mean, rstd = sb("ff_ss", [P, 2]), sb("ff_mean", [P, 2]), sb("ff_rstd", [P, 2])
        flat = mid[:].rearrange("p f t -> p (f t)")
        rows_in, rows_out = flat[0:16, 0:FF], flat[0:18, 0:FF]
        g_ps, u_ps = ps("g_ps", [P, 2, 512]), ps("u_ps", [P, 2, 512])
        d_ps, f_ps = ps("d_ps", [P, 2, 512]), ps("f_ps", [P, 2, 512])

        s_par, s_hist, s_h2 = sem("ff_params"), sem("ff_history"), sem("h2_loaded")
        s_w = [sem(f"w_gu_loaded{j}") for j in range(2)]
        s_wd = [sem(f"w_dn_loaded{j}") for j in range(2)]
        s_xr = [sem(f"xr_loaded{j}") for j in range(2)]
        s_ht, s_hk = sem("hist_turned"), sem("hist_kept")
        s_g, s_gk, s_u, s_mid = sem("g_done"), sem("g_kept"), sem("u_done"), sem("mid_done")
        s_conv, s_on = sem("ff_conv_done"), sem("gate_on_done")
        s_d, s_dk, s_f = sem("down_done"), sem("down_kept"), sem("down_turned")
        s_x3, s_ss, s_mean, s_rstd, s_y = sem("x3_done"), sem("ff_squares"), sem("ff_mean"), sem("ff_rstd"), sem("y_done")
        s_fuse = sem("f_ps_used")
        s_dve, s_store, s_tail, s_tk = sem("ff_dve"), sem("y_stored"), sem("tail_turned"), sem("tail_kept")
        s_tout = sem("tail_stored")

        wg = A["f_w_gate"][0].rearrange("(k p) (f c) -> f p k c", p=P, c=P)
        wu = A["f_w_up"][0].rearrange("(k p) (f c) -> f p k c", p=P, c=P)
        wd = A["f_w_down"][0].rearrange("(f p) (d c) -> d p f c", p=P, c=P)
        token_tiles = [(s, k) for s, (t0, n, ch) in enumerate(spans) for k in range(sum(w for _, w in ch) // P)]
        first_tile = [min(i for i, (s, _) in enumerate(token_tiles) if s == sp) for sp in range(NSP)] + [len(token_tiles)]

        block = ctx.enter_context(nc.Block())

        @block.sync
        def _(sp):
            def load_h2(s):
                t0, n, ch = spans[s]
                n = sum(w for _, w in ch)
                sp.dma_start(h2[:, :, 0:n], S["h2t"][:, :, t0:t0 + n]).then_inc(s_h2, 16)

            def load_gu(f, j):
                sp.dma_start(w_up[j][:, 0], wg[f] if isinstance(f, int) else
                             wg[bass.ds(f, 1)].rearrange("o p k c -> (o p) k c")).then_inc(s_w[j], 16)
                sp.dma_start(w_up[j][:, 1], wu[f] if isinstance(f, int) else
                             wu[bass.ds(f, 1)].rearrange("o p k c -> (o p) k c")).then_inc(s_w[j], 16)

            def load_dn(d, j):
                sp.dma_start(w_dn[j][:], wd[d] if isinstance(d, int) else
                             wd[bass.ds(d, 1)].rearrange("o p f c -> (o p) f c")).then_inc(s_wd[j], 16)

            def load_xr(i):
                sp.dma_start(xr[i % 2][:], S["x2"][i * P:(i + 1) * P, :]).then_inc(s_xr[i % 2], 16)

            sp.dma_start(rows_in, A["state_ffn_conv"][0].rearrange("b j n -> (b j) n")).then_inc(s_hist, 16)
            load_h2(0)
            load_gu(0, 0)
            load_gu(1, 1)
            load_xr(0)
            load_xr(1)
            for j in range(3):
                sp.dma_start(taps[:, :, j], A["f_conv_w"][0, j].rearrange("(f p) -> p f", p=P),
                             allow_slow_non_contiguous=True).then_inc(s_par, 16)
            sp.dma_start(taps[:, :, 3], A["f_conv_b"][0].rearrange("(f p) -> p f", p=P),
                         allow_slow_non_contiguous=True).then_inc(s_par, 16)
            sp.dma_start(g_fin[:], A["g_final"].partition_broadcast(P)).then_inc(s_par, 16)
            sp.dma_start(ffn_gate[:], S["ffn_gate"]).then_inc(s_par, 16)
            for s in range(NSP):
                with sp.Fori(1, KF // 2) as q:
                    for j in range(2):
                        sp.wait_ge(s_u, q * 2 + (s * KF + j - 1))
                        load_gu(q * 2 + j, j)
                for j in range(2):
                    if s:
                        sp.wait_ge(s_d, 2 * (s * KD - 1 + j))
                    load_dn(j, j)
                if s + 1 < NSP:
                    for j in range(2):
                        sp.wait_ge(s_u, (s + 1) * KF - 1 + j)
                        load_gu(j, j)
                    load_h2(s + 1)
                with sp.Fori(1, KD // 2) as q:
                    for j in range(2):
                        sp.wait_ge(s_d, q * 4 + 2 * (s * KD + j - 1))
                        load_dn(q * 2 + j, j)
                for i in range(first_tile[s], first_tile[s + 1]):
                    sp.wait_ge(s_y, i + 1)
                    if i < NT:
                        sp.dma_start(O["y_prompt"][0, i * P:(i + 1) * P, :], y[:]).then_inc(s_store, 16)
                    else:
                        sp.dma_start(O["y_sample"].rearrange("b t d -> (b t) d"), y[:]).then_inc(s_store, 16)
                    if i + 2 <= NT:
                        load_xr(i + 2)
            sp.wait_ge(s_tk, 6)
            sp.dma_start(O["s_ffn_conv"][0].rearrange("b j n -> (b j) n"), rows_out[0:16]).then_inc(s_tout, 16)
            sp.dma_start(O["p_ffn_conv"][0, 0], rows_out[16:18]).then_inc(s_tout, 16)
            sp.wait_ge(s_tout, 32)
            sp.wait_ge(s_store, 16 * (NT + 1))

        @block.tensor
        def _(pe):
            t = nc.tensor
            pe.wait_ge(s_hist, 16)
            for f in range(KF):
                last = t.transpose(f_ps[:, 0, f * 16:(f + 1) * 16], rows_in[:, f * P:(f + 1) * P], c["ident"][0:16, 0:16])
            last.then_inc(s_ht, 1)
            for s, (t0, n, chunks) in enumerate(spans):
                pe.wait_ge(s_h2, 16 * (s + 1))

                def step(q, j, first=False):
                    n_th = q * 2 + (s * KF + j)
                    pe.wait_ge(s_w[j], q * 32 + (s * KF // 2 * 32 + 32))
                    if not first:
                        pe.wait_ge(s_gk, n_th)
                    for b, (at, width) in enumerate(chunks):
                        for k in range(KD):
                            last = t.matmul(g_ps[:, b, 0:width], w_up[j][:, 0, k, :], h2[:, k, at:at + width],
                                            start=(k == 0), stop=(k == KD - 1))
                    last.then_inc(s_g, 1)
                    if not first:
                        pe.wait_ge(s_mid, n_th)
                    for b, (at, width) in enumerate(chunks):
                        for k in range(KD):
                            last = t.matmul(u_ps[:, b, 0:width], w_up[j][:, 1, k, :], h2[:, k, at:at + width],
                                            start=(k == 0), stop=(k == KD - 1))
                    last.then_inc(s_u, 1)

                step(0, 0, first=(s == 0))
                step(0, 1)
                with pe.Fori(1, KF // 2) as q:
                    step(q, 0)
                    step(q, 1)
                pe.wait_ge(s_mid, (s + 1) * KF)
                if s:
                    pe.wait_ge(s_ss, first_tile[s])

                def down_step(q, j, first=False):
                    pe.wait_ge(s_wd[j], q * 16 + (s * KD // 2 * 16 + 16))
                    for b, (at, width) in enumerate(chunks):
                        if not first:
                            pe.wait_ge(s_dk, q * 4 + (2 * (s * KD + j) + b - 1))
                        for f in range(KF):
                            last = t.matmul(d_ps[:, b, 0:width], w_dn[j][:, f, :], mid[:, f, at:at + width],
                                            start=(f == 0), stop=(f == KF - 1))
                        last.then_inc(s_d, 1)

                down_step(0, 0, first=(s == 0))
                down_step(0, 1)
                with pe.Fori(1, KD // 2) as q:
                    down_step(q, 0)
                    down_step(q, 1)
                if s == NSP - 1:
                    for f in range(KF):
                        if f % 4 == 0 and f >= 8:
                            pe.wait_ge(s_tk, f // 4 - 1)
                        ins = t.transpose(g_ps[0:18, f // 4 % 2, f % 4 * P:(f % 4 + 1) * P], tail[:, f, :], c["ident"][:])
                        if f % 4 == 3 or f == KF - 1:
                            ins.then_inc(s_tail, 1)
                pe.wait_ge(s_dk, 2 * KD * (s + 1))
                for i in range(first_tile[s], first_tile[s + 1]):
                    k = i - first_tile[s]
                    if i:
                        pe.wait_ge(s_fuse, i)
                    else:
                        pe.wait_ge(s_hk, 1)
                    for d in range(KD):
                        last = t.transpose(f_ps[:, d // 4, d % 4 * P:(d % 4 + 1) * P], down[:, d, k * P:(k + 1) * P],
                                           c["ident"][:])
                    last.then_inc(s_f, 1)

        @block.scalar
        def _(act):
            a = nc.scalar
            for s, (t0, n, chunks) in enumerate(spans):
                sample = s == NSP - 1

                def step(q, j, first=False):
                    n_th = q * 2 + (s * KF + j)
                    act.wait_ge(s_g, n_th + 1)
                    if not first:
                        act.wait_ge(s_conv, n_th)
                    for b, (at, width) in enumerate(chunks):
                        if sample and b == 1:
                            last = a.activation(g_s[:, :, 2:], g_ps[:, b, 0:width].rearrange("p (n t) -> p n t", n=NB),
                                                ACT.Copy)
                        else:
                            last = a.activation(g_buf[:, 2 + at:2 + at + width], g_ps[:, b, 0:width], ACT.Copy)
                        if b == NCH - 1:
                            last.then_inc(s_gk, 1)
                    act.wait_ge(s_conv, n_th + 1)
                    width = sum(w for _, w in chunks)
                    a.activation(gate_on[:, 0:width], conv[:, 0:width], ACT.Silu).then_inc(s_on, 1)

                step(0, 0, first=(s == 0))
                step(0, 1)
                with act.Fori(1, KF // 2) as q:
                    step(q, 0)
                    step(q, 1)

                def down_step(q, j):
                    for b, (at, width) in enumerate(chunks):
                        act.wait_ge(s_d, q * 4 + (2 * (s * KD + j) + b + 1))
                        dst = down[:, q * 2 + j, at:at + width] if isinstance(q, int) else \
                            down[:, bass.ds(q * 2 + j, 1), at:at + width].rearrange("p o t -> p (o t)")
                        a.activation(dst, d_ps[:, b, 0:width], ACT.Copy).then_inc(s_dk, 1)

                if s:
                    act.wait_ge(s_f, first_tile[s])
                down_step(0, 0)
                down_step(0, 1)
                with act.Fori(1, KD // 2) as q:
                    down_step(q, 0)
                    down_step(q, 1)
                for i in range(first_tile[s], first_tile[s + 1]):
                    act.wait_ge(s_x3, i + 1)
                    if i:
                        act.wait_ge(s_ss, i)
                    a.activation(d_ps[:].rearrange("p a n -> p (a n)"), xr[i % 2][:], ACT.Square,
                                 accum_out=ss[:, i % 2:i % 2 + 1]).then_inc(s_ss, 1)

        @block.gpsimd
        def _(pool):
            for i in range(NT + 1):
                j = i % 2
                pool.wait_ge(s_ss, i + 1)
                nc.gpsimd.tensor_scalar(mean[:, j:j + 1], ss[:, j:j + 1], 1.0 / D, EPS, ALU.mult, ALU.add
                                        ).then_inc(s_mean, 1)
                pool.wait_ge(s_mean, i + 1)
                nc.gpsimd.tensor_tensor(rstd[:, j:j + 1], mean[:, j:j + 1], c["minus_half"][:, 0:1], ALU.pow
                                        ).then_inc(s_rstd, 1)

        @block.vector
        def _(dve):
            v = nc.vector
            step_ = Steps(dve, s_dve)
            dve.wait_ge(s_ht, 1)
            v.tensor_copy(hist[:], f_ps[:, 0, 0:KF * 16].rearrange("p (f n) -> p f n", f=KF)).then_inc(s_hk, 1)
            step_(v.memset(g_buf[:, 0:2], 0.0))
            dve.wait_ge(s_par, 16 * 6)
            for s, (t0, n, chunks) in enumerate(spans):
                sample = s == NSP - 1
                width = sum(w for _, w in chunks)
                PER = 8 if sample else (6 if s else 5)
                base0 = step_.count

                def at_f(ap, f):
                    return ap[:, f] if isinstance(f, int) else ap[:, bass.ds(f, 1)].rearrange("p o n -> p (o n)")

                def step(q, j):
                    f = q * 2 + j
                    n_th = q * 2 + (s * KF + j)
                    step_.count = 0
                    step_.base = q * (2 * PER) + (base0 + j * PER)
                    step_(v.tensor_copy(tap[:], at_f(taps, f)))
                    if s:
                        step_(v.tensor_copy(g_buf[:, 0:2], at_f(tail, f)[:, 16:18]))
                    if sample:
                        step_(v.tensor_copy(g_s[:, :, 0:2], at_f(hist, f).rearrange("p (b j) -> p b j", b=NB)))
                    step_.settle()
                    dve.wait_ge(s_gk, n_th + 1)
                    gs = g_s[:]
                    cs = conv[:, n:n + P].rearrange("p (b t) -> p b t", b=NB) if sample else None
                    step_(v.tensor_scalar(conv[:, 0:n], g_buf[:, 0:n], tap[:, 0:1], tap[:, 3:4], ALU.mult, ALU.add))
                    if sample:
                        step_(v.tensor_scalar(cs, gs[:, :, 0:TS], tap[:, 0:1], tap[:, 3:4], ALU.mult, ALU.add))
                    step_.settle()
                    step_(v.scalar_tensor_tensor(conv[:, 0:n], g_buf[:, 1:n + 1], tap[:, 1:2], conv[:, 0:n],
                                                 ALU.mult, ALU.add))
                    if sample:
                        v.scalar_tensor_tensor(cs, gs[:, :, 1:TS + 1], tap[:, 1:2], cs, ALU.mult, ALU.add)
                        v.tensor_copy(at_f(tail, f)[:, 0:16].rearrange("p (b j) -> p b j", b=NB), gs[:, :, TS:TS + 2])
                    step_(v.tensor_copy(at_f(tail, f)[:, 16:18], g_buf[:, n:n + 2]))
                    step_.settle()
                    if sample:
                        v.scalar_tensor_tensor(cs, gs[:, :, 2:TS + 2], tap[:, 2:3], cs, ALU.mult, ALU.add)
                    v.scalar_tensor_tensor(conv[:, 0:n], g_buf[:, 2:n + 2], tap[:, 2:3], conv[:, 0:n],
                                           ALU.mult, ALU.add).then_inc(s_conv, 1)
                    dve.wait_ge(s_on, n_th + 1)
                    dve.wait_ge(s_u, n_th + 1)
                    for b, (at, w) in enumerate(chunks):
                        dst = at_f(mid, f)[:, at:at + w]
                        last = v.tensor_tensor(dst, gate_on[:, at:at + w], u_ps[:, b, 0:w], ALU.mult)
                        if b == NCH - 1:
                            last.then_inc(s_mid, 1)
                        else:
                            step_(last)
                    assert step_.count == PER

                step(0, 0)
                step(0, 1)
                with dve.Fori(1, KF // 2) as q:
                    step(q, 0)
                    step(q, 1)
                step_.base, step_.count = 0, base0 + KF * PER

                if sample:
                    for r in range(6):
                        dve.wait_ge(s_tail, r + 1)
                        w = min(4, KF - 4 * r) * P
                        v.tensor_copy(rows_out[:, r * 512:r * 512 + w], g_ps[0:18, r % 2, 0:w]).then_inc(s_tk, 1)

                def residual(i):
                    dve.wait_ge(s_f, i + 1)
                    dve.wait_ge(s_xr[i % 2], 16 * (i // 2 + 1))
                    who = 1 if i == NT else 0
                    if i:
                        dve.wait_ge(s_x3, i)
                    v.tensor_tensor(prod[:], f_ps[:].rearrange("p a n -> p (a n)"), ffn_gate[:, who, :],
                                    ALU.mult).then_inc(s_fuse, 1)
                    dve.wait_ge(s_fuse, i + 1)
                    v.tensor_tensor(xr[i % 2][:], xr[i % 2][:], prod[:], ALU.add).then_inc(s_x3, 1)

                def finish(i):
                    dve.wait_ge(s_rstd, i + 1)
                    if i:
                        dve.wait_ge(s_store, 16 * i)
                    v.scalar_tensor_tensor(y[:], xr[i % 2][:], rstd[:, i % 2:i % 2 + 1], g_fin[:], ALU.mult, ALU.mult
                                           ).then_inc(s_y, 1)

                tiles = range(first_tile[s], first_tile[s + 1])
                residual(tiles[0])
                for i in tiles:
                    if i + 1 in tiles:
                        residual(i + 1)
                    finish(i)


def bass_hybrid_chunk_streaming_encoder_step_kernel(nc, A, O):
    with ExitStack() as ctx:
        sb, _ = new_pools(nc, ctx)
        sem = Semaphores(nc)
        S = {name: nc.dram_tensor("scratch_" + name, shape, F32, kind="Internal").ap() for name, shape in {
            "proj": (SEQ + P, PW), "xbc": (P, KX, SEQ + 3), "xbc_s": (P, KX, P), "h2t": (P, KD, SEQ + P),
            "x2": (SEQ + P, D), "ffn_gate": (P, 2, D), "rel_row": (H, 768), "rel": (H, P, 768)}.items()}
        c, const_program = make_constants(nc, sb, sem)
        sem.constants_cut = sem["const_cut"]
        keep = {name: sb(name, [P, KD, 1 + NB]) for name in ("mix_scale", "mix_shift", "ffn_scale", "ffn_shift")}
        with ExitStack() as first:
            sb1, _ = new_pools(nc, first)
            keep["mix_gate"] = sb1("mix_gate", [P, 2, D])
            ya_sample = sb1("ya_sample", [P, GW])
            rel_bias_rows(nc, sem, A, S)
            with ExitStack() as second:
                sb2, _ = new_pools(nc, second)
                w_in_sb = sb2("w_in_sb", [P, KD * WIN + 520])
                modulation(nc, sem, A, S, c, const_program, keep, w_in_sb)
                projection(nc, sem, A, S, c, keep, w_in_sb)
            sem.give_back()
            sample_attention(nc, sem, A, S, c, ya_sample)
            mixers(nc, sem, A, O, S, c, keep, ya_sample)
        sem.give_back()
        feed_forward(nc, sem, A, O, S, c, keep)


class Semaphores:

    def __init__(self, nc):
        self.nc, self.made, self.group = nc, {}, []

    def give_back(self):
        self.nc.clear_and_free_semaphores(self.group)
        self.nc.all_engine_barrier()
        self.group = []

    def __call__(self, name):
        assert name not in self.made, name
        self.made[name] = self.nc.alloc_semaphore(name=name)
        self.group.append(self.made[name])
        return self.made[name]

    def __getitem__(self, name):
        return self.made[name]


_INS = ["x_prompt", "x_sample", "c_prompt", "c_sample", "cache_a_k", "cache_a_v", "state_b_c", "state_b_n", "state_b_m",
        "state_c_ssm", "state_c_conv", "state_ffn_conv", "w_ada", "b_ada", "g_norm_mix", "g_norm_ffn", "w_in", "w_out",
        "a_rel_bias", "b_i_bias", "b_f_bias", "b_norm_g", "c_conv_w", "c_conv_b", "c_dt_bias", "c_a_log", "c_d_skip",
        "c_norm_g", "d_norm_g", "d_w_s", "d_b_s", "f_w_gate", "f_w_up", "f_conv_w", "f_conv_b", "f_w_down", "g_final"]
_OUTS = {
    "y_prompt": (1, SEQ, D), "y_sample": (NB, TS, D), "p_a_k": (1, 1, HIST, H, DH), "p_a_v": (1, 1, HIST, H, DH),
    "p_b_c": (1, 1, H, DH, DH), "p_b_n": (1, 1, H, DH), "p_b_m": (1, 1, H), "p_c_ssm": (1, 1, H, DH, NSTATE),
    "p_c_conv": (1, 1, 3, XW), "p_ffn_conv": (1, 1, 2, FF), "s_a_k": (1, NB, TS, H, DH), "s_a_v": (1, NB, TS, H, DH),
    "s_b_c": (1, NB, H, DH, DH), "s_b_n": (1, NB, H, DH), "s_b_m": (1, NB, H), "s_c_ssm": (1, NB, H, DH, NSTATE),
    "s_c_conv": (1, NB, 3, XW), "s_ffn_conv": (1, NB, 2, FF), "s_d_v": (1, NB, TS, GW)}


def kernel(**inputs):
    import numpy as _np
    import concourse.bacc as _bacc
    from concourse.bass_utils import run_bass_kernel_spmd as _run

    nc = _bacc.Bacc("TRN2", target_bir_lowering=False, num_devices=1)
    arrays, A = {}, {}
    for name in _INS:
        a = _np.ascontiguousarray(inputs[name])
        if name == "a_rel_bias":
            name = "a_rel_bias_reversed"
            a = _np.ascontiguousarray(a[:, :, ::-1])
        arrays[f"in_{name}"] = a
        A[name] = nc.dram_tensor(f"in_{name}", a.shape, F32, kind="ExternalInput").ap()
    O = {name: nc.dram_tensor(f"out_{name}", shape, F32, kind="ExternalOutput").ap() for name, shape in _OUTS.items()}
    bass_hybrid_chunk_streaming_encoder_step_kernel(nc, A, O)
    r = _run(nc, [arrays], core_ids=[0])
    return tuple(r.results[0][f"out_{name}"] for name in _OUTS)
```

```python
from contextlib import ExitStack

import concourse.bass as bass
from concourse import mybir

F32 = mybir.dt.float32
ALU = mybir.AluOpType
ACT = mybir.ActivationFunctionType
AX = mybir.AxisListType.X

P = 128
D = 1024
KD = D // P
SEQ = 2048
NT = SEQ // P
NB, TS = 8, 16
GW = 256
H, DH = 4, 64
NSTATE = 128
XW = 768
KX = XW // P
WIN = 3340
X0 = 2056
PW = WIN - XW
FF = 2816
KF = FF // P
EPS = 1e-6
NEG = -1e30
HIST = 512
BAND = HIST + P
NPAST = HIST // P

QA, KA, VA, QB, KB, VB, OB, IB, FB, ZC, DT, UD, VD = (
    0, 256, 512, 768, 1024, 1280, 1536, 1792, 1796, 1800, 2056, 2060, 2316)


A0 = IB - 2 * GW
AW = PW - A0


def spread(ap, axis, n):
    shape = list(ap.shape)
    shape.insert(axis, n)
    return ap.unsqueeze(axis).to_broadcast(shape)


class Steps:

    def __init__(self, engine, sem):
        self.engine, self.sem, self.base, self.count, self.per_tile = engine, sem, 0, 0, None
        self.last = None

    def next(self):
        if self.count:
            self.per_tile = self.count
        self.base, self.count = self.base + self.count, 0

    def __call__(self, instruction):
        self.count += 1
        instruction.then_inc(self.sem, 1)
        self.last = (self.sem, self.base + self.count)

    def on(self, engine):
        self.engine = engine
        return self

    def settle(self):
        self.engine.wait_ge(*self.last)


class Tile:

    def __init__(self, pair, parity):
        self.pair, self.parity = pair, parity
        self.i = pair * 2 + parity
        self.first = isinstance(pair, int) and self.i == 0
        self.done = self.i + 1

    def nth(self, k, per):
        return self.i * per + (k + 1)


def new_pools(nc, ctx):
    def sb(name, shape, dt=F32):
        return ctx.enter_context(nc.sbuf_tensor(name, list(shape), dt))

    def ps(name, shape, dt=F32):
        return ctx.enter_context(nc.psum_tensor(name, list(shape), dt))

    return sb, ps


def make_constants(nc, sb, sem):
    c = {
        "ident": sb("ident", [P, P]),
        "ones": sb("ones", [P, P]),
        "tri": sb("tri", [P, P]),
        "tri_s": sb("tri_s", [P, P]),
        "pick": sb("pick", [H, H, P]),
        "stream": sb("stream", [P, NB]),
        "to_prompt": sb("to_prompt", [9, P]),
        "to_sample": sb("to_sample", [9, P]),
        "minus_half": sb("minus_half", [P, H]),
        "zeros": sb("zeros", [P, KX * 3]),
        "per_width": sb("per_width", [P, H + 2]),
        "eps": sb("eps", [P, H]),
    }
    made, cut = sem("const_made"), sem("const_cut")

    def program(pool):
        g = nc.gpsimd
        for name in ("ident", "pick", "to_prompt", "to_sample", "zeros"):
            g.memset(c[name][:], 0.0).then_inc(made, 1)
        for name in ("ones", "tri", "tri_s", "stream"):
            g.memset(c[name][:], 1.0).then_inc(made, 1)
        g.memset(c["minus_half"][:], -0.5).then_inc(made, 1)
        g.memset(c["eps"][:], EPS).then_inc(made, 1)
        g.memset(c["per_width"][:, 0:H], 1.0 / DH).then_inc(made, 1)
        g.memset(c["per_width"][:, H:H + 1], 1.0 / GW).then_inc(made, 1)
        g.memset(c["per_width"][:, H + 1:H + 2], 1.0 / D).then_inc(made, 1)
        pool.wait_ge(made, 14)
        n = 0

        def cut_out(ap, pattern, op, fill, base, rows):
            nonlocal n
            g.affine_select(out=ap, in_=ap, pattern=pattern, compare_op=op, fill=fill, base=base,
                            channel_multiplier=rows).then_inc(cut, 1)
            n += 1
            return n

        cut_out(c["ident"][:], [[-1, P]], ALU.not_equal, 1.0, 0, 1)
        cut_out(c["pick"][:], [[-1, H], [0, P]], ALU.not_equal, 1.0, 0, 1)
        cut_out(c["to_prompt"][:], [[0, P]], ALU.not_equal, 1.0, 0, 1)
        ts = c["to_sample"][:].rearrange("k (b t) -> k b t", b=NB)
        cut_out(ts, [[-1, NB], [0, TS]], ALU.not_equal, 1.0, -1, 1)
        cut_out(c["tri"][:], [[1, P]], ALU.is_ge, 0.0, 0, -1)
        cut_out(c["tri_s"][:], [[1, P]], ALU.is_ge, 0.0, 0, -1)
        cut_out(c["stream"][:], [[-TS, NB]], ALU.is_ge, 0.0, 0, 1)
        pool.wait_ge(cut, n)
        t3 = c["tri_s"][:].rearrange("p (b t) -> p b t", b=NB)
        cut_out(t3, [[-TS, NB], [0, TS]], ALU.is_ge, 0.0, 0, 1)
        cut_out(c["stream"][:], [[TS, NB]], ALU.is_ge, 0.0, TS - 1, -1)
        pool.wait_ge(cut, n)

    return c, program


def modulation(nc, sem, A, S, c, const_program, keep, w_in_sb):
    with ExitStack() as ctx:
        sb, ps = new_pools(nc, ctx)
        NS = 1 + NB
        NG = 6 * D // 512
        cond, cond_e, cond_r = sb("cond", [NS, D]), sb("cond_e", [NS, D]), sb("cond_r", [NS, D])
        cond_t = sb("cond_t", [P, KD, NS])
        w = [sb(f"w_ada{j}", [P, KD, 512]) for j in range(2)]
        bias, mod = sb("b_ada", [NS, 2, 512]), sb("mod", [NS, 6 * D])
        g_col = sb("g_col", [P, 2, KD])
        keep["ffn_gate"] = sb("ffn_gate", [P, 2, D])
        cond_ps = ps("cond_ps", [P, 512])
        mod_ps = ps("mod_ps", [P, 2, 512])
        col_ps = ps("col_ps", [P, 512])
        gate_ps = ps("gate_ps", [P, 4, 512])
        s_in, s_g = sem("mod_inputs"), sem("mod_gains")
        s_w = [sem(f"w_ada_loaded{j}") for j in range(2)]
        s_e, s_c, s_ct, s_ctc = sem("cond_exp"), sem("cond_silu"), sem("cond_turned"), sem("cond_kept")
        s_m, s_mk, s_col, s_gate, s_colk, s_gatek = (
            sem("mod_group"), sem("mod_kept"), sem("mod_cols"), sem("gate_rows"), sem("cols_kept"), sem("gates_kept"))
        s_v = sem("mod_dve")
        s_win, s_gout = sem("w_in_loaded"), sem("ffn_gate_stored")
        w_view = A["w_ada"][0].rearrange("(k p) n -> p k n", p=P)

        block = ctx.enter_context(nc.Block())

        @block.gpsimd
        def _(pool):
            const_program(pool)

        @block.sync
        def _(sp):
            sp.dma_start(cond[0:1, :], A["c_prompt"]).then_inc(s_in, 16)
            sp.dma_start(cond[1:NS, :], A["c_sample"]).then_inc(s_in, 16)
            for j in range(NG):
                if j >= 2:
                    sp.wait_ge(s_m, j - 1)
                    sp.wait_ge(s_mk, j - 1)
                sp.dma_start(bias[:, j % 2, :], A["b_ada"][0, j * 512:(j + 1) * 512].partition_broadcast(NS)
                             ).then_inc(s_w[j % 2], 16)
                sp.dma_start(w[j % 2][:], w_view[:, :, j * 512:(j + 1) * 512]).then_inc(s_w[j % 2], 16)
            w_in = A["w_in"][0].rearrange("(k p) n -> k p n", p=P)
            for k in range(KD):
                sp.dma_start(w_in_sb[:, k * WIN:(k + 1) * WIN], w_in[k]).then_inc(s_win, 16)
            sp.wait_ge(s_gatek, 8)
            sp.dma_start(S["ffn_gate"], keep["ffn_gate"][:]).then_inc(s_gout, 16)
            sp.wait_ge(s_gout, 16)

        @block.scalar
        def _(act):
            act.dma_start(g_col[:, 0, :], A["g_norm_mix"][0].rearrange("(k p) -> p k", p=P),
                          allow_slow_non_contiguous=True).then_inc(s_g, 16)
            act.dma_start(g_col[:, 1, :], A["g_norm_ffn"][0].rearrange("(k p) -> p k", p=P),
                          allow_slow_non_contiguous=True).then_inc(s_g, 16)
            act.wait_ge(s_in, 32)
            nc.scalar.activation(cond_e[:], cond[:], ACT.Silu).then_inc(s_e, 1)

        @block.vector
        def _(dve):
            dve.wait_ge(s_ct, 1)
            nc.vector.tensor_copy(cond_t[:], cond_ps[:, 0:KD * NS].rearrange("p (k s) -> p k s", k=KD)
                                  ).then_inc(s_ctc, 1)
            for j in range(NG):
                dve.wait_ge(s_m, j + 1)
                nc.vector.tensor_tensor(mod[:, j * 512:(j + 1) * 512], mod_ps[0:NS, j % 2, :],
                                        bias[:, j % 2, :], ALU.add).then_inc(s_mk, 1)
            dve.wait_ge(s_col, 1)
            dve.wait_ge(s_g, 32)
            cols = col_ps[:, 0:4 * KD * NS].rearrange("p (a k s) -> p a k s", a=4, k=KD)
            for a, norm in enumerate(("mix", "ffn")):
                nc.vector.tensor_copy(keep[norm + "_shift"][:], cols[:, 2 * a]).then_inc(s_colk, 1)
                nc.vector.tensor_scalar(keep[norm + "_scale"][:], cols[:, 2 * a + 1], 1.0, None, ALU.add
                                        ).then_inc(s_v, 1)
                dve.wait_ge(s_v, 2 * a + 1)
                nc.vector.tensor_tensor(keep[norm + "_scale"][:], keep[norm + "_scale"][:],
                                        spread(g_col[:, a, :], 2, NS), ALU.mult).then_inc(s_v, 1)
            n = 0
            for gate in ("mix_gate", "ffn_gate"):
                for who in range(2):
                    for half in range(2):
                        n += 1
                        dve.wait_ge(s_gate, n)
                        nc.vector.tensor_copy(keep[gate][:, who, half * 512:(half + 1) * 512],
                                              gate_ps[:, (n - 1) % 4, :]).then_inc(s_gatek, 1)
            dve.wait_ge(s_gatek, n)
            dve.wait_ge(s_colk, 2)
            dve.wait_ge(s_v, 4)

        @block.tensor
        def _(pe):
            t = nc.tensor
            pe.wait_ge(s_e, 1)
            pe.wait_ge(sem.constants_cut, 9)
            for k in range(KD):
                last = t.transpose(cond_ps[:, k * NS:(k + 1) * NS], cond_e[:, k * P:(k + 1) * P], c["ident"][0:NS, 0:NS])
            last.then_inc(s_ct, 1)
            pe.wait_ge(s_ctc, 1)
            for j in range(NG):
                pe.wait_ge(s_w[j % 2], 32 * (j // 2 + 1))
                if j >= 2:
                    pe.wait_ge(s_mk, j - 1)
                for k in range(KD):
                    last = t.matmul(mod_ps[0:NS, j % 2, :], cond_t[:, k, :], w[j % 2][:, k, :],
                                    start=(k == 0), stop=(k == KD - 1))
                last.then_inc(s_m, 1)
            pe.wait_ge(s_mk, NG)
            at = 0
            for piece in (0, 1, 3, 4):
                for k in range(KD):
                    last = t.transpose(col_ps[:, at:at + NS], mod[:, piece * D + k * P:piece * D + (k + 1) * P],
                                       c["ident"][0:NS, 0:NS])
                    at += NS
            last.then_inc(s_col, 1)
            n = 0
            for piece in (2, 5):
                for who in ("to_prompt", "to_sample"):
                    for half in range(2):
                        if n >= 4:
                            pe.wait_ge(s_gatek, n - 3)
                        at = piece * D + half * 512
                        t.matmul(gate_ps[:, n % 4, :], c[who][:], mod[:, at:at + 512], start=True, stop=True
                                 ).then_inc(s_gate, 1)
                        n += 1


def projection(nc, sem, A, S, c, keep, w_in_sb):
    with ExitStack() as ctx:
        sb, ps = new_pools(nc, ctx)
        x = [sb(f"x{j}", [P, D]) for j in range(2)]
        xn = [sb(f"xn{j}", [P, D]) for j in range(2)]
        squares = sb("squares", [P, D])
        ht = [sb(f"ht{j}", [P, KD, P]) for j in range(2)]
        out = [sb(f"proj_out{j}", [P, PW]) for j in range(2)]
        xout = [sb(f"xbc_out{j}", [P, KX, P]) for j in range(2)]
        ss, mean, rstd = sb("ss", [P, 2]), sb("mean", [P, 2]), sb("rstd", [P, 2])
        turned = ps("turned", [P, KD, P])
        unit = ps("unit", [P, 4, 512])
        s_x = [sem(f"x_loaded{j}") for j in range(2)]
        s_ss, s_mean, s_rstd, s_xn = sem("p1_squares"), sem("p1_mean"), sem("p1_rstd"), sem("p1_normed")
        s_t, s_ht, s_u, s_uk = sem("p1_turned"), sem("p1_ht"), sem("p1_unit"), sem("p1_unit_kept")
        s_o = [sem(f"p1_stored{j}") for j in range(2)]
        s_win, s_z = sem["w_in_loaded"], sem("p1_zero_columns")
        s_tmp = sem("p1_mod_products")

        groups = [(0, 1, 512, 0, 0), (512, 1, 512, 0, 512), (1024, 1, 384, 0, 1024), (1408, 1, 392, 0, 1408),
                  (1800, 2, 256, 1024, 1800), (3080, 1, 260, 0, 2312)]
        NU = len(groups) + 2

        def w_group(k, g):
            start, blocks, width, stride, _ = groups[g]
            at = k * WIN + start
            if blocks == 1:
                return w_in_sb[:, at:at + width]
            return w_in_sb[:, at:at + blocks * stride].rearrange("p (a n) -> p a n", a=blocks)[:, :, 0:width]

        block = ctx.enter_context(nc.Block())

        @block.sync
        def _(sp):
            xp = A["x_prompt"][0]
            xsamp = A["x_sample"].rearrange("b t d -> (b t) d")
            sp.dma_start(S["xbc"][:, :, 0:3], c["zeros"][:].rearrange("p (k j) -> p k j", k=KX)).then_inc(s_z, 16)
            sp.dma_start(x[0][:], xp[0:P, :]).then_inc(s_x[0], 16)
            sp.dma_start(x[1][:], xp[P:2 * P, :]).then_inc(s_x[1], 16)

            def store(t, sample=False):
                j = t.parity
                sp.wait_ge(s_uk, t.nth(NU - 1, NU))
                if sample:
                    sp.dma_start(S["proj"][SEQ:SEQ + P, :], out[j][:]).then_inc(s_o[j], 16)
                    sp.dma_start(S["xbc_s"][:, :, :], xout[j][:]).then_inc(s_o[j], 16)
                else:
                    sp.dma_start(S["proj"][bass.ds(t.i * P, P), :], out[j][:]).then_inc(s_o[j], 16)
                    sp.dma_start(S["xbc"][:, :, bass.ds(t.i * P + 3, P)], xout[j][:]).then_inc(s_o[j], 16)

            def both(pair, last=False):
                for j in range(2):
                    t = Tile(pair, j)
                    if last and j == 1:
                        store(t)
                        continue
                    sp.wait_ge(s_xn, t.nth(0, 1))
                    if last:
                        sp.dma_start(x[0][:], xsamp).then_inc(s_x[0], 16)
                    else:
                        sp.dma_start(x[j][:], xp[bass.ds(t.i * P + 2 * P, P), :]).then_inc(s_x[j], 16)
                    store(t)

            both(0)
            with sp.Fori(1, NT // 2 - 1) as pair:
                both(pair)
            both(NT // 2 - 1, last=True)
            store(Tile(NT // 2, 0), sample=True)
            sp.wait_ge(s_z, 16)
            sp.wait_ge(s_o[0], 32 * (NT // 2 + 1))
            sp.wait_ge(s_o[1], 32 * (NT // 2))

        @block.scalar
        def _(act):
            def squares_of(t):
                j = t.parity
                act.wait_ge(s_x[j], t.pair * 16 + 16)
                if not t.first:
                    act.wait_ge(s_ss, t.i * 1)
                nc.scalar.activation(squares[:], x[j][:], ACT.Square, accum_out=ss[:, j:j + 1]).then_inc(s_ss, 1)

            def keep_units(t, first_pair):
                j = t.parity
                if not first_pair:
                    act.wait_ge(s_o[j], t.pair * 32)
                for u in range(NU):
                    act.wait_ge(s_u, t.nth(u, NU))
                    if u < len(groups):
                        width, to = groups[u][1] * groups[u][2], groups[u][4]
                        nc.scalar.activation(out[j][:, to:to + width], unit[:, u % 4, 0:width], ACT.Copy
                                             ).then_inc(s_uk, 1)
                    else:
                        v = u - len(groups)
                        nc.scalar.activation(xout[j][:, 3 * v:3 * v + 3, :],
                                             unit[:, u % 4, 0:3 * P].rearrange("p (k t) -> p k t", k=3), ACT.Copy
                                             ).then_inc(s_uk, 1)

            def tiles(pair, first_pair=False, more=True):
                squares_of(Tile(pair, 1))
                keep_units(Tile(pair, 0), first_pair)
                if more:
                    squares_of(Tile(pair + 1, 0))
                keep_units(Tile(pair, 1), first_pair)

            squares_of(Tile(0, 0))
            tiles(0, first_pair=True)
            with act.Fori(1, NT // 2) as pair:
                tiles(pair)
            keep_units(Tile(NT // 2, 0), False)

        @block.gpsimd
        def _(pool):
            def rstd_of(t):
                j = t.parity
                pool.wait_ge(s_ss, t.done)
                nc.gpsimd.tensor_tensor(mean[:, j:j + 1], ss[:, j:j + 1], c["per_width"][:, H + 1:H + 2], ALU.mult
                                        ).then_inc(s_mean, 1)
                pool.wait_ge(s_mean, t.nth(0, 2))
                nc.gpsimd.tensor_tensor(mean[:, j:j + 1], mean[:, j:j + 1], c["eps"][:, 0:1], ALU.add
                                        ).then_inc(s_mean, 1)
                pool.wait_ge(s_mean, t.nth(1, 2))
                nc.gpsimd.tensor_tensor(rstd[:, j:j + 1], mean[:, j:j + 1], c["minus_half"][:, 0:1], ALU.pow
                                        ).then_inc(s_rstd, 1)

            rstd_of(Tile(0, 0))
            rstd_of(Tile(0, 1))
            with pool.Fori(1, NT // 2) as pair:
                rstd_of(Tile(pair, 0))
                rstd_of(Tile(pair, 1))
            rstd_of(Tile(NT // 2, 0))

        @block.vector
        def _(dve):
            def normalise(t):
                j = t.parity
                if not t.first:
                    pass
                dve.wait_ge(s_rstd, t.done)
                nc.vector.tensor_scalar(xn[j][:], x[j][:], rstd[:, j:j + 1], None, ALU.mult).then_inc(s_xn, 1)

            def keep_ht(t, sample=False, wait_used=True):
                j = t.parity
                dve.wait_ge(s_t, t.done)
                if wait_used:
                    dve.wait_ge(s_u, (t.i - 1) * NU)
                for k in range(KD):
                    if not sample:
                        ins = nc.vector.tensor_scalar(ht[j][:, k, :], turned[:, k, :], keep["mix_scale"][:, k, 0:1],
                                                      keep["mix_shift"][:, k, 0:1], ALU.mult, ALU.add)
                        if k == KD - 1:
                            ins.then_inc(s_ht, 1)
                    else:
                        wide = [P, NB, TS]
                        v = ht[j][:, k, :].rearrange("p (b t) -> p b t", b=NB)
                        nc.vector.tensor_tensor(v, turned[:, k, :].rearrange("p (b t) -> p b t", b=NB),
                                                keep["mix_scale"][:, k, 1:].unsqueeze(2).to_broadcast(wide),
                                                ALU.mult).then_inc(s_tmp, 1)
                        dve.wait_ge(s_tmp, k + 1)
                        ins = nc.vector.tensor_tensor(v, v, keep["mix_shift"][:, k, 1:].unsqueeze(2).to_broadcast(wide),
                                                      ALU.add)
                        if k == KD - 1:
                            ins.then_inc(s_ht, 1)

            def tile(t, first_use, sample=False):
                normalise(t)
                keep_ht(t, sample, not first_use)

            tile(Tile(0, 0), True)
            tile(Tile(0, 1), True)
            with dve.Fori(1, NT // 2) as pair:
                tile(Tile(pair, 0), False)
                tile(Tile(pair, 1), False)
            tile(Tile(NT // 2, 0), False, sample=True)

        @block.tensor
        def _(pe):
            def turn(t):
                j = t.parity
                pe.wait_ge(s_xn, t.done)
                if not t.first:
                    pe.wait_ge(s_ht, t.i * 1)
                for k in range(KD):
                    last = nc.tensor.transpose(turned[:, k, :], xn[j][:, k * P:(k + 1) * P], c["ident"][:])
                last.then_inc(s_t, 1)

            def project(t):
                j = t.parity
                pe.wait_ge(s_ht, t.done)
                for u in range(NU):
                    if not (t.first and u < 4):
                        pe.wait_ge(s_uk, t.i * NU + (u - 3))
                    if u < len(groups):
                        width, blocks = groups[u][2], groups[u][1]
                        dst = unit[:, u % 4, 0:width * blocks]
                        if blocks > 1:
                            dst = dst.rearrange("p (a n) -> p a n", a=blocks)
                        for k in range(KD):
                            last = nc.tensor.matmul(dst, ht[j][:, k, :], w_group(k, u), start=(k == 0),
                                                    stop=(k == KD - 1))
                    else:
                        for v in range(3):
                            col = X0 + (3 * (u - len(groups)) + v) * P
                            for k in range(KD):
                                last = nc.tensor.matmul(unit[:, u % 4, v * P:(v + 1) * P],
                                                        w_in_sb[:, k * WIN + col:k * WIN + col + P], ht[j][:, k, :],
                                                        start=(k == 0), stop=(k == KD - 1))
                    last.then_inc(s_u, 1)

            turn(Tile(0, 0))
            pe.wait_ge(s_win, 16 * KD)

            def tiles(pair):
                turn(Tile(pair, 1))
                project(Tile(pair, 0))
                turn(Tile(pair + 1, 0))
                project(Tile(pair, 1))

            tiles(0)
            with pe.Fori(1, NT // 2) as pair:
                tiles(pair)
            project(Tile(NT // 2, 0))


def rel_bias_rows(nc, sem, A, S):
    with ExitStack() as ctx:
        sb, _ = new_pools(nc, ctx)
        rev, ext = sb("rel_rev", [H, 257]), sb("rel_ext", [H, 768])
        s_in, s_e, s_row, s_rel = sem("rel_in"), sem("rel_extended"), sem("rel_row_stored"), sem("rel_stored")
        block = ctx.enter_context(nc.Block())

        @block.sync
        def _(sp):
            sp.dma_start(rev[:], A["a_rel_bias_reversed"][0]).then_inc(s_in, 16)
            sp.wait_ge(s_e, 2)
            sp.dma_start(S["rel_row"], ext[:]).then_inc(s_row, 16)
            sp.wait_ge(s_row, 16)
            for h in range(H):
                sp.dma_start(S["rel"][h], S["rel_row"][h].partition_broadcast(P)).then_inc(s_rel, 16)
            sp.wait_ge(s_rel, 16 * H)

        @block.vector
        def _(dve):
            dve.wait_ge(s_in, 16)
            nc.vector.tensor_copy(ext[:, 0:512], rev[:, 0:1].to_broadcast([H, 512])).then_inc(s_e, 1)
            dve.wait_ge(s_e, 1)
            nc.vector.tensor_copy(ext[:, 511:768], rev[:, 0:257]).then_inc(s_e, 1)


def rel_tile(S, rows, cols):
    flat = S["rel"].rearrange("h q u -> h (q u)")[:, 127:127 + P * 767]
    return flat.rearrange("h (q j) -> q h j", j=767)[rows, :, cols]


def sample_attention(nc, sem, A, S, c, ya_keep):
    with ExitStack() as ctx:
        sb, ps = new_pools(nc, ctx)
        pt = sb("sa_proj", [P, 768])
        k_in, v_in = sb("k_in", [P, NB, NPAST, GW]), sb("v_in", [P, NB, NPAST, GW])
        k_t = sb("k_t", [P, 2, NB, HIST])
        k_new = sb("k_new", [P, 2, P])
        band = sb("band_s", [P, H, BAND])
        q_z = sb("q_z", [P, H, P])
        q_m = [sb(f"q_m{j}", [P, NB, P]) for j in range(2)]
        stream_row = sb("stream_row", [P, NB, P])
        score, prob = sb("score_s", [P, BAND]), sb("prob_s", [P, BAND])
        prob_t = sb("prob_t_s", [P, BAND])
        wide, own = sb("wide_s", [P, NB, DH]), sb("own_s", [P, DH])
        nmax, total, inv = sb("nmax_s", [P, H]), sb("total_s", [P, H]), sb("inv_s", [P, H])
        turn_ps = ps("sa_turn", [P, 2, 512])
        s_ps = ps("sa_score", [P, 1024])
        p_ps = ps("sa_prob_t", [P, 1024])
        o_ps, n_ps = ps("sa_out", [P, 512]), ps("sa_new", [P, 512])
        s_in, s_k, s_v, s_band = sem("sa_proj_loaded"), sem("sa_k_loaded"), sem("sa_v_loaded"), sem("sa_band_loaded")
        s_neg, s_row, s_z = sem("sa_band_masked"), sem("sa_stream_row"), sem("sa_q_zero")
        s_qt, s_q, s_kt, s_kk = sem("sa_qk_turned"), sem("sa_qk_kept"), sem("sa_k_turned"), sem("sa_k_kept")
        s_qm, s_s, s_mx, s_p, s_pt, s_ptk, s_o, s_dve = (
            sem("sa_q_masked"), sem("sa_scores"), sem("sa_max"), sem("sa_probs"), sem("sa_probs_turned"),
            sem("sa_probs_kept"), sem("sa_out_done"), sem("sa_dve"))
        s_used = sem("sa_out_used")
        block = ctx.enter_context(nc.Block())

        @block.sync
        def _(sp):
            sp.dma_start(pt[:], S["proj"][SEQ:SEQ + P, 0:768]).then_inc(s_in, 16)
            for b in range(NB):
                sp.dma_start(k_in[:, b], A["cache_a_k"][0, b].rearrange("(n p) h d -> p n (h d)", p=P)).then_inc(s_k, 16)
            for b in range(NB):
                sp.dma_start(v_in[:, b], A["cache_a_v"][0, b].rearrange("(n p) h d -> p n (h d)", p=P)).then_inc(s_v, 16)
            sp.wait_ge(s_neg, 1)
            for b in range(NB):
                rows = slice(b * TS, (b + 1) * TS)
                sp.dma_start(band[rows, :, 0:HIST], rel_tile(S, slice(0, TS), slice(0, HIST))).then_inc(s_band, 16)
                sp.dma_start(band[rows, :, HIST + b * TS:HIST + (b + 1) * TS],
                             rel_tile(S, slice(0, TS), slice(HIST, HIST + TS))).then_inc(s_band, 16)

        @block.gpsimd
        def _(pool):
            nc.gpsimd.memset(band[:], NEG).then_inc(s_neg, 1)
            nc.gpsimd.memset(q_z[:], 0.0).then_inc(s_z, 1)
            nc.gpsimd.memset(stream_row[:], 0.0).then_inc(s_row, 1)
            pool.wait_ge(s_row, 1)
            sr = stream_row[:].rearrange("p n (b t) -> p n b t", b=NB)
            nc.gpsimd.affine_select(out=sr, in_=sr, pattern=[[1, NB], [-1, NB], [0, TS]], compare_op=ALU.not_equal,
                                    fill=1.0, base=0, channel_multiplier=0).then_inc(s_row, 1)

        @block.tensor
        def _(pe):
            t = nc.tensor
            pe.wait_ge(s_in, 16)
            for a in range(4):
                last = t.transpose(turn_ps[:, 0, a * P:(a + 1) * P], pt[:, a * P:(a + 1) * P], c["ident"][:])
            last.then_inc(s_qt, 1)
            n = 0
            pe.wait_ge(s_k, 16 * NB)
            for b in range(NB):
                for pair in range(2):
                    n += 1
                    if n >= 2:
                        pe.wait_ge(s_kk, n - 2) if n > 2 else None
                    if n == 2:
                        pe.wait_ge(s_q, 3)
                    for m in range(NPAST):
                        last = t.transpose(turn_ps[:, n % 2, m * P:(m + 1) * P], k_in[:, b, m, pair * P:(pair + 1) * P],
                                           c["ident"][:])
                    last.then_inc(s_kt, 1)
            pe.wait_ge(s_kk, 2 * NB)
            pe.wait_ge(s_v, 16 * NB)
            for h in range(H):
                pe.wait_ge(s_qm, h + 1)
                if h:
                    pe.wait_ge(s_mx, h)
                for b in range(NB):
                    t.matmul(s_ps[:, 0:HIST], q_m[h % 2][:, b, :], k_t[:, h // 2, b, :], start=(b == 0),
                             stop=(b == NB - 1))
                t.matmul(s_ps[:, HIST:BAND], q_z[:, h, :], k_new[:, h // 2, :], start=True, stop=True).then_inc(s_s, 1)
                pe.wait_ge(s_p, h + 1)
                for m in range(NPAST + 1):
                    last = t.transpose(p_ps[:, m * P:(m + 1) * P], prob[:, m * P:(m + 1) * P], c["ident"][:])
                last.then_inc(s_pt, 1)
                pe.wait_ge(s_ptk, h + 1)
                if h:
                    pe.wait_ge(s_used, h)
                for m in range(NPAST):
                    t.matmul(o_ps[:].rearrange("p (b d) -> p b d", b=NB), prob_t[:, m * P:(m + 1) * P],
                             v_in[:, :, m, h * DH:(h + 1) * DH], start=(m == 0), stop=(m == NPAST - 1))
                t.matmul(n_ps[:, 0:DH], prob_t[:, HIST:BAND], pt[:, VA + h * DH:VA + (h + 1) * DH], start=True,
                         stop=True).then_inc(s_o, 1)

        @block.scalar
        def _(act):
            for n in range(1, 2 * NB + 1):
                b, pair = (n - 1) // 2, (n - 1) % 2
                act.wait_ge(s_kt, n)
                nc.scalar.activation(k_t[:, pair, b, :], turn_ps[:, n % 2, :], ACT.Copy).then_inc(s_kk, 1)
            for h in range(H):
                act.wait_ge(s_mx, h + 1)
                if h:
                    act.wait_ge(s_pt, h)
                nc.scalar.activation(prob[:], score[:], ACT.Exp, bias=nmax[:, h:h + 1], accum_out=total[:, h:h + 1]
                                     ).then_inc(s_p, 1)
                act.wait_ge(s_pt, h + 1)
                if h:
                    act.wait_ge(s_o, h)
                nc.scalar.activation(prob_t[:], p_ps[:, 0:BAND], ACT.Copy).then_inc(s_ptk, 1)

        @block.vector
        def _(dve):
            v = nc.vector
            step = Steps(dve, s_dve)
            dve.wait_ge(s_qt, 1)
            dve.wait_ge(s_z, 1)
            qk = turn_ps[:, 0, :].rearrange("p (a t) -> p a t", a=4)
            v.tensor_copy(q_z[0:64, 0:4:2, :], qk[0:64, 0:2, :]).then_inc(s_q, 1)
            v.tensor_copy(q_z[64:128, 1:4:2, :], qk[64:128, 0:2, :]).then_inc(s_q, 1)
            v.tensor_copy(k_new[:], qk[:, 2:4, :]).then_inc(s_q, 1)
            dve.wait_ge(s_q, 3)
            dve.wait_ge(s_row, 2)
            dve.wait_ge(s_band, 32 * NB)

            def mask_q(h):
                if h >= 2:
                    dve.wait_ge(s_s, h - 1)
                v.tensor_tensor(q_m[h % 2][:], spread(q_z[:, h, :], 1, NB), stream_row[:], ALU.mult).then_inc(s_qm, 1)

            mask_q(0)
            for h in range(H):
                if h + 1 < H:
                    mask_q(h + 1)
                dve.wait_ge(s_s, h + 1)
                if h:
                    dve.wait_ge(s_p, h)
                step(v.scalar_tensor_tensor(score[:], s_ps[:, 0:BAND], DH ** -0.5, band[:, h, :], ALU.mult, ALU.add))
                step.settle()
                v.tensor_reduce(nmax[:, h:h + 1], score[:], AX, ALU.max, negate=True).then_inc(s_mx, 1)
                dve.wait_ge(s_p, h + 1)
                step(v.reciprocal(inv[:, h:h + 1], total[:, h:h + 1]))
                dve.wait_ge(s_o, h + 1)
                step(v.tensor_tensor(wide[:], o_ps[:].rearrange("p (b d) -> p b d", b=NB), spread(c["stream"][:], 2, DH),
                                     ALU.mult))
                step.settle()
                step(v.tensor_reduce(own[:], wide[:].rearrange("p b d -> p d b"), AX, ALU.add))
                step.settle()
                v.tensor_tensor(own[:], own[:], n_ps[:, 0:DH], ALU.add).then_inc(s_used, 1)
                dve.wait_ge(s_used, h + 1)
                step(v.tensor_scalar(ya_keep[:, h * DH:(h + 1) * DH], own[:], inv[:, h:h + 1], None, ALU.mult))
            step.settle()


ROWS = 8
R_INTER, R_FLOOR, R_WB, R_CS, R_WC, R_A, R_NCS, R_DT = range(ROWS)


def mixers(nc, sem, A, O, S, c, keep, ya_sample):
    with ExitStack() as ctx:
        sb, ps = new_pools(nc, ctx)
        w_out = sb("w_out", [P, KD, D])
        taps_c = sb("taps_c", [P, 5, KX])
        gb, gc, gd = sb("gb", [P, GW]), sb("gc", [P, GW]), sb("gd", [P, GW])
        skip = sb("skip", [P, H])
        row_par = sb("row_par", [H, 8])
        ws_t = sb("ws_t", [P, H, P])
        bs = sb("bs", [P, H])
        pt_a = [sb(f"pt_a{j}", [P, AW]) for j in range(2)]
        pt_b = [sb(f"pt_b{j}", [P, 4 * GW]) for j in range(2)]
        xt = [sb(f"xt{j}", [P, KX * NB * (TS + 3)]) for j in range(2)]
        xr = sb("xr", [P, D])
        acc, xc = sb("acc", [P, KX, P]), [sb(f"xc{j}", [P, KX, P]) for j in range(2)]
        uvs, szs = [sb(f"uv{j}", [P, 2 * GW]) for j in range(2)], [sb(f"sz{j}", [P, GW]) for j in range(2)]
        stats, mv, rs_d, rsd_m = sb("stats", [P, 6]), sb("mv", [P, 2]), sb("rs_d", [P, 1]), sb("rsd_m", [P, 1])
        vn = sb("vn", [P, GW])
        u_in, soft = sb("u_in", [H, 2, P]), sb("soft", [H, 2, P])
        ig, nb, mx = sb("ig", [H, P]), sb("nb", [H, P]), sb("mx", [H, P])
        sp_, la = soft, u_in[:, 0, :]
        row, arg, bc = sb("row", [H, ROWS, P]), sb("arg", [H, 5, P]), [sb(f"bc{j}", [H, 2, P]) for j in range(2)]
        ends = [sb(f"ends{j}", [H, 2, NB]) for j in range(2)]
        col = [sb(f"col{j}", [P, ROWS, H]) for j in range(2)]
        qkb = sb("qkb", [DH, 2 * H, P])
        dec_arg = sb("dec_arg", [P, 2 * H, P])
        wt, gt = sb("wt", [P, H, P]), sb("gt", [P, H, P])
        ws_in = wt
        v1, v1w = sb("v1", [P, H, DH + 1]), sb("v1w", [P, H, DH + 1])
        xs_b = sb("xs_b", [P, 2 * GW])
        xdt, xwl, xsk = sb("xdt", [P, H, DH]), sb("xwl", [P, H, DH]), sb("xsk", [P, H, DH])
        to = sb("to", [P, GW])
        nums, den = sb("nums", [P, H, DH + 1]), sb("den", [P, H])
        fd = nums[:, :, 0:DH]
        hb, sq, sums = sb("hb", [P, H, DH]), sb("sq", [P, H, DH]), sb("sums", [P, H])
        ssb, rsb_m, rsb = sb("ssb", [P, H]), sb("rsb_m", [P, H]), sb("rsb", [P, H])
        yz, ssc, rsc_m, rsc = sb("yz", [P, GW]), sb("ssc", [P, 1]), sb("rsc_m", [P, 1]), sb("rsc", [P, 1])
        y = [sb(f"y_mix{j}", [P, D]) for j in range(2)]
        yt = sb("yt", [P, KD, P])
        prod = sb("prod2", [P, D])
        ss2, rs2_m, rs2 = sb("ss2", [P, 1]), sb("rs2_m", [P, 1]), sb("rs2", [P, 1])
        sc_ps, pr_ps = ps("sc_ps", [P, 1024]), ps("pr_ps", [P, 1024])
        b01, b23 = ps("b01", [P, 1024]), ps("b23", [P, 1024])
        DEC = 512 - 2 * H * NB

        names = """rows_turned qk_turned scores_done cols_turned pv_done bcast_done qkb_turned cb_done qk_done
            xsb_turned nums_done ys_done state_ps_done f_done y_turned out_done h2_turned
            load_done0 load_done1 tile_stored
            gelu_done tap0_done softplus_done xc_done rows_exp prob_done prob_kept gate_tanh qkb_kept dec_exp xsb_kept
            sq_c_done yt_kept sq2_done xn2_done h2_kept
            v1_copied v1w_done xd_done rstd_d_done dec_masked rstd_b_done rstd_c_done rstd_2_done xwl_done skip_done
            qk_kept rows_in conv_done max_done args_done rows_done cols_kept var_done vn_done ya_done dec_ready
            w_done g_done yb_centred yz_done x2_done y_ready states_done probs_turned
            score_read out_read nums_read h2_half load_b0 load_b1
            dve_step act_step pool_step params_loaded w_out_loaded spatial_turned alog_exp setup_dve
            vall_loaded xres_loaded""".split()
        E = {n: sem("m_" + n) for n in names}
        s_load_a, s_load_b = [E["load_done0"], E["load_done1"]], [E["load_b0"], E["load_b1"]]
        s_final, s_final2, s_ones = sem("m_final_stored"), sem("m_sample_stored"), sem("m_ones")
        N_PARAMS = 16
        steps_of = {}

        def engines(scope):
            sample = scope["sample"]
            band, k_t, v_all = scope.get("band"), scope.get("k_t"), scope.get("v_all")
            q_z, score, prob_t = (scope.get(n) for n in ("q_z", "score", "prob_t"))
            prob = score
            nmax, total, inv = (scope.get(n) for n in ("nmax", "total", "inv"))
            cst, hst, m0 = scope["cst"], scope["hst"], scope["m0"]
            mask = scope["mask"]
            batch = NB if sample else 1

            def x_view(t, j):
                flat = xt[t.parity]
                if sample:
                    return flat[:, 0:KX * NB * (TS + 3)].rearrange("p (k b t) -> p k b t", k=KX, b=NB)[:, :, :, j:j + TS]
                return flat[:, 0:KX * (P + 3)].rearrange("p (k t) -> p k t", k=KX)[:, :, j:j + P]

            def chan(ap, k):
                a = ap[:, k, :]
                return a.rearrange("p (b t) -> p b t", b=NB) if sample else a

            def blocks(i):
                return (i + 1) if isinstance(i, int) and i < NPAST else NPAST + 1

            def later(t, n=1):
                return not (isinstance(t.i, int) and t.i < n)

            W1 = DH + 1
            heads = "p (h d) -> p h d"

            def tensor_iteration(pe, t1, t2, t3):
                T = nc.tensor
                if t1:
                    p, i = pt_a[t1.parity], t1.i
                    pe.wait_ge(s_load_a[t1.parity], t1.pair * 48 + 48)
                    if later(t1):
                        pe.wait_ge(E["rows_in"], t1.i * 1)
                        if not sample:
                            pe.wait_ge(E["prob_kept"], t1.i * H)
                    if later(t1, 2):
                        pe.wait_ge(E["y_ready"], t1.i - 1)
                    for n, at in enumerate((IB, FB, DT)):
                        last = T.transpose(sc_ps[0:H, 640 + n * P:640 + (n + 1) * P], p[:, at - A0:at - A0 + H], c["ident"][:])
                    last.then_inc(E["rows_turned"], 1)
                    if not sample:
                        for a in range(4):
                            last = T.transpose(pr_ps[:, a * P:(a + 1) * P], p[:, a * P:(a + 1) * P], c["ident"][:])
                        last.then_inc(E["qk_turned"], 1)
                        nk = blocks(i)
                        first_key = (i - (nk - 1)) * P
                if t3:
                    pe.wait_ge(E["y_ready"], t3.done)
                    pe.wait_ge(E["states_done"], t3.done)
                    for k in range(KD):
                        last = T.transpose(b01[:, k * P:(k + 1) * P], y[t3.parity][:, k * P:(k + 1) * P], c["ident"][:])
                    last.then_inc(E["y_turned"], 1)
                    pe.wait_ge(E["yt_kept"], t3.done)
                if t2:
                    pb = pt_b[t2.parity]
                    pe.wait_ge(s_load_b[t2.parity], t2.pair * 16 + 16)
                    for n, at in enumerate((QB, KB)):
                        for h in range(H):
                            last = T.matmul(b01[0:DH, (n * H + h) * P:(n * H + h + 1) * P],
                                            pb[:, at - QB + h * DH:at - QB + (h + 1) * DH], c["ident"][:], start=True, stop=True)
                    last.then_inc(E["qkb_turned"], 1)

                def scores(h):
                    n1 = min(nk * P, 512)
                    if h:
                        pe.wait_ge(E["score_read"], t1.nth(h - 1, H))
                    ins = T.matmul(sc_ps[:, 0:n1], q_z[:, h, :], k_t[:, h // 2, bass.ds(first_key, n1)],
                                   start=True, stop=True)
                    if nk > 4:
                        ins = T.matmul(sc_ps[:, 512:640], q_z[:, h, :], k_t[:, h // 2, bass.ds(first_key + 512, P)],
                                       start=True, stop=True)
                    ins.then_inc(E["scores_done"], 1)

                def attend(h):
                    if not t1 or sample:
                        return
                    pe.wait_ge(E["prob_done"], t1.nth(h, H))
                    if h == 0:
                        pe.wait_ge(E["cols_kept"], t1.done)
                    else:
                        pe.wait_ge(E["prob_kept"], t1.nth(h - 1, H))
                    for m in range(nk):
                        last = T.transpose(pr_ps[:, m * P:(m + 1) * P], prob[h % 2][:, m * P:(m + 1) * P], c["ident"][:])
                    last.then_inc(E["probs_turned"], 1)
                    if h + 1 < H:
                        scores(h + 1)
                    pe.wait_ge(E["prob_kept"], t1.nth(h, H))
                    if h == 0:
                        pe.wait_ge(E["vall_loaded"], 16)
                        if later(t1):
                            pe.wait_ge(E["ya_done"], t1.i * 1)
                    for m in range(nk):
                        if isinstance(i, int):
                            v = v_all[:, i - (nk - 1) + m, h * DH:(h + 1) * DH]
                        else:
                            v = v_all[:, bass.ds(i + (m - (nk - 1)), 1), h * DH:(h + 1) * DH].rearrange("p o d -> p (o d)")
                        last = T.matmul(pr_ps[:, 768 + h * DH:768 + (h + 1) * DH], prob_t[h % 2][:, m * P:(m + 1) * P], v,
                                        start=(m == 0), stop=(m == nk - 1))
                    last.then_inc(E["pv_done"], 1)

                if t1 and not sample:
                    pe.wait_ge(E["qk_kept"], t1.nth(2, 3))
                    scores(0)
                if t3:
                    pe.wait_ge(E["w_out_loaded"], 16)
                    for half in range(2):
                        for k in range(KD):
                            last = T.matmul(b23[:, half * 512:(half + 1) * 512], yt[:, k, :],
                                            w_out[:, k, half * 512:(half + 1) * 512], start=(k == 0), stop=(k == KD - 1))
                    last.then_inc(E["out_done"], 1)
                if t2:
                    pe.wait_ge(E["qkb_kept"], t2.done)
                    for r in range(2):
                        for h in range(H):
                            last = T.matmul(b01[:, r * 512 + h * P:r * 512 + (h + 1) * P], c["pick"][:, h, :],
                                            bc[t2.parity][:, r, :], start=True, stop=True)
                    last.then_inc(E["bcast_done"], 1)
                if t1:
                    pe.wait_ge(E["rows_done"], t1.done)
                    for r in range(ROWS):
                        last = T.matmul(pr_ps[:, 640 + r * H:640 + (r + 1) * H], row[:, r, :], c["ident"][0:H, 0:H],
                                        start=True, stop=True)
                    last.then_inc(E["cols_turned"], 1)
                if t2:
                    if t3:
                        pe.wait_ge(E["out_read"], t3.done)
                    pe.wait_ge(E["xc_done"], t2.done)
                    for g in range(2):
                        last = T.matmul(b23[:, g * P:(g + 1) * P], xc[t2.parity][:, 2 + g, :], xc[t2.parity][:, 4 + g, :],
                                        start=True, stop=True)
                    for n, rows in enumerate((DH, P)):
                        for h in range(H):
                            at = DEC + (n * H + h) * batch
                            last = T.matmul(b23[0:rows, at:at + batch], c["pick"][:, h, 0:rows], ends[t2.parity][:, n, 0:batch],
                                            start=True, stop=True)
                    for h in range(H):
                        last = T.matmul(b23[:, 512 + h * P:512 + (h + 1) * P], qkb[:, H + h, :], qkb[:, h, :], start=True, stop=True)
                    last.then_inc(E["qk_done"], 1)
                attend(0)
                attend(1)
                if t2:
                    pe.wait_ge(E["dec_ready"], t2.done)
                    for k in range(4):
                        last = T.transpose(b01[:, k * P:(k + 1) * P], xc[t2.parity][:, k, :], c["ident"][:])
                    last.then_inc(E["xsb_turned"], 1)
                if t3:
                    pe.wait_ge(E["xn2_done"], t3.done)
                    for k in range(4):
                        last = T.transpose(b01[:, 512 + k * P:512 + (k + 1) * P], prod[:, k * P:(k + 1) * P], c["ident"][:])
                    last.then_inc(E["h2_turned"], 1)
                attend(2)
                if t3:
                    pe.wait_ge(E["h2_half"], t3.nth(0, 2))
                    for k in range(4):
                        last = T.transpose(b01[:, 512 + k * P:512 + (k + 1) * P], prod[:, (4 + k) * P:(5 + k) * P], c["ident"][:])
                    last.then_inc(E["h2_turned"], 1)
                if t2:
                    pe.wait_ge(E["g_done"], t2.done)
                    pe.wait_ge(E["v1_copied"], t2.done)
                    pe.wait_ge(E["xsb_kept"], t2.done)
                    if later(t2):
                        pe.wait_ge(E["states_done"], t2.i * 1)
                    for h in range(H):
                        last = T.matmul(b01[:, h * W1:(h + 1) * W1], wt[:, h, :], v1[:, h, :], start=True, stop=True)
                    if not sample:
                        for h in range(H):
                            last = T.matmul(b23[:, h * W1:(h + 1) * W1], qkb[:, h, :], cst[:, h, :], start=True, stop=True)
                        last.then_inc(E["nums_done"], 1)
                    else:
                        for h in range(H):
                            if h:
                                pe.wait_ge(scope["n2_used"], h)
                            for half in range(2):
                                last = T.matmul(sc_ps[:, half * 512:half * 512 + 4 * W1].rearrange("p (b e) -> p b e", b=4),
                                                qkb[:, h, :], cst[:, h, 4 * half:4 * half + 4, :], start=True, stop=True)
                            last.then_inc(scope["n2_done"], 1)
                    pe.wait_ge(E["xd_done"], t2.done)
                    for h in range(H):
                        last = T.matmul(b23[:, 512 + h * DH:512 + (h + 1) * DH], gt[:, h, :], xdt[:, h, :], start=True,
                                        stop=True)
                    if not sample:
                        for h in range(H):
                            last = T.matmul(b23[:, 768 + h * DH:768 + (h + 1) * DH], xc[t2.parity][:, 4 + h // 2, :],
                                            hst[:, h, :], start=True, stop=True)
                    last.then_inc(E["ys_done"], 1)
                attend(3)
                if t2:
                    kb = KB - QB
                    if not sample:
                        pe.wait_ge(E["vn_done"], t2.done)
                        for g in range(H):
                            last = T.matmul(sc_ps[:, 640 + g * DH:640 + (g + 1) * DH], scope["ws_t"][:, g, :],
                                            vn[:, g * DH:(g + 1) * DH], start=True, stop=True)
                        last.then_inc(E["f_done"], 1)
                        pe.wait_ge(E["v1w_done"], t2.done)
                        pe.wait_ge(E["xwl_done"], t2.done)
                        pe.wait_ge(E["nums_read"], t2.done)
                        if t3:
                            pe.wait_ge(E["h2_half"], t3.nth(1, 2))
                        for h in range(H):
                            T.matmul(b01[0:DH, 512 + 0 + h * DH:512 + (h + 1) * DH], pb[:, kb + h * DH:kb + (h + 1) * DH],
                                     v1w[:, h, 0:DH], start=True, stop=True)
                        for h in range(H):
                            T.matmul(b01[0:DH, 768 + h:768 + h + 1], pb[:, kb + h * DH:kb + (h + 1) * DH],
                                     v1w[:, h, DH:W1], start=True, stop=True)
                        for h in range(H):
                            last = T.matmul(b23[:, h * DH:(h + 1) * DH], xs_b[:, GW + h // 2 * P:GW + (h // 2 + 1) * P],
                                            xwl[:, h, :], start=True, stop=True)
                        last.then_inc(E["state_ps_done"], 1)
                    else:
                        for h in range(H):
                            pe.wait_ge(scope["n2_used"], H + h)
                            T.matmul(sc_ps[:, 0:512].rearrange("p (b e) -> p b e", b=NB), xc[t2.parity][:, 4 + h // 2, :],
                                     hst[:, h, :, :], start=True, stop=True).then_inc(scope["n2_done"], 1)
                        for h in range(H):
                            pe.wait_ge(scope["n2_used"], 2 * H + h)
                            pe.wait_ge(scope["vws_done"], h + 1)
                            for half in range(2):
                                last = T.matmul(sc_ps[0:DH, half * 512:half * 512 + 4 * W1], pb[:, kb + h * DH:kb + (h + 1) * DH],
                                                scope["vws"][h % 2][:, 4 * half * W1:(4 * half + 4) * W1], start=True, stop=True)
                            last.then_inc(scope["n2_done"], 1)
                        for h in range(H):
                            pe.wait_ge(scope["n2_used"], 3 * H + h)
                            pe.wait_ge(scope["vws_done"], H + h + 1)
                            T.matmul(sc_ps[:, 0:512], xs_b[:, GW + h // 2 * P:GW + (h // 2 + 1) * P],
                                     scope["vws"][h % 2][:, 0:512], start=True, stop=True).then_inc(scope["n2_done"], 1)
                        pe.wait_ge(E["vn_done"], t2.done)
                        pe.wait_ge(scope["n2_used"], 4 * H)
                        for g in range(H):
                            last = T.matmul(sc_ps[:, 640 + g * DH:640 + (g + 1) * DH], scope["ws_t"][:, g, :],
                                            vn[:, g * DH:(g + 1) * DH], start=True, stop=True)
                        last.then_inc(E["f_done"], 1)

            def scalar_iteration(act, step, t1, t2, t3):
                a = nc.scalar
                if t3:
                    act.wait_ge(E["y_turned"], t3.done)
                    if later(t3):
                        act.wait_ge(E["tile_stored"], t3.i * 32)
                    a.activation(yt[:], b01[:].rearrange("p (k t) -> p k t", k=KD), ACT.Copy).then_inc(E["yt_kept"], 1)
                if t1:
                    p, uv, sz = pt_a[t1.parity], uvs[t1.parity], szs[t1.parity]
                    act.wait_ge(s_load_a[t1.parity], t1.pair * 48 + 48)
                    if later(t1, 2):
                        act.wait_ge(E["y_ready"], t1.i - 1)
                    step(a.activation(uv[:], p[:, UD - A0:UD - A0 + 2 * GW], ACT.Gelu_apprx_tanh))
                    a.activation(sz[:], p[:, ZC - A0:ZC - A0 + GW], ACT.Silu).then_inc(E["gelu_done"], 1)
                    if sample:
                        act.wait_ge(scope["xt_loaded"], 16 * scope["xt_dmas"])
                    if later(t1):
                        act.wait_ge(E["xc_done"], t1.i * 1)
                    for k in range(KX):
                        ins = a.activation(chan(acc, k), x_view(t1, 0)[:, k], ACT.Identity, scale=taps_c[:, 0, k:k + 1],
                                           bias=taps_c[:, 4, k:k + 1])
                    ins.then_inc(E["tap0_done"], 1)
                if t2:
                    act.wait_ge(E["qkb_turned"], t2.done)
                    a.activation(qkb[:], b01[0:DH, :].rearrange("p (a t) -> p a t", a=2 * H), ACT.Copy
                                 ).then_inc(E["qkb_kept"], 1)
                if t1:
                    act.wait_ge(E["conv_done"], t1.done)
                    if later(t1, 2):
                        act.wait_ge(E["ys_done"], t1.i - 1)
                    a.activation(xc[t1.parity][:], acc[:], ACT.Silu).then_inc(E["xc_done"], 1)
                    act.wait_ge(E["rows_in"], t1.done)
                    step(a.activation(soft[:], u_in[:], ACT.Abs))
                    step.settle()
                    step(a.activation(soft[:], soft[:], ACT.Exp, scale=-1.0))
                    step.settle()
                    a.activation(soft[:], soft[:], ACT.Ln, bias=1.0).then_inc(E["softplus_done"], 1)
                    act.wait_ge(E["args_done"], t1.done)
                    a.activation(row[:, 0:5, :], arg[:], ACT.Exp).then_inc(E["rows_exp"], 1)
                    w = blocks(t1.i) * P

                def probs(h):
                    if not t1 or sample:
                        return
                    act.wait_ge(E["max_done"], t1.nth(h, H))
                    if h == 0 and later(t1):
                        act.wait_ge(E["ya_done"], t1.i * 1)
                    a.activation(prob[h % 2][:, 0:w], score[h % 2][:, 0:w], ACT.Exp, bias=nmax[:, h:h + 1],
                                 accum_out=total[:, h:h + 1]).then_inc(E["prob_done"], 1)

                def keep_probs(h):
                    if not t1 or sample:
                        return
                    act.wait_ge(E["probs_turned"], t1.nth(h, H))
                    if h >= 2:
                        act.wait_ge(E["pv_done"], t1.nth(h - 2, H))
                    elif later(t1):
                        act.wait_ge(E["pv_done"], t1.i * H + (h - 1))
                    a.activation(prob_t[h % 2][:, 0:w], pr_ps[:, 0:w], ACT.Copy).then_inc(E["prob_kept"], 1)

                probs(0)
                keep_probs(0)
                if t2:
                    act.wait_ge(E["dec_ready"], t2.done)
                    a.activation(dec_arg[:], dec_arg[:], ACT.Exp).then_inc(E["dec_exp"], 1)
                probs(1)
                if t3:
                    act.wait_ge(E["x2_done"], t3.done)
                    a.activation(prod[:], xr[:], ACT.Square, accum_out=ss2[:]).then_inc(E["sq2_done"], 1)
                keep_probs(1)
                if t3:
                    act.wait_ge(E["rstd_2_done"], t3.done)
                    a.activation(prod[:], xr[:], ACT.Copy, scale=rs2[:, 0:1]).then_inc(E["xn2_done"], 1)
                probs(2)
                if t2:
                    act.wait_ge(E["xsb_turned"], t2.done)
                    if later(t2) and not sample:
                        act.wait_ge(E["state_ps_done"], t2.i * 1)
                    a.activation(xs_b[:], b01[:, 0:512], ACT.Copy).then_inc(E["xsb_kept"], 1)
                    act.wait_ge(s_load_b[t2.parity], t2.pair * 16 + 16)
                    if later(t2):
                        act.wait_ge(E["y_ready"], t2.i * 1)
                    a.activation(to[:], pt_b[t2.parity][:, OB - QB:OB - QB + GW], ACT.Tanh, scale=0.5
                                 ).then_inc(E["gate_tanh"], 1)

                def keep_h2(half):
                    if not t3:
                        return
                    act.wait_ge(E["h2_turned"], t3.nth(half, 2))
                    for k in range(4):
                        kk = half * 4 + k
                        if not sample:
                            ins = a.activation(yt[:, kk, :], b01[:, 512 + k * P:512 + (k + 1) * P], ACT.Identity,
                                               scale=keep["ffn_scale"][:, kk, 0:1], bias=keep["ffn_shift"][:, kk, 0:1])
                        else:
                            for b in range(NB):
                                ins = a.activation(yt[:, kk, b * TS:(b + 1) * TS],
                                                   b01[:, 512 + k * P + b * TS:512 + k * P + (b + 1) * TS],
                                                   ACT.Identity, scale=keep["ffn_scale"][:, kk, 1 + b:2 + b],
                                                   bias=keep["ffn_shift"][:, kk, 1 + b:2 + b])
                    ins.then_inc(E["h2_half"], 1)

                keep_h2(0)
                keep_probs(2)
                probs(3)
                keep_h2(1)
                keep_probs(3)
                if t2:
                    act.wait_ge(E["yz_done"], t2.done)
                    a.activation(xdt[:].rearrange("p h d -> p (h d)"), yz[:], ACT.Square, accum_out=ssc[:]
                                 ).then_inc(E["sq_c_done"], 1)

            def pool_iteration(pool, step, t1, t2, t3):
                g = nc.gpsimd

                def rstd(out, mid, square_sum, at, width, signal):
                    step(g.tensor_tensor(mid, square_sum, c["per_width"][:, at:at + width], ALU.mult))
                    step.settle()
                    step(g.tensor_tensor(mid, mid, c["eps"][:, 0:width], ALU.add))
                    step.settle()
                    g.tensor_tensor(out, mid, c["minus_half"][:, 0:width], ALU.pow).then_inc(E[signal], 1)

                if t2:
                    cl = col[t2.parity]
                    pool.wait_ge(s_load_b[t2.parity], t2.pair * 16 + 16)
                    pool.wait_ge(E["cols_kept"], t2.done)
                    if later(t2):
                        pool.wait_ge(E["ys_done"], t2.i * 1)
                        if not sample:
                            pool.wait_ge(E["state_ps_done"], t2.i * 1)
                    g.tensor_tensor(v1[:, :, 0:DH], pt_b[t2.parity][:, VB - QB:VB - QB + GW].rearrange(heads, h=H),
                                    c["ones"][:, 0:1].unsqueeze(2).to_broadcast([P, H, DH]), ALU.mult
                                    ).then_inc(E["v1_copied"], 1)
                    pool.wait_ge(E["v1_copied"], t2.done)
                    g.tensor_tensor(v1w[:], v1[:], spread(cl[:, R_WB, :], 2, W1), ALU.mult).then_inc(E["v1w_done"], 1)
                    pool.wait_ge(E["var_done"], t2.done)
                    step(g.tensor_tensor(rsd_m[:], mv[:, 1:2], c["eps"][:, 0:1], ALU.add))
                    step.settle()
                    g.tensor_tensor(rs_d[:], rsd_m[:], c["minus_half"][:, 0:1], ALU.pow).then_inc(E["rstd_d_done"], 1)
                    pool.wait_ge(E["dec_exp"], t2.done)
                    g.tensor_tensor(dec_arg[:], dec_arg[:], spread(mask[:], 1, 2 * H), ALU.mult).then_inc(E["dec_masked"], 1)
                if t3:
                    pool.wait_ge(E["sq2_done"], t3.done)
                    rstd(rs2[:], rs2_m[:], ss2[:], H + 1, 1, "rstd_2_done")
                if t2:
                    pool.wait_ge(E["xsb_kept"], t2.done)
                    if later(t2):
                        pool.wait_ge(E["sq_c_done"], t2.i * 1)
                    xs = xs_b[:, 0:GW].rearrange(heads, h=H)
                    g.tensor_tensor(xdt[:], xs, spread(cl[:, R_DT, :], 2, DH), ALU.mult).then_inc(E["xd_done"], 1)
                    g.tensor_tensor(xwl[:], xs, spread(cl[:, R_WC, :], 2, DH), ALU.mult).then_inc(E["xwl_done"], 1)
                    g.tensor_tensor(xsk[:], xs, spread(skip[:], 2, DH), ALU.mult).then_inc(E["skip_done"], 1)
                    pool.wait_ge(E["yb_centred"], t2.done)
                    rstd(rsb[:], rsb_m[:], ssb[:], 0, H, "rstd_b_done")
                    pool.wait_ge(E["sq_c_done"], t2.done)
                    rstd(rsc[:], rsc_m[:], ssc[:], H, 1, "rstd_c_done")

            def vector_iteration(dve, step, t1, t2, t3):
                v = nc.vector
                if t1:
                    dve.wait_ge(E["rows_turned"], t1.done)
                    step(v.tensor_scalar(u_in[:, 0, :], sc_ps[0:H, 640 + P:640 + 2 * P], row_par[:, 1:2], -1.0, ALU.add, ALU.mult))
                    step(v.tensor_scalar(ig[:], sc_ps[0:H, 640:640 + P], row_par[:, 0:1], None, ALU.add))
                    v.tensor_scalar(u_in[:, 1, :], sc_ps[0:H, 640 + 2 * P:640 + 3 * P], row_par[:, 2:3], None, ALU.add
                                    ).then_inc(E["rows_in"], 1)
                    if not sample:
                        dve.wait_ge(E["qk_turned"], t1.done)
                        qk = pr_ps[:, 0:512].rearrange("p (a t) -> p a t", a=4)
                        v.tensor_copy(q_z[0:64, 0:4:2, :], qk[0:64, 0:2, :]).then_inc(E["qk_kept"], 1)
                        v.tensor_copy(q_z[64:128, 1:4:2, :], qk[64:128, 0:2, :]).then_inc(E["qk_kept"], 1)
                        v.tensor_copy(k_t[:, :, bass.ds(t1.i * P, P)], qk[:, 2:4, :]).then_inc(E["qk_kept"], 1)
                    dve.wait_ge(E["tap0_done"], t1.done)
                    for tap in range(1, 4):
                        for k in range(KX):
                            ins = v.scalar_tensor_tensor(chan(acc, k), x_view(t1, tap)[:, k], taps_c[:, tap, k:k + 1],
                                                         chan(acc, k), ALU.mult, ALU.add)
                        if tap < 3:
                            step(ins)
                            step.settle()
                    ins.then_inc(E["conv_done"], 1)

                def scores(h):
                    if not t1 or sample:
                        return
                    w = blocks(t1.i) * P
                    dve.wait_ge(E["scores_done"], t1.nth(h, H))
                    if h >= 2:
                        dve.wait_ge(E["probs_turned"], t1.nth(h - 2, H))
                    v.scalar_tensor_tensor(score[h % 2][:, 0:w], sc_ps[:, 0:w], DH ** -0.5,
                                           band[:, h, BAND - w:BAND], ALU.mult, ALU.add).then_inc(E["score_read"], 1)
                    dve.wait_ge(E["score_read"], t1.nth(h, H))
                    v.tensor_reduce(nmax[:, h:h + 1], score[h % 2][:, 0:w], AX, ALU.max, negate=True
                                    ).then_inc(E["max_done"], 1)

                scores(0)
                if t1:
                    bcj = bc[t1.parity]
                    dve.wait_ge(E["softplus_done"], t1.done)
                    step(v.scalar_tensor_tensor(sp_[:], u_in[:], 0.0, soft[:], ALU.max, ALU.add))
                    step.settle()
                    step(v.tensor_scalar(la, sp_[:, 1, :], row_par[:, 4:5], None, ALU.mult))
                    step(v.tensor_copy(row[:, R_DT, :], sp_[:, 1, :]))
                    segments = [(b * TS, (b + 1) * TS) for b in range(NB)] if sample else [(0, P)]
                    for lo, hi in segments:
                        ins = v.tensor_tensor_scan(nb[:, lo:hi], c["ones"][0:H, lo:hi], sp_[:, 0, lo:hi], 0.0, ALU.mult, ALU.add)
                    step(ins)
                    step.settle()
                    for lo, hi in segments:
                        ins = v.tensor_tensor_scan(arg[:, 3, lo:hi], c["ones"][0:H, lo:hi], u_in[:, 0, lo:hi], 0.0, ALU.mult, ALU.add)
                    step(v.tensor_tensor(row[:, R_A, :], ig[:], nb[:], ALU.add))
                    step.settle()
                    for n, (lo, hi) in enumerate(segments):
                        ins = v.tensor_tensor_scan(mx[:, lo:hi], row[:, R_A, lo:hi], row[:, R_A, lo:hi], m0[:, n:n + 1],
                                                   ALU.max, ALU.max)
                    step(v.tensor_copy(bcj[:, 1, :], arg[:, 3, :]))
                    step.settle()
                    step(v.tensor_scalar(row[:, R_NCS, :], arg[:, 3, :], -1.0, None, ALU.mult))
                    step(v.tensor_tensor(arg[:, 1, :], nb[:], mx[:], ALU.subtract))
                    step(v.tensor_scalar(bcj[:, 0, :], mx[:], -1.0, None, ALU.mult))
                    if not sample:
                        step(v.tensor_scalar(arg[:, 0, :], mx[:], m0[:, 0:1], -1.0, ALU.subtract, ALU.mult))
                        step(v.tensor_scalar(arg[:, 2, :], row[:, R_A, :], mx[:, P - 1:P], None, ALU.subtract))
                        step(v.tensor_scalar(arg[:, 4, :], arg[:, 3, :], arg[:, 3, P - 1:P], -1.0, ALU.subtract, ALU.mult))
                        step.settle()
                        v.tensor_tensor(m0[:], mx[:, P - 1:P], nb[:, P - 1:P], ALU.subtract).then_inc(E["args_done"], 1)
                    else:
                        def streams(ap):
                            return ap.rearrange("h (b t) -> h b t", b=NB)

                        step(v.tensor_tensor(streams(arg[:, 0, :]), spread(m0[:], 2, TS), streams(mx[:]), ALU.subtract))
                        step(v.tensor_tensor(streams(arg[:, 2, :]), streams(row[:, R_A, :]), spread(mx[:, TS - 1:P:TS], 2, TS),
                                             ALU.subtract))
                        step(v.tensor_tensor(streams(arg[:, 4, :]), spread(arg[:, 3, TS - 1:P:TS], 2, TS),
                                             streams(arg[:, 3, :]), ALU.subtract))
                        step.settle()
                        v.tensor_tensor(m0[:], mx[:, TS - 1:P:TS], nb[:, TS - 1:P:TS], ALU.subtract).then_inc(E["args_done"], 1)
                if t2:
                    dve.wait_ge(E["cols_kept"], t2.done)
                    dve.wait_ge(E["bcast_done"], t2.done)
                    if later(t2):
                        dve.wait_ge(E["g_done"], t2.i * 1)
                    for n, r in enumerate((R_A, R_NCS)):
                        for h in range(H):
                            at = n * 512 + h * P
                            ins = v.tensor_scalar(dec_arg[:, n * H + h, :], b01[:, at:at + P], col[t2.parity][:, r, h:h + 1], 0.0,
                                                  ALU.add, ALU.min)
                    ins.then_inc(E["dec_ready"], 1)
                if t1:
                    dve.wait_ge(E["rows_exp"], t1.done)
                    n_last = slice(TS - 1, P, TS) if sample else slice(P - 1, P)
                    step(v.tensor_copy(ends[t1.parity][:, 0, 0:batch], row[:, R_INTER, n_last]))
                    step(v.tensor_copy(ends[t1.parity][:, 1, 0:batch], row[:, R_CS, n_last]))
                    v.tensor_tensor(row[:, R_WC, :], row[:, R_WC, :], row[:, R_DT, :], ALU.mult).then_inc(E["rows_done"], 1)
                if t2:
                    step(v.bn_stats(stats[:], uvs[t2.parity][:, GW:2 * GW]))
                if t3:
                    dve.wait_ge(E["out_done"], t3.done)
                    dve.wait_ge(E["xres_loaded"], t3.i * 16 + 16)
                    if later(t3):
                        dve.wait_ge(E["h2_turned"], t3.i * 2)
                    v.tensor_tensor(prod[:], b23[:], keep["mix_gate"][:, 1 if sample else 0, :], ALU.mult
                                    ).then_inc(E["out_read"], 1)
                    dve.wait_ge(E["out_read"], t3.done)
                    v.tensor_tensor(xr[:], xr[:], prod[:], ALU.add).then_inc(E["x2_done"], 1)
                elif t2:
                    step.settle()
                if t2:
                    v.bn_aggr(mv[:], stats[:]).then_inc(E["var_done"], 1)
                if t1:
                    dve.wait_ge(E["cols_turned"], t1.done)
                    v.tensor_copy(col[t1.parity][:], pr_ps[:, 640:640 + ROWS * H].rearrange("p (r h) -> p r h", r=ROWS)
                                  ).then_inc(E["cols_kept"], 1)
                scores(1)
                scores(2)
                if t2:
                    uv, sz, cl, yj = uvs[t2.parity], szs[t2.parity], col[t2.parity], y[t2.parity]
                    dve.wait_ge(E["rstd_d_done"], t2.done)
                    if later(t2):
                        dve.wait_ge(E["f_done"], t2.i * 1)
                    step(v.tensor_scalar(vn[:], uv[:, GW:2 * GW], mv[:, 0:1], rs_d[:, 0:1], ALU.subtract, ALU.mult))
                    step.settle()
                    v.tensor_tensor(vn[:], vn[:], gd[:], ALU.mult).then_inc(E["vn_done"], 1)
                    dve.wait_ge(E["dec_masked"], t2.done)
                    dve.wait_ge(E["qk_done"], t2.done)
                    step(v.scalar_tensor_tensor(wt[:], b23[:, 512:1024].rearrange("p (h t) -> p h t", h=H), DH ** -0.5,
                                                dec_arg[:, 0:H, :], ALU.mult, ALU.mult))
                    for grp in range(2):
                        ins = v.tensor_tensor(gt[:, 2 * grp:2 * grp + 2, :], spread(b23[:, grp * P:(grp + 1) * P], 1, 2),
                                              dec_arg[:, H + 2 * grp:H + 2 * grp + 2, :], ALU.mult)
                    ins.then_inc(E["g_done"], 1)
                scores(3)
                if t2:
                    if not sample:
                        dve.wait_ge(E["nums_done"], t2.done)
                        step(v.tensor_tensor(nums[:], b23[:, 0:H * W1].rearrange("p (h e) -> p h e", h=H),
                                             spread(cl[:, R_INTER, :], 2, W1), ALU.mult))
                    else:
                        wide = scope["wide"]
                        for h in range(H):
                            dve.wait_ge(scope["n2_done"], h + 1)
                            for half in range(2):
                                ins = v.tensor_tensor(wide[:, 4 * half:4 * half + 4, :],
                                                      sc_ps[:, half * 512:half * 512 + 4 * W1].rearrange("p (b e) -> p b e", b=4),
                                                      spread(c["stream"][:, 4 * half:4 * half + 4], 2, W1), ALU.mult)
                            ins.then_inc(scope["n2_used"], 1)
                            dve.wait_ge(scope["n2_used"], h + 1)
                            step(v.tensor_reduce(nums[:, h, :], wide[:].rearrange("p b e -> p e b"), AX, ALU.add))
                            step.settle()
                        step(v.tensor_tensor(nums[:], nums[:], spread(cl[:, R_INTER, :], 2, W1), ALU.mult))
                    step.settle()
                    v.tensor_tensor(nums[:], nums[:], b01[:, 0:H * W1].rearrange("p (h e) -> p h e", h=H), ALU.add
                                    ).then_inc(E["nums_read"], 1)
                    dve.wait_ge(E["nums_read"], t2.done)
                    dn = nums[:, :, DH]
                    step(v.scalar_tensor_tensor(den[:], dn, -1.0, dn, ALU.mult, ALU.max))
                    step.settle()
                    step(v.tensor_tensor(den[:], den[:], cl[:, R_FLOOR, :], ALU.max))
                    step.settle()
                    step(v.reciprocal(den[:], den[:]))
                    step.settle()
                    step(v.tensor_tensor(hb[:], nums[:, :, 0:DH], spread(den[:], 2, DH), ALU.mult))
                    step.settle()
                    step(v.tensor_reduce(sums[:], hb[:], AX, ALU.add))
                    step.settle()
                    step(v.tensor_scalar(sums[:], sums[:], 1.0 / DH, None, ALU.mult))
                    step.settle()
                    step(v.tensor_tensor(hb[:], hb[:], spread(sums[:], 2, DH), ALU.subtract))
                    step.settle()
                    step(v.tensor_tensor(sq[:], hb[:], hb[:], ALU.mult))
                    step.settle()
                    v.tensor_reduce(ssb[:], sq[:], AX, ALU.add).then_inc(E["yb_centred"], 1)
                    dve.wait_ge(E["ys_done"], t2.done)
                    yz3 = yz[:].rearrange(heads, h=H)
                    if not sample:
                        step(v.tensor_tensor(yz3, b23[:, 768:1024].rearrange(heads, h=H),
                                             spread(cl[:, R_CS, :], 2, DH), ALU.mult))
                    else:
                        for h in range(H):
                            dve.wait_ge(scope["n2_done"], H + h + 1)
                            v.tensor_tensor(wide[:, :, 0:DH], sc_ps[:, 0:512].rearrange("p (b e) -> p b e", b=NB),
                                            spread(c["stream"][:], 2, DH), ALU.mult).then_inc(scope["n2_used"], 1)
                            dve.wait_ge(scope["n2_used"], H + h + 1)
                            step(v.tensor_reduce(yz3[:, h, :], wide[:, :, 0:DH].rearrange("p b e -> p e b"), AX, ALU.add))
                            step.settle()
                        step(v.tensor_tensor(yz3, yz3, spread(cl[:, R_CS, :], 2, DH), ALU.mult))
                    step.settle()
                    step(v.tensor_tensor(yz[:], yz[:], b23[:, 512:768], ALU.add))
                    dve.wait_ge(E["skip_done"], t2.done)
                    step.settle()
                    step(v.tensor_tensor(yz3, yz3, xsk[:], ALU.add))
                    step.settle()
                    v.tensor_tensor(yz[:], yz[:], sz[:], ALU.mult).then_inc(E["yz_done"], 1)
                    dve.wait_ge(E["rstd_b_done"], t2.done)
                    step(v.tensor_tensor(hb[:], hb[:], spread(rsb[:], 2, DH), ALU.mult))
                    dve.wait_ge(E["gate_tanh"], t2.done)
                    step.settle()
                    step(v.scalar_tensor_tensor(sq[:].rearrange("p h d -> p (h d)"), to[:], 1.0,
                                                hb[:].rearrange("p h d -> p (h d)"), ALU.add, ALU.mult))
                    step.settle()
                    step(v.tensor_tensor(yj[:, GW:2 * GW], sq[:].rearrange("p h d -> p (h d)"), gb[:], ALU.mult))
                if t1 and not sample:
                    dve.wait_ge(E["pv_done"], t1.nth(H - 1, H))
                    if later(t1, 2):
                        dve.wait_ge(E["y_turned"], t1.i - 1)
                    step(v.reciprocal(inv[:], total[:]))
                    step.settle()
                    v.tensor_tensor(y[t1.parity][:, 0:GW].rearrange(heads, h=H),
                                    pr_ps[:, 768:1024].rearrange(heads, h=H), spread(inv[:], 2, DH), ALU.mult
                                    ).then_inc(E["ya_done"], 1)
                elif t1:
                    step(v.tensor_copy(y[t1.parity][:, 0:GW], ya_sample[:]))
                if t2:
                    if not sample:
                        dve.wait_ge(E["state_ps_done"], t2.done)
                        step(v.tensor_tensor(cst[:], cst[:], spread(b23[0:DH, DEC:DEC + H], 2, W1), ALU.mult))
                        step(v.tensor_tensor(hst[:], hst[:], spread(b23[:, DEC + H:DEC + 2 * H], 2, DH), ALU.mult))
                        step.settle()
                        step(v.scalar_tensor_tensor(cst[:, :, 0:DH], b01[0:DH, 512:768].rearrange(heads, h=H),
                                                    DH ** -0.5, cst[:, :, 0:DH], ALU.mult, ALU.add))
                        step(v.scalar_tensor_tensor(cst[:, :, DH], b01[0:DH, 768:768 + H], DH ** -0.5, cst[:, :, DH],
                                                    ALU.mult, ALU.add))
                        v.tensor_tensor(hst[:], hst[:], b23[:, 0:256].rearrange("p (h e) -> p h e", h=H), ALU.add
                                        ).then_inc(E["states_done"], 1)
                    else:
                        vws = scope["vws"]

                        def weigh(n):
                            h = n % H
                            if n >= 2:
                                dve.wait_ge(scope["n2_done"], 2 * H + n - 1)
                            width, src = (W1, v1w) if n < H else (DH, xwl)
                            dst = vws[n % 2][:, 0:NB * width].rearrange("p (b e) -> p b e", b=NB)
                            v.tensor_tensor(dst, spread(src[:, h, :], 1, NB), spread(c["stream"][:], 2, width), ALU.mult
                                            ).then_inc(scope["vws_done"], 1)

                        dve.wait_ge(E["v1w_done"], t2.done)
                        dve.wait_ge(E["xwl_done"], t2.done)
                        weigh(0)
                        weigh(1)
                        for n in range(2 * H):
                            h = n % H
                            if n < H:
                                dec = spread(b23[0:DH, DEC + h * NB:DEC + (h + 1) * NB], 2, W1)
                                step(v.tensor_tensor(cst[:, h], cst[:, h], dec, ALU.mult))
                                dve.wait_ge(scope["n2_done"], 2 * H + n + 1)
                                step.settle()
                                for half in range(2):
                                    b4 = slice(4 * half, 4 * half + 4)
                                    ins = v.scalar_tensor_tensor(
                                        cst[:, h, b4, :],
                                        sc_ps[0:DH, half * 512:half * 512 + 4 * W1].rearrange("p (b e) -> p b e", b=4),
                                        DH ** -0.5, cst[:, h, b4, :], ALU.mult, ALU.add)
                                ins.then_inc(scope["n2_used"], 1)
                            else:
                                dec = spread(b23[:, DEC + (H + h) * NB:DEC + (H + h + 1) * NB], 2, DH)
                                step(v.tensor_tensor(hst[:, h], hst[:, h], dec, ALU.mult))
                                dve.wait_ge(scope["n2_done"], 2 * H + n + 1)
                                step.settle()
                                ins = v.tensor_tensor(hst[:, h], hst[:, h], sc_ps[:, 0:512].rearrange("p (b e) -> p b e", b=NB),
                                                      ALU.add)
                                ins.then_inc(scope["n2_used"], 1)
                            if n + 2 < 2 * H:
                                weigh(n + 2)
                        dve.wait_ge(scope["n2_used"], 4 * H)
                        v.tensor_copy(stats[:, 0:1], stats[:, 0:1]).then_inc(E["states_done"], 1)
                    dve.wait_ge(E["f_done"], t2.done)
                    step(v.tensor_tensor(fd, sc_ps[:, 640:640 + GW].rearrange(heads, h=H),
                                         spread(scope["bs"][:], 2, DH), ALU.add))
                    step.settle()
                    step(v.tensor_tensor(yj[:, 3 * GW:4 * GW].rearrange(heads, h=H), fd,
                                         uv[:, 0:GW].rearrange(heads, h=H), ALU.mult))
                    dve.wait_ge(E["rstd_c_done"], t2.done)
                    step.settle()
                    v.scalar_tensor_tensor(yj[:, 2 * GW:3 * GW], yz[:], rsc[:, 0:1], gc[:], ALU.mult, ALU.mult
                                           ).then_inc(E["y_ready"], 1)

            return tensor_iteration, scalar_iteration, pool_iteration, vector_iteration

        def prompt_iterations(engine, iteration, steps=None):
            def run(n, front, middle, back):
                args = [Tile(*at) if at else None for at in (front, middle, back)]
                if steps:
                    iteration(engine, steps, *args)
                else:
                    iteration(engine, *args)

            def at(n):
                return (n // 2, n % 2) if 0 <= n < NT else None

            for n in range(NPAST):
                if steps:
                    steps.next()
                run(n, at(n), at(n - 1), at(n - 2))
            if steps:
                steps.next()
                first = steps.base
            with engine.Fori(NPAST // 2, NT // 2) as pair:
                if steps:
                    steps.base = pair * (2 * steps.per_tile) + (first - NPAST * steps.per_tile)
                    steps.count = 0
                run(None, (pair, 0), (pair - 1, 1), (pair - 1, 0))
                run(None, (pair, 1), (pair, 0), (pair - 1, 1))
                assert not steps or steps.count == 2 * steps.per_tile, (steps.count, steps.per_tile)
            if steps:
                steps.base, steps.count = first + (NT - NPAST) * steps.per_tile, 0
            for n in (NT, NT + 1):
                if steps:
                    steps.next()
                run(n, at(n), at(n - 1), at(n - 2))

        def sample_iterations(engine, iteration, steps=None):
            t = Tile(NT // 2, 0)
            for parts in ((t, None, None), (None, t, None), (None, None, t)):
                if steps:
                    steps.next()
                    iteration(engine, steps, *parts)
                else:
                    iteration(engine, *parts)

        with ExitStack() as pctx:
            psb, _ = new_pools(nc, pctx)
            scope = {
                "sample": False, "mask": c["tri"], "ws_t": ws_t, "bs": bs,
                "band": psb("band", [P, H, BAND]), "k_t": psb("k_t_p", [P, 2, SEQ]), "v_all": psb("v_all", [P, NT, GW]),
                "q_z": psb("q_z_p", [P, H, P]), "score": [psb(f"score{n}", [P, BAND]) for n in range(2)],
                "prob_t": [psb(f"prob_t{n}", [P, BAND]) for n in range(2)],
                "nmax": psb("nmax", [P, H]), "total": psb("total", [P, H]), "inv": psb("inv", [P, H]),
                "cst": psb("cst", [DH, H, DH + 1]), "hst": psb("hst", [P, H, DH]), "m0": psb("m0", [H, 1]),
            }
            band, cst, hst, m0 = (scope[n] for n in ("band", "cst", "hst", "m0"))
            ssm_out = prod[0:DH, 0:512]
            tensor_iteration, scalar_iteration, pool_iteration, vector_iteration = engines(scope)
            block = pctx.enter_context(nc.Block())

            @block.sync
            def _(sp):
                def load_a(i, j):
                    sp.dma_start(pt_a[j][:, 0:2 * GW], S["proj"][bass.ds(i * P, P), 0:2 * GW]).then_inc(s_load_a[j], 16)
                    sp.dma_start(pt_a[j][:, 2 * GW:], S["proj"][bass.ds(i * P, P), IB:PW]).then_inc(s_load_a[j], 16)
                    sp.dma_start(xt[j][:, 0:KX * (P + 3)].rearrange("p (k t) -> p k t", k=KX),
                                 S["xbc"][:, :, bass.ds(i * P, P + 3)]).then_inc(s_load_a[j], 16)

                def load_b(i, j):
                    sp.dma_start(pt_b[j][:], S["proj"][bass.ds(i * P, P), QB:IB]).then_inc(s_load_b[j], 16)

                def load_x(i):
                    sp.dma_start(xr[:], A["x_prompt"][0, bass.ds(i * P, P), :]).then_inc(E["xres_loaded"], 16)

                params = [(row_par[:, n:n + 1], A[name].rearrange("a h -> h a"))
                          for n, name in enumerate(("b_i_bias", "b_f_bias", "c_dt_bias", "c_a_log"))]
                params += [(skip[:], A["c_d_skip"][0].partition_broadcast(P)),
                           (gb[:], A["b_norm_g"][0].partition_broadcast(P)),
                           (gc[:], A["c_norm_g"][0].partition_broadcast(P)),
                           (gd[:], A["d_norm_g"][0].partition_broadcast(P)),
                           (bs[:], A["d_b_s"][0].rearrange("g t -> t g")),
                           (taps_c[:, 4, :], A["c_conv_b"][0].rearrange("(k p) -> p k", p=P)),
                           (ws_in[:], A["d_w_s"][0].rearrange("g t s -> t g s")),
                           (band[:], rel_tile(S, slice(0, P), slice(0, BAND)))]
                params += [(taps_c[:, n, :], A["c_conv_w"][0, n].rearrange("(k p) -> p k", p=P)) for n in range(4)]
                for dst, src in params:
                    sp.dma_start(dst, src, allow_slow_non_contiguous=True).then_inc(E["params_loaded"], 16)
                assert len(params) == N_PARAMS
                for i in range(2):
                    load_a(i, i)
                for i in range(2):
                    load_b(i, i)
                sp.dma_start(scope["v_all"][:], S["proj"][0:SEQ, VA:VA + GW].rearrange("(n p) d -> p n d", p=P)
                             ).then_inc(E["vall_loaded"], 16)
                load_x(0)
                sp.dma_start(w_out[:], A["w_out"][0].rearrange("(k p) n -> p k n", p=P)).then_inc(E["w_out_loaded"], 16)

                def iteration(front, middle, back, more=True):
                    if front:
                        sp.wait_ge(E["qk_turned"], front.done)
                        sp.wait_ge(E["gelu_done"], front.done)
                        sp.wait_ge(E["conv_done"], front.done)
                        load_a(front.i + 2, front.parity)
                    if back:
                        sp.wait_ge(E["h2_half"], back.nth(1, 2))
                        sp.dma_start(S["x2"][bass.ds(back.i * P, P), :], xr[:]).then_inc(E["tile_stored"], 16)
                        sp.dma_start(S["h2t"][:, :, bass.ds(back.i * P, P)], yt[:]).then_inc(E["tile_stored"], 16)
                        if more:
                            sp.wait_ge(E["tile_stored"], back.i * 32 + 32)
                            load_x(back.i + 1)
                    if middle:
                        sp.wait_ge(E["gate_tanh"], middle.done)
                        sp.wait_ge(E["state_ps_done"], middle.done)
                        load_b(middle.i + 2, middle.parity)

                def tile_at(n, end=NT):
                    return Tile(n // 2, n % 2) if 0 <= n < end else None

                for n in range(NPAST):
                    iteration(tile_at(n), tile_at(n - 1), tile_at(n - 2))
                with sp.Fori(NPAST // 2, NT // 2 - 1) as pair:
                    iteration(Tile(pair, 0), Tile(pair - 1, 1), Tile(pair - 1, 0))
                    iteration(Tile(pair, 1), Tile(pair, 0), Tile(pair - 1, 1))
                for n in range(NT - 2, NT + 2):
                    iteration(tile_at(n, NT - 2), tile_at(n - 1, NT - 2), tile_at(n - 2), more=n < NT + 1)
                sp.wait_ge(E["tile_stored"], 32 * NT)
                sp.wait_ge(E["setup_dve"], 9)
                copies = [(O["p_c_ssm"][0, 0].rearrange("h p n -> p h n"), ssm_out.rearrange("p (h n) -> p h n", h=H)),
                          (O["p_b_c"][0, 0].rearrange("h d e -> d h e"), cst[:, :, 0:DH]),
                          (O["p_b_n"][0, 0].rearrange("h d -> d h"), cst[:, :, DH]),
                          (O["p_b_m"][0].rearrange("a h -> h a"), m0[:]),
                          (O["p_a_k"][0, 0].rearrange("t h d -> t (h d)"), S["proj"][SEQ - HIST:SEQ, KA:KA + GW]),
                          (O["p_a_v"][0, 0].rearrange("t h d -> t (h d)"), S["proj"][SEQ - HIST:SEQ, VA:VA + GW]),
                          (O["s_a_k"][0].rearrange("b t h d -> (b t) (h d)"), S["proj"][SEQ:SEQ + P, KA:KA + GW]),
                          (O["s_a_v"][0].rearrange("b t h d -> (b t) (h d)"), S["proj"][SEQ:SEQ + P, VA:VA + GW])]
                for n in range(3):
                    copies.append((O["p_c_conv"][0, 0, n].rearrange("(k p) -> p k", p=P), S["xbc"][:, :, SEQ + n]))
                for dst, src in copies:
                    sp.dma_start(dst, src, allow_slow_non_contiguous=True).then_inc(s_final, 16)
                sp.wait_ge(s_final, 16 * len(copies))

            @block.tensor
            def _(pe):
                pe.wait_ge(E["params_loaded"], 16 * N_PARAMS)
                for g in range(H):
                    last = nc.tensor.transpose(b01[:, g * P:(g + 1) * P], ws_in[:, g, :], c["ident"][:])
                last.then_inc(E["spatial_turned"], 1)
                pe.wait_ge(E["setup_dve"], 7)
                prompt_iterations(pe, tensor_iteration)
                pe.wait_ge(E["states_done"], NT)
                for h in range(H):
                    last = nc.tensor.transpose(pr_ps[0:DH, h * P:(h + 1) * P], hst[:, h, :], c["ident"][:])
                last.then_inc(E["spatial_turned"], 1)

            @block.scalar
            def _(act):
                step = Steps(act, E["act_step"])
                act.wait_ge(E["params_loaded"], 16 * N_PARAMS)
                nc.scalar.activation(row_par[:, 4:5], row_par[:, 3:4], ACT.Exp).then_inc(E["alog_exp"], 1)
                prompt_iterations(act, scalar_iteration, step)
                steps_of["act"] = step

            @block.gpsimd
            def _(pool):
                step = Steps(pool, E["pool_step"])
                nc.gpsimd.memset(v1[:, :, DH:DH + 1], 1.0).then_inc(s_ones, 1)
                nc.gpsimd.memset(scope["q_z"][:], 0.0).then_inc(s_ones, 1)
                pool.wait_ge(s_ones, 2)
                pool.wait_ge(E["params_loaded"], 16 * N_PARAMS)
                prompt_iterations(pool, pool_iteration, step)
                steps_of["pool"] = step

            @block.vector
            def _(dve):
                step = Steps(dve, E["dve_step"])
                v, ready = nc.vector, E["setup_dve"]
                dve.wait_ge(E["params_loaded"], 16 * N_PARAMS)
                v.memset(cst[:], 0.0).then_inc(ready, 1)
                v.memset(hst[:], 0.0).then_inc(ready, 1)
                v.memset(m0[:], 0.0).then_inc(ready, 1)
                v.memset(band[0:64, :, BAND - 64:BAND], NEG).then_inc(ready, 1)
                v.memset(band[64:128, :, 0:64], NEG).then_inc(ready, 1)
                v.tensor_scalar(gb[:], gb[:], 0.5, None, ALU.mult).then_inc(ready, 1)
                dve.wait_ge(E["spatial_turned"], 1)
                v.tensor_tensor(ws_t[:], b01[:, 0:512].rearrange("p (g t) -> p g t", g=H), spread(c["tri"][:], 1, H),
                                ALU.mult).then_inc(ready, 1)
                dve.wait_ge(E["alog_exp"], 1)
                v.tensor_scalar(row_par[:, 4:5], row_par[:, 4:5], -1.0, None, ALU.mult).then_inc(ready, 1)
                dve.wait_ge(ready, 8)
                dve.wait_ge(s_ones, 2)
                prompt_iterations(dve, vector_iteration, step)
                dve.wait_ge(E["spatial_turned"], 2)
                v.tensor_copy(ssm_out, pr_ps[0:DH, 0:512]).then_inc(ready, 1)
                steps_of["dve"] = step

        with ExitStack() as sctx:
            ssb_, _ = new_pools(nc, sctx)
            W1 = DH + 1
            scope = {
                "sample": True, "mask": c["tri_s"], "ws_t": ssb_("ws_t_s", [P, H, P]), "bs": ssb_("bs_s", [P, H]),
                "cst": ssb_("cst_s", [DH, H, NB, W1]), "hst": ssb_("hst_s", [P, H, NB, DH]), "m0": ssb_("m0_s", [H, NB]),
                "wide": ssb_("wide_m", [P, NB, W1]), "vws": [ssb_(f"vws{n}", [P, NB * W1]) for n in range(2)],
                "n2_done": sem("ms_wide_done"), "n2_used": sem("ms_wide_used"), "vws_done": sem("ms_vws_done"),
                "xt_loaded": sem("ms_xt_loaded"), "xt_dmas": KX * (NB + 1),
            }
            cst, hst, m0 = scope["cst"], scope["hst"], scope["m0"]
            ssm = ssb_("ssm_rows", [DH, NB * H, P])
            ws16, ws_wide = ssb_("ws16", [P, H, TS]), ssb_("ws_wide", [P, H, P])
            s_in, s_ssm, s_t, s_k, s_wide = (sem("ms_in"), sem("ms_ssm_loaded"), sem("ms_turned"), sem("ms_kept"),
                                             sem("ms_spatial_spread"))
            tensor_iteration, scalar_iteration, pool_iteration, vector_iteration = engines(scope)
            block = sctx.enter_context(nc.Block())

            @block.sync
            def _(sp):
                for b in range(NB):
                    rows = slice(b * TS, (b + 1) * TS)
                    sp.dma_start(ws16[rows], A["d_w_s"][0, :, 0:TS, 0:TS].rearrange("g t s -> t g s")).then_inc(s_in, 16)
                    sp.dma_start(scope["bs"][rows], A["d_b_s"][0, :, 0:TS].rearrange("g t -> t g"),
                                 allow_slow_non_contiguous=True).then_inc(s_in, 16)
                sp.dma_start(ssm[:], A["state_c_ssm"][0].rearrange("b h p n -> p (b h) n")).then_inc(s_ssm, 16)
                for b in range(NB):
                    sp.dma_start(cst[:, :, b, 0:DH], A["state_b_c"][0, b].rearrange("h d e -> d h e")).then_inc(s_in, 16)
                    sp.dma_start(cst[:, :, b, DH], A["state_b_n"][0, b].rearrange("h d -> d h"),
                                 allow_slow_non_contiguous=True).then_inc(s_in, 16)
                sp.dma_start(m0[:], A["state_b_m"][0].rearrange("b h -> h b"), allow_slow_non_contiguous=True
                             ).then_inc(s_in, 16)
                third = (PW - IB) // 3
                for n in range(3):
                    sp.dma_start(pt_a[0][:, 2 * GW + n * third:2 * GW + (n + 1) * third],
                                 S["proj"][SEQ:SEQ + P, IB + n * third:IB + (n + 1) * third]).then_inc(s_load_a[0], 16)
                sp.dma_start(pt_b[0][:], S["proj"][SEQ:SEQ + P, QB:IB]).then_inc(s_load_b[0], 16)
                sp.dma_start(xr[:], A["x_sample"].rearrange("b t d -> (b t) d")).then_inc(E["xres_loaded"], 16)
                for k in range(KX):
                    view = xt[0][:].rearrange("p (k b t) -> p k b t", k=KX, b=NB)[:, k]
                    sp.dma_start(view[:, :, 3:], S["xbc_s"][:, k, :].rearrange("p (b t) -> p b t", b=NB)
                                 ).then_inc(scope["xt_loaded"], 16)
                    for b in range(NB):
                        sp.dma_start(view[:, b, 0:3], A["state_c_conv"][0, b, :, k * P:(k + 1) * P].rearrange("j p -> p j"),
                                     allow_slow_non_contiguous=True).then_inc(scope["xt_loaded"], 16)
                sp.wait_ge(E["h2_half"], 2 * (NT + 1))
                out = [(S["h2t"][:, :, SEQ:SEQ + P], yt[:]), (S["x2"][SEQ:SEQ + P, :], xr[:]),
                       (O["s_d_v"][0].rearrange("b t d -> (b t) d"), vn[:]),
                       (O["s_b_m"][0].rearrange("b h -> h b"), m0[:])]
                for b in range(NB):
                    out.append((O["s_b_c"][0, b].rearrange("h d e -> d h e"), cst[:, :, b, 0:DH]))
                    out.append((O["s_b_n"][0, b].rearrange("h d -> d h"), cst[:, :, b, DH]))
                    for n in range(3):
                        out.append((O["s_c_conv"][0, b, n].rearrange("(k p) -> p k", p=P),
                                    S["xbc_s"][:, :, b * TS + TS - 3 + n]))
                for dst, src in out:
                    sp.dma_start(dst, src, allow_slow_non_contiguous=True).then_inc(s_final2, 16)
                sp.wait_ge(s_k, 5 + NB)
                sp.dma_start(O["s_c_ssm"][0].rearrange("b h p n -> p (b h) n"), ssm[:]).then_inc(s_final2, 16)
                sp.wait_ge(s_final2, 16 * (len(out) + 1))

            @block.tensor
            def _(pe):
                pe.wait_ge(s_ssm, 16)
                for h in range(H):
                    if h >= 2:
                        pe.wait_ge(s_k, h - 1)
                    for b in range(NB):
                        last = nc.tensor.transpose(sc_ps[:, h % 2 * 512 + b * DH:h % 2 * 512 + (b + 1) * DH], ssm[:, b * H + h, :],
                                                   c["ident"][0:DH, 0:DH])
                    last.then_inc(s_t, 1)
                pe.wait_ge(s_wide, 1)
                for g in range(H):
                    last = nc.tensor.transpose(b01[:, g * P:(g + 1) * P], ws_wide[:, g, :], c["ident"][:])
                last.then_inc(s_t, 1)
                pe.wait_ge(s_k, 5)
                pe.wait_ge(s_in, 16 * (4 * NB + 1))
                sample_iterations(pe, tensor_iteration)
                for b in range(NB):
                    if b >= 2:
                        pe.wait_ge(s_k, 5 + b - 1)
                    for h in range(H):
                        last = nc.tensor.transpose(pr_ps[0:DH, b % 2 * 512 + h * P:b % 2 * 512 + (h + 1) * P],
                                                   hst[:, h, b, :], c["ident"][:])
                    last.then_inc(s_t, 1)

            @block.scalar
            def _(act):
                sample_iterations(act, scalar_iteration, steps_of["act"].on(act))

            @block.gpsimd
            def _(pool):
                sample_iterations(pool, pool_iteration, steps_of["pool"].on(pool))

            @block.vector
            def _(dve):
                v = nc.vector
                for h in range(H):
                    dve.wait_ge(s_t, h + 1)
                    v.tensor_copy(hst[:, h], sc_ps[:, h % 2 * 512:h % 2 * 512 + 512].rearrange("p (b d) -> p b d", b=NB)).then_inc(s_k, 1)
                dve.wait_ge(s_in, 16 * (4 * NB + 1))
                v.tensor_copy(ws_wide[:].rearrange("p g (b s) -> p g b s", b=NB), spread(ws16[:], 2, NB)
                              ).then_inc(s_wide, 1)
                dve.wait_ge(s_t, 5)
                v.tensor_tensor(scope["ws_t"][:], b01[:, 0:512].rearrange("p (g t) -> p g t", g=H),
                                spread(c["tri_s"][:], 1, H), ALU.mult).then_inc(s_k, 1)
                dve.wait_ge(s_k, 5)
                sample_iterations(dve, vector_iteration, steps_of["dve"].on(dve))
                for b in range(NB):
                    dve.wait_ge(s_t, 6 + b)
                    v.tensor_copy(ssm[:, b * H:(b + 1) * H, :],
                                  pr_ps[0:DH, b % 2 * 512:b % 2 * 512 + 512].rearrange("p (h n) -> p h n", h=H)
                                  ).then_inc(s_k, 1)


def feed_forward(nc, sem, A, O, S, c, keep):
    with ExitStack() as ctx:
        sb, ps = new_pools(nc, ctx)
        spans = [(0, 768, [(0, 384), (384, 384)]), (768, 768, [(0, 384), (384, 384)]),
                 (1536, 512, [(0, 512), (512, 128)])]
        NSP, MAXT = len(spans), 768
        NCH = 2
        h2 = sb("h2", [P, KD, MAXT])
        mid = sb("mid", [P, KF, MAXT])
        down = sb("down", [P, KD, MAXT])
        w_up = [sb(f"w_gu{j}", [P, 2, KD, P]) for j in range(2)]
        w_dn = [sb(f"w_dn{j}", [P, KF, P]) for j in range(2)]
        g_buf, g_s = sb("g_buf", [P, 2 + MAXT]), sb("g_s", [P, NB, 2 + TS])
        conv, gate_on = sb("conv", [P, MAXT]), sb("gate_on", [P, MAXT])
        taps, tap = sb("taps", [P, KF, 4]), sb("tap", [P, 4])
        tail = sb("tail", [P, KF, 18])
        hist = sb("hist", [P, KF, 16])
        xr = [sb(f"xr{j}", [P, D]) for j in range(2)]
        ffn_gate = sb("ffn_gate_in", [P, 2, D])
        y, prod = sb("y", [P, D]), sb("prod", [P, D])
        g_fin = sb("g_fin", [P, D])
        ss, mean, rstd = sb("ff_ss", [P, 2]), sb("ff_mean", [P, 2]), sb("ff_rstd", [P, 2])
        flat = mid[:].rearrange("p f t -> p (f t)")
        rows_in, rows_out = flat[0:16, 0:FF], flat[0:18, 0:FF]
        g_ps, u_ps = ps("g_ps", [P, 2, 512]), ps("u_ps", [P, 2, 512])
        d_ps, f_ps = ps("d_ps", [P, 2, 512]), ps("f_ps", [P, 2, 512])

        s_par, s_hist, s_h2 = sem("ff_params"), sem("ff_history"), sem("h2_loaded")
        s_w = [sem(f"w_gu_loaded{j}") for j in range(2)]
        s_wd = [sem(f"w_dn_loaded{j}") for j in range(2)]
        s_xr = [sem(f"xr_loaded{j}") for j in range(2)]
        s_ht, s_hk = sem("hist_turned"), sem("hist_kept")
        s_g, s_gk, s_u, s_mid = sem("g_done"), sem("g_kept"), sem("u_done"), sem("mid_done")
        s_conv, s_on = sem("ff_conv_done"), sem("gate_on_done")
        s_d, s_dk, s_f = sem("down_done"), sem("down_kept"), sem("down_turned")
        s_x3, s_ss, s_mean, s_rstd, s_y = sem("x3_done"), sem("ff_squares"), sem("ff_mean"), sem("ff_rstd"), sem("y_done")
        s_fuse = sem("f_ps_used")
        s_dve, s_store, s_tail, s_tk = sem("ff_dve"), sem("y_stored"), sem("tail_turned"), sem("tail_kept")
        s_tout = sem("tail_stored")

        wg = A["f_w_gate"][0].rearrange("(k p) (f c) -> f p k c", p=P, c=P)
        wu = A["f_w_up"][0].rearrange("(k p) (f c) -> f p k c", p=P, c=P)
        wd = A["f_w_down"][0].rearrange("(f p) (d c) -> d p f c", p=P, c=P)
        token_tiles = [(s, k) for s, (t0, n, ch) in enumerate(spans) for k in range(sum(w for _, w in ch) // P)]
        first_tile = [min(i for i, (s, _) in enumerate(token_tiles) if s == sp) for sp in range(NSP)] + [len(token_tiles)]

        block = ctx.enter_context(nc.Block())

        @block.sync
        def _(sp):
            def load_h2(s):
                t0, n, ch = spans[s]
                n = sum(w for _, w in ch)
                sp.dma_start(h2[:, :, 0:n], S["h2t"][:, :, t0:t0 + n]).then_inc(s_h2, 16)

            def load_gu(f, j):
                sp.dma_start(w_up[j][:, 0], wg[f] if isinstance(f, int) else
                             wg[bass.ds(f, 1)].rearrange("o p k c -> (o p) k c")).then_inc(s_w[j], 16)
                sp.dma_start(w_up[j][:, 1], wu[f] if isinstance(f, int) else
                             wu[bass.ds(f, 1)].rearrange("o p k c -> (o p) k c")).then_inc(s_w[j], 16)

            def load_dn(d, j):
                sp.dma_start(w_dn[j][:], wd[d] if isinstance(d, int) else
                             wd[bass.ds(d, 1)].rearrange("o p f c -> (o p) f c")).then_inc(s_wd[j], 16)

            def load_xr(i):
                sp.dma_start(xr[i % 2][:], S["x2"][i * P:(i + 1) * P, :]).then_inc(s_xr[i % 2], 16)

            sp.dma_start(rows_in, A["state_ffn_conv"][0].rearrange("b j n -> (b j) n")).then_inc(s_hist, 16)
            load_h2(0)
            load_gu(0, 0)
            load_gu(1, 1)
            load_xr(0)
            load_xr(1)
            for j in range(3):
                sp.dma_start(taps[:, :, j], A["f_conv_w"][0, j].rearrange("(f p) -> p f", p=P),
                             allow_slow_non_contiguous=True).then_inc(s_par, 16)
            sp.dma_start(taps[:, :, 3], A["f_conv_b"][0].rearrange("(f p) -> p f", p=P),
                         allow_slow_non_contiguous=True).then_inc(s_par, 16)
            sp.dma_start(g_fin[:], A["g_final"].partition_broadcast(P)).then_inc(s_par, 16)
            sp.dma_start(ffn_gate[:], S["ffn_gate"]).then_inc(s_par, 16)
            for s in range(NSP):
                with sp.Fori(1, KF // 2) as q:
                    for j in range(2):
                        sp.wait_ge(s_u, q * 2 + (s * KF + j - 1))
                        load_gu(q * 2 + j, j)
                for j in range(2):
                    if s:
                        sp.wait_ge(s_d, 2 * (s * KD - 1 + j))
                    load_dn(j, j)
                if s + 1 < NSP:
                    for j in range(2):
                        sp.wait_ge(s_u, (s + 1) * KF - 1 + j)
                        load_gu(j, j)
                    load_h2(s + 1)
                with sp.Fori(1, KD // 2) as q:
                    for j in range(2):
                        sp.wait_ge(s_d, q * 4 + 2 * (s * KD + j - 1))
                        load_dn(q * 2 + j, j)
                for i in range(first_tile[s], first_tile[s + 1]):
                    sp.wait_ge(s_y, i + 1)
                    if i < NT:
                        sp.dma_start(O["y_prompt"][0, i * P:(i + 1) * P, :], y[:]).then_inc(s_store, 16)
                    else:
                        sp.dma_start(O["y_sample"].rearrange("b t d -> (b t) d"), y[:]).then_inc(s_store, 16)
                    if i + 2 <= NT:
                        load_xr(i + 2)
            sp.wait_ge(s_tk, 6)
            sp.dma_start(O["s_ffn_conv"][0].rearrange("b j n -> (b j) n"), rows_out[0:16]).then_inc(s_tout, 16)
            sp.dma_start(O["p_ffn_conv"][0, 0], rows_out[16:18]).then_inc(s_tout, 16)
            sp.wait_ge(s_tout, 32)
            sp.wait_ge(s_store, 16 * (NT + 1))

        @block.tensor
        def _(pe):
            t = nc.tensor
            pe.wait_ge(s_hist, 16)
            for f in range(KF):
                last = t.transpose(f_ps[:, 0, f * 16:(f + 1) * 16], rows_in[:, f * P:(f + 1) * P], c["ident"][0:16, 0:16])
            last.then_inc(s_ht, 1)
            for s, (t0, n, chunks) in enumerate(spans):
                pe.wait_ge(s_h2, 16 * (s + 1))

                def step(q, j, first=False):
                    n_th = q * 2 + (s * KF + j)
                    pe.wait_ge(s_w[j], q * 32 + (s * KF // 2 * 32 + 32))
                    if not first:
                        pe.wait_ge(s_gk, n_th)
                    for b, (at, width) in enumerate(chunks):
                        for k in range(KD):
                            last = t.matmul(g_ps[:, b, 0:width], w_up[j][:, 0, k, :], h2[:, k, at:at + width],
                                            start=(k == 0), stop=(k == KD - 1))
                    last.then_inc(s_g, 1)
                    if not first:
                        pe.wait_ge(s_mid, n_th)
                    for b, (at, width) in enumerate(chunks):
                        for k in range(KD):
                            last = t.matmul(u_ps[:, b, 0:width], w_up[j][:, 1, k, :], h2[:, k, at:at + width],
                                            start=(k == 0), stop=(k == KD - 1))
                    last.then_inc(s_u, 1)

                step(0, 0, first=(s == 0))
                step(0, 1)
                with pe.Fori(1, KF // 2) as q:
                    step(q, 0)
                    step(q, 1)
                pe.wait_ge(s_mid, (s + 1) * KF)
                if s:
                    pe.wait_ge(s_ss, first_tile[s])

                def down_step(q, j, first=False):
                    pe.wait_ge(s_wd[j], q * 16 + (s * KD // 2 * 16 + 16))
                    for b, (at, width) in enumerate(chunks):
                        if not first:
                            pe.wait_ge(s_dk, q * 4 + (2 * (s * KD + j) + b - 1))
                        for f in range(KF):
                            last = t.matmul(d_ps[:, b, 0:width], w_dn[j][:, f, :], mid[:, f, at:at + width],
                                            start=(f == 0), stop=(f == KF - 1))
                        last.then_inc(s_d, 1)

                down_step(0, 0, first=(s == 0))
                down_step(0, 1)
                with pe.Fori(1, KD // 2) as q:
                    down_step(q, 0)
                    down_step(q, 1)
                if s == NSP - 1:
                    for f in range(KF):
                        if f % 4 == 0 and f >= 8:
                            pe.wait_ge(s_tk, f // 4 - 1)
                        ins = t.transpose(g_ps[0:18, f // 4 % 2, f % 4 * P:(f % 4 + 1) * P], tail[:, f, :], c["ident"][:])
                        if f % 4 == 3 or f == KF - 1:
                            ins.then_inc(s_tail, 1)
                pe.wait_ge(s_dk, 2 * KD * (s + 1))
                for i in range(first_tile[s], first_tile[s + 1]):
                    k = i - first_tile[s]
                    if i:
                        pe.wait_ge(s_fuse, i)
                    else:
                        pe.wait_ge(s_hk, 1)
                    for d in range(KD):
                        last = t.transpose(f_ps[:, d // 4, d % 4 * P:(d % 4 + 1) * P], down[:, d, k * P:(k + 1) * P],
                                           c["ident"][:])
                    last.then_inc(s_f, 1)

        @block.scalar
        def _(act):
            a = nc.scalar
            for s, (t0, n, chunks) in enumerate(spans):
                sample = s == NSP - 1

                def step(q, j, first=False):
                    n_th = q * 2 + (s * KF + j)
                    act.wait_ge(s_g, n_th + 1)
                    if not first:
                        act.wait_ge(s_conv, n_th)
                    for b, (at, width) in enumerate(chunks):
                        if sample and b == 1:
                            last = a.activation(g_s[:, :, 2:], g_ps[:, b, 0:width].rearrange("p (n t) -> p n t", n=NB),
                                                ACT.Copy)
                        else:
                            last = a.activation(g_buf[:, 2 + at:2 + at + width], g_ps[:, b, 0:width], ACT.Copy)
                        if b == NCH - 1:
                            last.then_inc(s_gk, 1)
                    act.wait_ge(s_conv, n_th + 1)
                    width = sum(w for _, w in chunks)
                    a.activation(gate_on[:, 0:width], conv[:, 0:width], ACT.Silu).then_inc(s_on, 1)

                step(0, 0, first=(s == 0))
                step(0, 1)
                with act.Fori(1, KF // 2) as q:
                    step(q, 0)
                    step(q, 1)

                def down_step(q, j):
                    for b, (at, width) in enumerate(chunks):
                        act.wait_ge(s_d, q * 4 + (2 * (s * KD + j) + b + 1))
                        dst = down[:, q * 2 + j, at:at + width] if isinstance(q, int) else \
                            down[:, bass.ds(q * 2 + j, 1), at:at + width].rearrange("p o t -> p (o t)")
                        a.activation(dst, d_ps[:, b, 0:width], ACT.Copy).then_inc(s_dk, 1)

                if s:
                    act.wait_ge(s_f, first_tile[s])
                down_step(0, 0)
                down_step(0, 1)
                with act.Fori(1, KD // 2) as q:
                    down_step(q, 0)
                    down_step(q, 1)
                for i in range(first_tile[s], first_tile[s + 1]):
                    act.wait_ge(s_x3, i + 1)
                    if i:
                        act.wait_ge(s_ss, i)
                    a.activation(d_ps[:].rearrange("p a n -> p (a n)"), xr[i % 2][:], ACT.Square,
                                 accum_out=ss[:, i % 2:i % 2 + 1]).then_inc(s_ss, 1)

        @block.gpsimd
        def _(pool):
            for i in range(NT + 1):
                j = i % 2
                pool.wait_ge(s_ss, i + 1)
                nc.gpsimd.tensor_scalar(mean[:, j:j + 1], ss[:, j:j + 1], 1.0 / D, EPS, ALU.mult, ALU.add
                                        ).then_inc(s_mean, 1)
                pool.wait_ge(s_mean, i + 1)
                nc.gpsimd.tensor_tensor(rstd[:, j:j + 1], mean[:, j:j + 1], c["minus_half"][:, 0:1], ALU.pow
                                        ).then_inc(s_rstd, 1)

        @block.vector
        def _(dve):
            v = nc.vector
            step_ = Steps(dve, s_dve)
            dve.wait_ge(s_ht, 1)
            v.tensor_copy(hist[:], f_ps[:, 0, 0:KF * 16].rearrange("p (f n) -> p f n", f=KF)).then_inc(s_hk, 1)
            step_(v.memset(g_buf[:, 0:2], 0.0))
            dve.wait_ge(s_par, 16 * 6)
            for s, (t0, n, chunks) in enumerate(spans):
                sample = s == NSP - 1
                width = sum(w for _, w in chunks)
                PER = 8 if sample else (6 if s else 5)
                base0 = step_.count

                def at_f(ap, f):
                    return ap[:, f] if isinstance(f, int) else ap[:, bass.ds(f, 1)].rearrange("p o n -> p (o n)")

                def step(q, j):
                    f = q * 2 + j
                    n_th = q * 2 + (s * KF + j)
                    step_.count = 0
                    step_.base = q * (2 * PER) + (base0 + j * PER)
                    step_(v.tensor_copy(tap[:], at_f(taps, f)))
                    if s:
                        step_(v.tensor_copy(g_buf[:, 0:2], at_f(tail, f)[:, 16:18]))
                    if sample:
                        step_(v.tensor_copy(g_s[:, :, 0:2], at_f(hist, f).rearrange("p (b j) -> p b j", b=NB)))
                    step_.settle()
                    dve.wait_ge(s_gk, n_th + 1)
                    gs = g_s[:]
                    cs = conv[:, n:n + P].rearrange("p (b t) -> p b t", b=NB) if sample else None
                    step_(v.tensor_scalar(conv[:, 0:n], g_buf[:, 0:n], tap[:, 0:1], tap[:, 3:4], ALU.mult, ALU.add))
                    if sample:
                        step_(v.tensor_scalar(cs, gs[:, :, 0:TS], tap[:, 0:1], tap[:, 3:4], ALU.mult, ALU.add))
                    step_.settle()
                    step_(v.scalar_tensor_tensor(conv[:, 0:n], g_buf[:, 1:n + 1], tap[:, 1:2], conv[:, 0:n],
                                                 ALU.mult, ALU.add))
                    if sample:
                        v.scalar_tensor_tensor(cs, gs[:, :, 1:TS + 1], tap[:, 1:2], cs, ALU.mult, ALU.add)
                        v.tensor_copy(at_f(tail, f)[:, 0:16].rearrange("p (b j) -> p b j", b=NB), gs[:, :, TS:TS + 2])
                    step_(v.tensor_copy(at_f(tail, f)[:, 16:18], g_buf[:, n:n + 2]))
                    step_.settle()
                    if sample:
                        v.scalar_tensor_tensor(cs, gs[:, :, 2:TS + 2], tap[:, 2:3], cs, ALU.mult, ALU.add)
                    v.scalar_tensor_tensor(conv[:, 0:n], g_buf[:, 2:n + 2], tap[:, 2:3], conv[:, 0:n],
                                           ALU.mult, ALU.add).then_inc(s_conv, 1)
                    dve.wait_ge(s_on, n_th + 1)
                    dve.wait_ge(s_u, n_th + 1)
                    for b, (at, w) in enumerate(chunks):
                        dst = at_f(mid, f)[:, at:at + w]
                        last = v.tensor_tensor(dst, gate_on[:, at:at + w], u_ps[:, b, 0:w], ALU.mult)
                        if b == NCH - 1:
                            last.then_inc(s_mid, 1)
                        else:
                            step_(last)
                    assert step_.count == PER

                step(0, 0)
                step(0, 1)
                with dve.Fori(1, KF // 2) as q:
                    step(q, 0)
                    step(q, 1)
                step_.base, step_.count = 0, base0 + KF * PER

                if sample:
                    for r in range(6):
                        dve.wait_ge(s_tail, r + 1)
                        w = min(4, KF - 4 * r) * P
                        v.tensor_copy(rows_out[:, r * 512:r * 512 + w], g_ps[0:18, r % 2, 0:w]).then_inc(s_tk, 1)

                def residual(i):
                    dve.wait_ge(s_f, i + 1)
                    dve.wait_ge(s_xr[i % 2], 16 * (i // 2 + 1))
                    who = 1 if i == NT else 0
                    if i:
                        dve.wait_ge(s_x3, i)
                    v.tensor_tensor(prod[:], f_ps[:].rearrange("p a n -> p (a n)"), ffn_gate[:, who, :],
                                    ALU.mult).then_inc(s_fuse, 1)
                    dve.wait_ge(s_fuse, i + 1)
                    v.tensor_tensor(xr[i % 2][:], xr[i % 2][:], prod[:], ALU.add).then_inc(s_x3, 1)

                def finish(i):
                    dve.wait_ge(s_rstd, i + 1)
                    if i:
                        dve.wait_ge(s_store, 16 * i)
                    v.scalar_tensor_tensor(y[:], xr[i % 2][:], rstd[:, i % 2:i % 2 + 1], g_fin[:], ALU.mult, ALU.mult
                                           ).then_inc(s_y, 1)

                tiles = range(first_tile[s], first_tile[s + 1])
                residual(tiles[0])
                for i in tiles:
                    if i + 1 in tiles:
                        residual(i + 1)
                    finish(i)


def bass_hybrid_chunk_streaming_encoder_step_kernel(nc, A, O):
    with ExitStack() as ctx:
        sb, _ = new_pools(nc, ctx)
        sem = Semaphores(nc)
        S = {name: nc.dram_tensor("scratch_" + name, shape, F32, kind="Internal").ap() for name, shape in {
            "proj": (SEQ + P, PW), "xbc": (P, KX, SEQ + 3), "xbc_s": (P, KX, P), "h2t": (P, KD, SEQ + P),
            "x2": (SEQ + P, D), "ffn_gate": (P, 2, D), "rel_row": (H, 768), "rel": (H, P, 768)}.items()}
        c, const_program = make_constants(nc, sb, sem)
        sem.constants_cut = sem["const_cut"]
        keep = {name: sb(name, [P, KD, 1 + NB]) for name in ("mix_scale", "mix_shift", "ffn_scale", "ffn_shift")}
        with ExitStack() as first:
            sb1, _ = new_pools(nc, first)
            keep["mix_gate"] = sb1("mix_gate", [P, 2, D])
            ya_sample = sb1("ya_sample", [P, GW])
            rel_bias_rows(nc, sem, A, S)
            with ExitStack() as second:
                sb2, _ = new_pools(nc, second)
                w_in_sb = sb2("w_in_sb", [P, KD * WIN + 520])
                modulation(nc, sem, A, S, c, const_program, keep, w_in_sb)
                projection(nc, sem, A, S, c, keep, w_in_sb)
            sem.give_back()
            sample_attention(nc, sem, A, S, c, ya_sample)
            mixers(nc, sem, A, O, S, c, keep, ya_sample)
        sem.give_back()
        feed_forward(nc, sem, A, O, S, c, keep)


class Semaphores:

    def __init__(self, nc):
        self.nc, self.made, self.group = nc, {}, []

    def give_back(self):
        self.nc.clear_and_free_semaphores(self.group)
        self.nc.all_engine_barrier()
        self.group = []

    def __call__(self, name):
        assert name not in self.made, name
        self.made[name] = self.nc.alloc_semaphore(name=name)
        self.group.append(self.made[name])
        return self.made[name]

    def __getitem__(self, name):
        return self.made[name]


_INS = ["x_prompt", "x_sample", "c_prompt", "c_sample", "cache_a_k", "cache_a_v", "state_b_c", "state_b_n", "state_b_m",
        "state_c_ssm", "state_c_conv", "state_ffn_conv", "w_ada", "b_ada", "g_norm_mix", "g_norm_ffn", "w_in", "w_out",
        "a_rel_bias", "b_i_bias", "b_f_bias", "b_norm_g", "c_conv_w", "c_conv_b", "c_dt_bias", "c_a_log", "c_d_skip",
        "c_norm_g", "d_norm_g", "d_w_s", "d_b_s", "f_w_gate", "f_w_up", "f_conv_w", "f_conv_b", "f_w_down", "g_final"]
_OUTS = {
    "y_prompt": (1, SEQ, D), "y_sample": (NB, TS, D), "p_a_k": (1, 1, HIST, H, DH), "p_a_v": (1, 1, HIST, H, DH),
    "p_b_c": (1, 1, H, DH, DH), "p_b_n": (1, 1, H, DH), "p_b_m": (1, 1, H), "p_c_ssm": (1, 1, H, DH, NSTATE),
    "p_c_conv": (1, 1, 3, XW), "p_ffn_conv": (1, 1, 2, FF), "s_a_k": (1, NB, TS, H, DH), "s_a_v": (1, NB, TS, H, DH),
    "s_b_c": (1, NB, H, DH, DH), "s_b_n": (1, NB, H, DH), "s_b_m": (1, NB, H), "s_c_ssm": (1, NB, H, DH, NSTATE),
    "s_c_conv": (1, NB, 3, XW), "s_ffn_conv": (1, NB, 2, FF), "s_d_v": (1, NB, TS, GW)}


def kernel(**inputs):
    import numpy as _np
    import concourse.bacc as _bacc
    from concourse.bass_utils import run_bass_kernel_spmd as _run

    nc = _bacc.Bacc("TRN2", target_bir_lowering=False, num_devices=1)
    arrays, A = {}, {}
    for name in _INS:
        a = _np.ascontiguousarray(inputs[name])
        if name == "a_rel_bias":
            name = "a_rel_bias_reversed"
            a = _np.ascontiguousarray(a[:, :, ::-1])
        arrays[f"in_{name}"] = a
        A[name] = nc.dram_tensor(f"in_{name}", a.shape, F32, kind="ExternalInput").ap()
    O = {name: nc.dram_tensor(f"out_{name}", shape, F32, kind="ExternalOutput").ap() for name, shape in _OUTS.items()}
    bass_hybrid_chunk_streaming_encoder_step_kernel(nc, A, O)
    r = _run(nc, [arrays], core_ids=[0])
    return tuple(r.results[0][f"out_{name}"] for name in _OUTS)
```

```python
from contextlib import ExitStack

import concourse.bass as bass
from concourse import mybir

F32 = mybir.dt.float32
F32R = mybir.dt.float32r
ALU = mybir.AluOpType
ACT = mybir.ActivationFunctionType
AX = mybir.AxisListType.X

P = 128
D = 1024
KD = D // P
SEQ = 2048
NT = SEQ // P
NB, TS = 8, 16
GW = 256
H, DH = 4, 64
NSTATE = 128
XW = 768
KX = XW // P
WIN = 3340
X0 = 2056
PW = WIN - XW
FF = 2816
KF = FF // P
EPS = 1e-6
NEG = -1e30
HIST = 512
BAND = HIST + P
NPAST = HIST // P

QA, KA, VA, QB, KB, VB, OB, IB, FB, ZC, DT, UD, VD = (
    0, 256, 512, 768, 1024, 1280, 1536, 1792, 1796, 1800, 2056, 2060, 2316)


A0 = IB - 2 * GW
AW = PW - A0


def spread(ap, axis, n):
    shape = list(ap.shape)
    shape.insert(axis, n)
    return ap.unsqueeze(axis).to_broadcast(shape)


class Steps:

    def __init__(self, engine, sem):
        self.engine, self.sem, self.base, self.count, self.per_tile = engine, sem, 0, 0, None
        self.last = None

    def next(self):
        if self.count:
            self.per_tile = self.count
        self.base, self.count = self.base + self.count, 0

    def enter(self, q, first, per):
        self.next()
        self.start = self.base
        self.base = q * per + (self.start - first * per)

    def leave(self, trips, per):
        assert self.count == per, (self.count, per)
        self.base, self.count = self.start + trips * per, 0

    def __call__(self, instruction):
        self.count += 1
        instruction.then_inc(self.sem, 1)
        self.last = (self.sem, self.base + self.count)

    def on(self, engine):
        self.engine = engine
        return self

    def settle(self):
        self.engine.wait_ge(*self.last)


class Tile:

    def __init__(self, pair, parity):
        self.pair, self.parity = pair, parity
        self.i = pair * 2 + parity
        self.first = isinstance(pair, int) and self.i == 0
        self.done = self.i + 1

    def nth(self, k, per):
        return self.i * per + (k + 1)


def new_pools(nc, ctx):
    def sb(name, shape, dt=F32):
        return ctx.enter_context(nc.sbuf_tensor(name, list(shape), dt))

    def ps(name, shape, dt=F32):
        return ctx.enter_context(nc.psum_tensor(name, list(shape), dt))

    return sb, ps


def make_constants(nc, sb, sem):
    c = {
        "ident": sb("ident", [P, P]),
        "ones": sb("ones", [P, P]),
        "tri": sb("tri", [P, P]),
        "tri_s": sb("tri_s", [P, P]),
        "pick": sb("pick", [H, H, P]),
        "stream": sb("stream", [P, NB]),
        "to_prompt": sb("to_prompt", [9, P]),
        "to_sample": sb("to_sample", [9, P]),
        "minus_half": sb("minus_half", [P, H]),
        "zeros": sb("zeros", [P, KX * 3]),
        "per_width": sb("per_width", [P, H + 2]),
        "eps": sb("eps", [P, H]),
    }
    made, cut = sem("const_made"), sem("const_cut")

    def program(pool):
        g = nc.gpsimd
        for name in ("ident", "pick", "to_prompt", "to_sample", "zeros"):
            g.memset(c[name][:], 0.0).then_inc(made, 1)
        for name in ("ones", "tri", "tri_s", "stream"):
            g.memset(c[name][:], 1.0).then_inc(made, 1)
        g.memset(c["minus_half"][:], -0.5).then_inc(made, 1)
        g.memset(c["eps"][:], EPS).then_inc(made, 1)
        g.memset(c["per_width"][:, 0:H], 1.0 / DH).then_inc(made, 1)
        g.memset(c["per_width"][:, H:H + 1], 1.0 / GW).then_inc(made, 1)
        g.memset(c["per_width"][:, H + 1:H + 2], 1.0 / D).then_inc(made, 1)
        pool.wait_ge(made, 14)
        n = 0

        def cut_out(ap, pattern, op, fill, base, rows):
            nonlocal n
            g.affine_select(out=ap, in_=ap, pattern=pattern, compare_op=op, fill=fill, base=base,
                            channel_multiplier=rows).then_inc(cut, 1)
            n += 1
            return n

        cut_out(c["ident"][:], [[-1, P]], ALU.not_equal, 1.0, 0, 1)
        cut_out(c["pick"][:], [[-1, H], [0, P]], ALU.not_equal, 1.0, 0, 1)
        cut_out(c["to_prompt"][:], [[0, P]], ALU.not_equal, 1.0, 0, 1)
        ts = c["to_sample"][:].rearrange("k (b t) -> k b t", b=NB)
        cut_out(ts, [[-1, NB], [0, TS]], ALU.not_equal, 1.0, -1, 1)
        cut_out(c["tri"][:], [[1, P]], ALU.is_ge, 0.0, 0, -1)
        cut_out(c["tri_s"][:], [[1, P]], ALU.is_ge, 0.0, 0, -1)
        cut_out(c["stream"][:], [[-TS, NB]], ALU.is_ge, 0.0, 0, 1)
        pool.wait_ge(cut, n)
        t3 = c["tri_s"][:].rearrange("p (b t) -> p b t", b=NB)
        cut_out(t3, [[-TS, NB], [0, TS]], ALU.is_ge, 0.0, 0, 1)
        cut_out(c["stream"][:], [[TS, NB]], ALU.is_ge, 0.0, TS - 1, -1)
        pool.wait_ge(cut, n)

    return c, program


def modulation(nc, sem, A, S, c, const_program, keep, w_in_sb):
    with ExitStack() as ctx:
        sb, ps = new_pools(nc, ctx)
        NS = 1 + NB
        NG = 6 * D // 512
        cond, cond_e, cond_r = sb("cond", [NS, D]), sb("cond_e", [NS, D]), sb("cond_r", [NS, D])
        cond_t = sb("cond_t", [P, KD, NS])
        w = [sb(f"w_ada{j}", [P, KD, 512]) for j in range(2)]
        bias, mod = sb("b_ada", [NS, 2, 512]), sb("mod", [NS, 6 * D])
        g_col = sb("g_col", [P, 2, KD])
        keep["ffn_gate"] = sb("ffn_gate", [P, 2, D])
        cond_ps = ps("cond_ps", [P, 512])
        mod_ps = ps("mod_ps", [P, 2, 512])
        col_ps = ps("col_ps", [P, 512])
        gate_ps = ps("gate_ps", [P, 4, 512])
        s_in, s_g = sem("mod_inputs"), sem("mod_gains")
        s_w = [sem(f"w_ada_loaded{j}") for j in range(2)]
        s_e, s_c, s_ct, s_ctc = sem("cond_exp"), sem("cond_silu"), sem("cond_turned"), sem("cond_kept")
        s_m, s_mk, s_col, s_gate, s_colk, s_gatek = (
            sem("mod_group"), sem("mod_kept"), sem("mod_cols"), sem("gate_rows"), sem("cols_kept"), sem("gates_kept"))
        s_v = sem("mod_dve")
        s_win, s_gout = sem("w_in_loaded"), sem("ffn_gate_stored")
        w_view = A["w_ada"][0].rearrange("(k p) n -> p k n", p=P)

        block = ctx.enter_context(nc.Block())

        @block.gpsimd
        def _(pool):
            const_program(pool)

        @block.sync
        def _(sp):
            sp.dma_start(cond[0:1, :], A["c_prompt"]).then_inc(s_in, 16)
            sp.dma_start(cond[1:NS, :], A["c_sample"]).then_inc(s_in, 16)
            for j in range(NG):
                if j >= 2:
                    sp.wait_ge(s_m, j - 1)
                    sp.wait_ge(s_mk, j - 1)
                sp.dma_start(bias[:, j % 2, :], A["b_ada"][0, j * 512:(j + 1) * 512].partition_broadcast(NS)
                             ).then_inc(s_w[j % 2], 16)
                sp.dma_start(w[j % 2][:], w_view[:, :, j * 512:(j + 1) * 512]).then_inc(s_w[j % 2], 16)
            w_in = A["w_in"][0].rearrange("(k p) n -> k p n", p=P)
            for k in range(KD):
                sp.dma_start(w_in_sb[:, k * WIN:(k + 1) * WIN], w_in[k]).then_inc(s_win, 16)
            sp.wait_ge(s_gatek, 8)
            sp.dma_start(S["ffn_gate"], keep["ffn_gate"][:]).then_inc(s_gout, 16)
            sp.wait_ge(s_gout, 16)

        @block.scalar
        def _(act):
            act.dma_start(g_col[:, 0, :], A["g_norm_mix"][0].rearrange("(k p) -> p k", p=P),
                          allow_slow_non_contiguous=True).then_inc(s_g, 16)
            act.dma_start(g_col[:, 1, :], A["g_norm_ffn"][0].rearrange("(k p) -> p k", p=P),
                          allow_slow_non_contiguous=True).then_inc(s_g, 16)
            act.wait_ge(s_in, 32)
            nc.scalar.activation(cond_e[:], cond[:], ACT.Silu).then_inc(s_e, 1)

        @block.vector
        def _(dve):
            dve.wait_ge(s_ct, 1)
            nc.vector.tensor_copy(cond_t[:], cond_ps[:, 0:KD * NS].rearrange("p (k s) -> p k s", k=KD)
                                  ).then_inc(s_ctc, 1)
            for j in range(NG):
                dve.wait_ge(s_m, j + 1)
                nc.vector.tensor_tensor(mod[:, j * 512:(j + 1) * 512], mod_ps[0:NS, j % 2, :],
                                        bias[:, j % 2, :], ALU.add).then_inc(s_mk, 1)
            dve.wait_ge(s_col, 1)
            dve.wait_ge(s_g, 32)
            cols = col_ps[:, 0:4 * KD * NS].rearrange("p (a k s) -> p a k s", a=4, k=KD)
            for a, norm in enumerate(("mix", "ffn")):
                nc.vector.tensor_copy(keep[norm + "_shift"][:], cols[:, 2 * a]).then_inc(s_colk, 1)
                nc.vector.tensor_scalar(keep[norm + "_scale"][:], cols[:, 2 * a + 1], 1.0, None, ALU.add
                                        ).then_inc(s_v, 1)
                dve.wait_ge(s_v, 2 * a + 1)
                nc.vector.tensor_tensor(keep[norm + "_scale"][:], keep[norm + "_scale"][:],
                                        spread(g_col[:, a, :], 2, NS), ALU.mult).then_inc(s_v, 1)
            n = 0
            for gate in ("mix_gate", "ffn_gate"):
                for who in range(2):
                    for half in range(2):
                        n += 1
                        dve.wait_ge(s_gate, n)
                        nc.vector.tensor_copy(keep[gate][:, who, half * 512:(half + 1) * 512],
                                              gate_ps[:, (n - 1) % 4, :]).then_inc(s_gatek, 1)
            dve.wait_ge(s_gatek, n)
            dve.wait_ge(s_colk, 2)
            dve.wait_ge(s_v, 4)

        @block.tensor
        def _(pe):
            t = nc.tensor
            pe.wait_ge(s_e, 1)
            pe.wait_ge(sem.constants_cut, 9)
            for k in range(KD):
                last = t.transpose(cond_ps[:, k * NS:(k + 1) * NS], cond_e[:, k * P:(k + 1) * P], c["ident"][0:NS, 0:NS])
            last.then_inc(s_ct, 1)
            pe.wait_ge(s_ctc, 1)
            for j in range(NG):
                pe.wait_ge(s_w[j % 2], 32 * (j // 2 + 1))
                if j >= 2:
                    pe.wait_ge(s_mk, j - 1)
                for k in range(KD):
                    last = t.matmul(mod_ps[0:NS, j % 2, :], cond_t[:, k, :], w[j % 2][:, k, :],
                                    start=(k == 0), stop=(k == KD - 1))
                last.then_inc(s_m, 1)
            pe.wait_ge(s_mk, NG)
            at = 0
            for piece in (0, 1, 3, 4):
                for k in range(KD):
                    last = t.transpose(col_ps[:, at:at + NS], mod[:, piece * D + k * P:piece * D + (k + 1) * P],
                                       c["ident"][0:NS, 0:NS])
                    at += NS
            last.then_inc(s_col, 1)
            n = 0
            for piece in (2, 5):
                for who in ("to_prompt", "to_sample"):
                    for half in range(2):
                        if n >= 4:
                            pe.wait_ge(s_gatek, n - 3)
                        at = piece * D + half * 512
                        t.matmul(gate_ps[:, n % 4, :], c[who][:], mod[:, at:at + 512], start=True, stop=True
                                 ).then_inc(s_gate, 1)
                        n += 1


def projection(nc, sem, A, S, c, keep, w_in_sb):
    with ExitStack() as ctx:
        sb, ps = new_pools(nc, ctx)
        x = [sb(f"x{j}", [P, D]) for j in range(2)]
        xn = [sb(f"xn{j}", [P, D]) for j in range(2)]
        squares = sb("squares", [P, D])
        ht = [sb(f"ht{j}", [P, KD, P]) for j in range(2)]
        out = [sb(f"proj_out{j}", [P, PW]) for j in range(2)]
        xout = [sb(f"xbc_out{j}", [P, KX, P]) for j in range(2)]
        ss, mean, rstd = sb("ss", [P, 2]), sb("mean", [P, 2]), sb("rstd", [P, 2])
        turned = ps("turned", [P, KD, P])
        unit = ps("unit", [P, 4, 512])
        s_x = [sem(f"x_loaded{j}") for j in range(2)]
        s_ss, s_mean, s_rstd, s_xn = sem("p1_squares"), sem("p1_mean"), sem("p1_rstd"), sem("p1_normed")
        s_t, s_ht, s_u, s_uk = sem("p1_turned"), sem("p1_ht"), sem("p1_unit"), sem("p1_unit_kept")
        s_o = [sem(f"p1_stored{j}") for j in range(2)]
        s_win, s_z = sem["w_in_loaded"], sem("p1_zero_columns")
        s_tmp = sem("p1_mod_products")

        groups = [(0, 1, 512, 0, 0), (512, 1, 512, 0, 512), (1024, 1, 384, 0, 1024), (1408, 1, 392, 0, 1408),
                  (1800, 2, 256, 1024, 1800), (3080, 1, 260, 0, 2312)]
        NU = len(groups) + 2

        def w_group(k, g):
            start, blocks, width, stride, _ = groups[g]
            at = k * WIN + start
            if blocks == 1:
                return w_in_sb[:, at:at + width]
            return w_in_sb[:, at:at + blocks * stride].rearrange("p (a n) -> p a n", a=blocks)[:, :, 0:width]

        block = ctx.enter_context(nc.Block())

        @block.sync
        def _(sp):
            xp = A["x_prompt"][0]
            xsamp = A["x_sample"].rearrange("b t d -> (b t) d")
            sp.dma_start(S["xbc"][:, :, 0:3], c["zeros"][:].rearrange("p (k j) -> p k j", k=KX)).then_inc(s_z, 16)
            sp.dma_start(x[0][:], xp[0:P, :]).then_inc(s_x[0], 16)
            sp.dma_start(x[1][:], xp[P:2 * P, :]).then_inc(s_x[1], 16)

            def store(t, sample=False):
                j = t.parity
                sp.wait_ge(s_uk, t.nth(NU - 1, NU))
                if sample:
                    sp.dma_start(S["proj"][SEQ:SEQ + P, :], out[j][:]).then_inc(s_o[j], 16)
                    sp.dma_start(S["xbc_s"][:, :, :], xout[j][:]).then_inc(s_o[j], 16)
                else:
                    sp.dma_start(S["proj"][bass.ds(t.i * P, P), :], out[j][:]).then_inc(s_o[j], 16)
                    sp.dma_start(S["xbc"][:, :, bass.ds(t.i * P + 3, P)], xout[j][:]).then_inc(s_o[j], 16)

            def both(pair, last=False):
                for j in range(2):
                    t = Tile(pair, j)
                    if last and j == 1:
                        store(t)
                        continue
                    sp.wait_ge(s_xn, t.nth(0, 1))
                    if last:
                        sp.dma_start(x[0][:], xsamp).then_inc(s_x[0], 16)
                    else:
                        sp.dma_start(x[j][:], xp[bass.ds(t.i * P + 2 * P, P), :]).then_inc(s_x[j], 16)
                    store(t)

            both(0)
            with sp.Fori(1, NT // 2 - 1) as pair:
                both(pair)
            both(NT // 2 - 1, last=True)
            store(Tile(NT // 2, 0), sample=True)
            sp.wait_ge(s_z, 16)
            sp.wait_ge(s_o[0], 32 * (NT // 2 + 1))
            sp.wait_ge(s_o[1], 32 * (NT // 2))

        @block.scalar
        def _(act):
            def squares_of(t):
                j = t.parity
                act.wait_ge(s_x[j], t.pair * 16 + 16)
                if not t.first:
                    act.wait_ge(s_ss, t.i * 1)
                nc.scalar.activation(squares[:], x[j][:], ACT.Square, accum_out=ss[:, j:j + 1]).then_inc(s_ss, 1)

            def keep_units(t, first_pair):
                j = t.parity
                if not first_pair:
                    act.wait_ge(s_o[j], t.pair * 32)
                for u in range(NU):
                    act.wait_ge(s_u, t.nth(u, NU))
                    if u < len(groups):
                        width, to = groups[u][1] * groups[u][2], groups[u][4]
                        nc.scalar.activation(out[j][:, to:to + width], unit[:, u % 4, 0:width], ACT.Copy
                                             ).then_inc(s_uk, 1)
                    else:
                        v = u - len(groups)
                        nc.scalar.activation(xout[j][:, 3 * v:3 * v + 3, :],
                                             unit[:, u % 4, 0:3 * P].rearrange("p (k t) -> p k t", k=3), ACT.Copy
                                             ).then_inc(s_uk, 1)

            def tiles(pair, first_pair=False, last=False):
                squares_of(Tile(pair + 1, 0))
                keep_units(Tile(pair, 0), first_pair)
                if not last:
                    squares_of(Tile(pair + 1, 1))
                keep_units(Tile(pair, 1), first_pair)

            squares_of(Tile(0, 0))
            squares_of(Tile(0, 1))
            tiles(0, first_pair=True)
            with act.Fori(1, NT // 2 - 1) as pair:
                tiles(pair)
            tiles(NT // 2 - 1, last=True)
            keep_units(Tile(NT // 2, 0), False)

        @block.gpsimd
        def _(pool):
            def rstd_of(t):
                j = t.parity
                pool.wait_ge(s_ss, t.done)
                nc.gpsimd.tensor_tensor(mean[:, j:j + 1], ss[:, j:j + 1], c["per_width"][:, H + 1:H + 2], ALU.mult
                                        ).then_inc(s_mean, 1)
                pool.wait_ge(s_mean, t.nth(0, 2))
                nc.gpsimd.tensor_tensor(mean[:, j:j + 1], mean[:, j:j + 1], c["eps"][:, 0:1], ALU.add
                                        ).then_inc(s_mean, 1)
                pool.wait_ge(s_mean, t.nth(1, 2))
                nc.gpsimd.tensor_tensor(rstd[:, j:j + 1], mean[:, j:j + 1], c["minus_half"][:, 0:1], ALU.pow
                                        ).then_inc(s_rstd, 1)

            rstd_of(Tile(0, 0))
            rstd_of(Tile(0, 1))
            with pool.Fori(1, NT // 2) as pair:
                rstd_of(Tile(pair, 0))
                rstd_of(Tile(pair, 1))
            rstd_of(Tile(NT // 2, 0))

        @block.vector
        def _(dve):
            def normalise(t):
                j = t.parity
                dve.wait_ge(s_rstd, t.done)
                nc.vector.tensor_scalar(xn[j][:], x[j][:], rstd[:, j:j + 1], None, ALU.mult).then_inc(s_xn, 1)

            def keep_ht(t, sample=False, wait_used=True):
                j = t.parity
                dve.wait_ge(s_t, t.done)
                if wait_used:
                    dve.wait_ge(s_u, (t.i - 1) * NU)
                for k in range(KD):
                    if not sample:
                        ins = nc.vector.tensor_scalar(ht[j][:, k, :], turned[:, k, :], keep["mix_scale"][:, k, 0:1],
                                                      keep["mix_shift"][:, k, 0:1], ALU.mult, ALU.add)
                        if k == KD - 1:
                            ins.then_inc(s_ht, 1)
                    else:
                        wide = [P, NB, TS]
                        v = ht[j][:, k, :].rearrange("p (b t) -> p b t", b=NB)
                        nc.vector.tensor_tensor(v, turned[:, k, :].rearrange("p (b t) -> p b t", b=NB),
                                                keep["mix_scale"][:, k, 1:].unsqueeze(2).to_broadcast(wide),
                                                ALU.mult).then_inc(s_tmp, 1)
                        dve.wait_ge(s_tmp, k + 1)
                        ins = nc.vector.tensor_tensor(v, v, keep["mix_shift"][:, k, 1:].unsqueeze(2).to_broadcast(wide),
                                                      ALU.add)
                        if k == KD - 1:
                            ins.then_inc(s_ht, 1)

            def tile(t, first_use, sample=False):
                normalise(t)
                keep_ht(t, sample, not first_use)

            tile(Tile(0, 0), True)
            tile(Tile(0, 1), True)
            with dve.Fori(1, NT // 2) as pair:
                tile(Tile(pair, 0), False)
                tile(Tile(pair, 1), False)
            tile(Tile(NT // 2, 0), False, sample=True)

        @block.tensor
        def _(pe):
            def turn(t):
                j = t.parity
                pe.wait_ge(s_xn, t.done)
                if not t.first:
                    pe.wait_ge(s_ht, t.i * 1)
                for k in range(KD):
                    last = nc.tensor.transpose(turned[:, k, :], xn[j][:, k * P:(k + 1) * P], c["ident"][:])
                last.then_inc(s_t, 1)

            def project(t):
                j = t.parity
                pe.wait_ge(s_ht, t.done)
                for u in range(NU):
                    if not (t.first and u < 4):
                        pe.wait_ge(s_uk, t.i * NU + (u - 3))
                    if u < len(groups):
                        width, blocks = groups[u][2], groups[u][1]
                        dst = unit[:, u % 4, 0:width * blocks]
                        if blocks > 1:
                            dst = dst.rearrange("p (a n) -> p a n", a=blocks)
                        for k in range(KD):
                            last = nc.tensor.matmul(dst, ht[j][:, k, :], w_group(k, u), start=(k == 0),
                                                    stop=(k == KD - 1))
                    else:
                        for v in range(3):
                            col = X0 + (3 * (u - len(groups)) + v) * P
                            for k in range(KD):
                                last = nc.tensor.matmul(unit[:, u % 4, v * P:(v + 1) * P],
                                                        w_in_sb[:, k * WIN + col:k * WIN + col + P], ht[j][:, k, :],
                                                        start=(k == 0), stop=(k == KD - 1))
                    last.then_inc(s_u, 1)

            turn(Tile(0, 0))
            pe.wait_ge(s_win, 16 * KD)

            def tiles(pair):
                turn(Tile(pair, 1))
                project(Tile(pair, 0))
                turn(Tile(pair + 1, 0))
                project(Tile(pair, 1))

            tiles(0)
            with pe.Fori(1, NT // 2) as pair:
                tiles(pair)
            project(Tile(NT // 2, 0))


def rel_bias_rows(nc, sem, A, S):
    with ExitStack() as ctx:
        sb, _ = new_pools(nc, ctx)
        rev, ext = sb("rel_rev", [H, 257]), sb("rel_ext", [H, 768])
        s_in, s_e, s_row, s_rel = sem("rel_in"), sem("rel_extended"), sem("rel_row_stored"), sem("rel_stored")
        block = ctx.enter_context(nc.Block())

        @block.sync
        def _(sp):
            sp.dma_start(rev[:], A["a_rel_bias_reversed"][0]).then_inc(s_in, 16)
            sp.wait_ge(s_e, 2)
            sp.dma_start(S["rel_row"], ext[:]).then_inc(s_row, 16)
            sp.wait_ge(s_row, 16)
            for h in range(H):
                sp.dma_start(S["rel"][h], S["rel_row"][h].partition_broadcast(P)).then_inc(s_rel, 16)
            sp.wait_ge(s_rel, 16 * H)

        @block.vector
        def _(dve):
            dve.wait_ge(s_in, 16)
            nc.vector.tensor_copy(ext[:, 0:512], rev[:, 0:1].to_broadcast([H, 512])).then_inc(s_e, 1)
            dve.wait_ge(s_e, 1)
            nc.vector.tensor_copy(ext[:, 511:768], rev[:, 0:257]).then_inc(s_e, 1)


def rel_tile(S, rows, cols):
    flat = S["rel"].rearrange("h q u -> h (q u)")[:, 127:127 + P * 767]
    return flat.rearrange("h (q j) -> q h j", j=767)[rows, :, cols]


def sample_attention(nc, sem, A, S, c, ya_keep):
    with ExitStack() as ctx:
        sb, ps = new_pools(nc, ctx)
        pt = sb("sa_proj", [P, 768])
        k_in, v_in = sb("k_in", [P, NB, NPAST, GW]), sb("v_in", [P, NB, NPAST, GW])
        k_t = sb("k_t", [P, 2, NB, HIST])
        k_new = sb("k_new", [P, 2, P])
        band = sb("band_s", [P, H, BAND])
        q_z = sb("q_z", [P, H, P])
        q_m = [sb(f"q_m{j}", [P, NB, P]) for j in range(2)]
        stream_row = sb("stream_row", [P, NB, P])
        score, prob = sb("score_s", [P, BAND]), sb("prob_s", [P, BAND])
        prob_t = sb("prob_t_s", [P, BAND])
        wide, own = sb("wide_s", [P, NB, DH]), sb("own_s", [P, DH])
        nmax, total, inv = sb("nmax_s", [P, H]), sb("total_s", [P, H]), sb("inv_s", [P, H])
        turn_ps = ps("sa_turn", [P, 2, 512])
        s_ps = ps("sa_score", [P, 1024])
        p_ps = ps("sa_prob_t", [P, 1024])
        o_ps, n_ps = ps("sa_out", [P, 512]), ps("sa_new", [P, 512])
        s_in, s_v, s_band = sem("sa_proj_loaded"), sem("sa_v_loaded"), sem("sa_band_loaded")
        s_k = [sem(f"sa_k_loaded{b}") for b in range(NB)]
        s_neg, s_row, s_z = sem("sa_band_masked"), sem("sa_stream_row"), sem("sa_q_zero")
        s_qt, s_q, s_kt, s_kk = sem("sa_qk_turned"), sem("sa_qk_kept"), sem("sa_k_turned"), sem("sa_k_kept")
        s_qm, s_s, s_mx, s_p, s_pt, s_ptk, s_o, s_dve = (
            sem("sa_q_masked"), sem("sa_scores"), sem("sa_max"), sem("sa_probs"), sem("sa_probs_turned"),
            sem("sa_probs_kept"), sem("sa_out_done"), sem("sa_dve"))
        s_used = sem("sa_out_used")
        block = ctx.enter_context(nc.Block())

        @block.sync
        def _(sp):
            sp.dma_start(pt[:], S["proj"][SEQ:SEQ + P, 0:768]).then_inc(s_in, 16)
            for b in range(NB):
                sp.dma_start(k_in[:, b], A["cache_a_k"][0, b].rearrange("(n p) h d -> p n (h d)", p=P)).then_inc(s_k[b], 16)
            for b in range(NB):
                sp.dma_start(v_in[:, b], A["cache_a_v"][0, b].rearrange("(n p) h d -> p n (h d)", p=P)).then_inc(s_v, 16)
            sp.wait_ge(s_neg, 1)
            for b in range(NB):
                rows = slice(b * TS, (b + 1) * TS)
                sp.dma_start(band[rows, :, 0:HIST], rel_tile(S, slice(0, TS), slice(0, HIST))).then_inc(s_band, 16)
                sp.dma_start(band[rows, :, HIST + b * TS:HIST + (b + 1) * TS],
                             rel_tile(S, slice(0, TS), slice(HIST, HIST + TS))).then_inc(s_band, 16)

        @block.gpsimd
        def _(pool):
            nc.gpsimd.memset(band[:], NEG).then_inc(s_neg, 1)
            nc.gpsimd.memset(q_z[:], 0.0).then_inc(s_z, 1)
            nc.gpsimd.memset(stream_row[:], 0.0).then_inc(s_row, 1)
            pool.wait_ge(s_row, 1)
            sr = stream_row[:].rearrange("p n (b t) -> p n b t", b=NB)
            nc.gpsimd.affine_select(out=sr, in_=sr, pattern=[[1, NB], [-1, NB], [0, TS]], compare_op=ALU.not_equal,
                                    fill=1.0, base=0, channel_multiplier=0).then_inc(s_row, 1)

        @block.tensor
        def _(pe):
            t = nc.tensor
            pe.wait_ge(s_in, 16)
            for a in range(4):
                last = t.transpose(turn_ps[:, 0, a * P:(a + 1) * P], pt[:, a * P:(a + 1) * P], c["ident"][:])
            last.then_inc(s_qt, 1)
            n = 0
            for b in range(NB):
                pe.wait_ge(s_k[b], 16)
                for pair in range(2):
                    n += 1
                    if n >= 2:
                        pe.wait_ge(s_kk, n - 2) if n > 2 else None
                    if n == 2:
                        pe.wait_ge(s_q, 3)
                    for m in range(NPAST):
                        last = t.transpose(turn_ps[:, n % 2, m * P:(m + 1) * P], k_in[:, b, m, pair * P:(pair + 1) * P],
                                           c["ident"][:])
                    last.then_inc(s_kt, 1)
            pe.wait_ge(s_kk, 2 * NB)
            pe.wait_ge(s_v, 16 * NB)
            for h in range(H):
                pe.wait_ge(s_qm, h + 1)
                if h:
                    pe.wait_ge(s_mx, h)
                for b in range(NB):
                    t.matmul(s_ps[:, 0:HIST], q_m[h % 2][:, b, :], k_t[:, h // 2, b, :], start=(b == 0),
                             stop=(b == NB - 1))
                t.matmul(s_ps[:, HIST:BAND], q_z[:, h, :], k_new[:, h // 2, :], start=True, stop=True).then_inc(s_s, 1)
                pe.wait_ge(s_p, h + 1)
                for m in range(NPAST + 1):
                    last = t.transpose(p_ps[:, m * P:(m + 1) * P], prob[:, m * P:(m + 1) * P], c["ident"][:])
                last.then_inc(s_pt, 1)
                pe.wait_ge(s_ptk, h + 1)
                if h:
                    pe.wait_ge(s_used, h)
                for m in range(NPAST):
                    t.matmul(o_ps[:].rearrange("p (b d) -> p b d", b=NB), prob_t[:, m * P:(m + 1) * P],
                             v_in[:, :, m, h * DH:(h + 1) * DH], start=(m == 0), stop=(m == NPAST - 1))
                t.matmul(n_ps[:, 0:DH], prob_t[:, HIST:BAND], pt[:, VA + h * DH:VA + (h + 1) * DH], start=True,
                         stop=True).then_inc(s_o, 1)

        @block.scalar
        def _(act):
            for n in range(1, 2 * NB + 1):
                b, pair = (n - 1) // 2, (n - 1) % 2
                act.wait_ge(s_kt, n)
                nc.scalar.activation(k_t[:, pair, b, :], turn_ps[:, n % 2, :], ACT.Copy).then_inc(s_kk, 1)
            for h in range(H):
                act.wait_ge(s_mx, h + 1)
                if h:
                    act.wait_ge(s_pt, h)
                nc.scalar.activation(prob[:], score[:], ACT.Exp, bias=nmax[:, h:h + 1], accum_out=total[:, h:h + 1]
                                     ).then_inc(s_p, 1)
                act.wait_ge(s_pt, h + 1)
                if h:
                    act.wait_ge(s_o, h)
                nc.scalar.activation(prob_t[:], p_ps[:, 0:BAND], ACT.Copy).then_inc(s_ptk, 1)

        @block.vector
        def _(dve):
            v = nc.vector
            step = Steps(dve, s_dve)
            dve.wait_ge(s_qt, 1)
            dve.wait_ge(s_z, 1)
            qk = turn_ps[:, 0, :].rearrange("p (a t) -> p a t", a=4)
            v.tensor_copy(q_z[0:64, 0:4:2, :], qk[0:64, 0:2, :]).then_inc(s_q, 1)
            v.tensor_copy(q_z[64:128, 1:4:2, :], qk[64:128, 0:2, :]).then_inc(s_q, 1)
            v.tensor_copy(k_new[:], qk[:, 2:4, :]).then_inc(s_q, 1)
            dve.wait_ge(s_q, 3)
            dve.wait_ge(s_row, 2)
            dve.wait_ge(s_band, 32 * NB)

            def mask_q(h):
                if h >= 2:
                    dve.wait_ge(s_s, h - 1)
                v.tensor_tensor(q_m[h % 2][:], spread(q_z[:, h, :], 1, NB), stream_row[:], ALU.mult).then_inc(s_qm, 1)

            mask_q(0)
            for h in range(H):
                if h + 1 < H:
                    mask_q(h + 1)
                dve.wait_ge(s_s, h + 1)
                if h:
                    dve.wait_ge(s_p, h)
                step(v.scalar_tensor_tensor(score[:], s_ps[:, 0:BAND], DH ** -0.5, band[:, h, :], ALU.mult, ALU.add))
                step.settle()
                v.tensor_reduce(nmax[:, h:h + 1], score[:], AX, ALU.max, negate=True).then_inc(s_mx, 1)
                dve.wait_ge(s_p, h + 1)
                step(v.reciprocal(inv[:, h:h + 1], total[:, h:h + 1]))
                dve.wait_ge(s_o, h + 1)
                step(v.tensor_tensor(wide[:], o_ps[:].rearrange("p (b d) -> p b d", b=NB), spread(c["stream"][:], 2, DH),
                                     ALU.mult))
                step.settle()
                step(v.tensor_reduce(own[:], wide[:].rearrange("p b d -> p d b"), AX, ALU.add))
                step.settle()
                v.tensor_tensor(own[:], own[:], n_ps[:, 0:DH], ALU.add).then_inc(s_used, 1)
                dve.wait_ge(s_used, h + 1)
                step(v.tensor_scalar(ya_keep[:, h * DH:(h + 1) * DH], own[:], inv[:, h:h + 1], None, ALU.mult))
            step.settle()


ROWS = 8
R_INTER, R_FLOOR, R_WB, R_CS, R_WC, R_A, R_NCS, R_DT = range(ROWS)


def mixers(nc, sem, A, O, S, c, keep, ya_sample):
    with ExitStack() as ctx:
        sb, ps = new_pools(nc, ctx)
        w_out = sb("w_out", [P, KD, D])
        taps_c = sb("taps_c", [P, 5, KX])
        gb, gc, gd = sb("gb", [P, GW]), sb("gc", [P, GW]), sb("gd", [P, GW])
        skip = sb("skip", [P, H])
        row_par = sb("row_par", [H, 8])
        ws_t = sb("ws_t", [P, H, P])
        bs = sb("bs", [P, H])
        pt_a = [sb(f"pt_a{j}", [P, AW]) for j in range(2)]
        pt_b = [sb(f"pt_b{j}", [P, 4 * GW]) for j in range(2)]
        xt = [sb(f"xt{j}", [P, KX * NB * (TS + 3)]) for j in range(2)]
        xr = sb("xr", [P, D])
        acc, xc = sb("acc", [P, KX, P]), [sb(f"xc{j}", [P, KX, P]) for j in range(2)]
        uvs, szs = [sb(f"uv{j}", [P, 2 * GW]) for j in range(2)], [sb(f"sz{j}", [P, GW]) for j in range(2)]
        stats, mv, rs_d, rsd_m = sb("stats", [P, 6]), sb("mv", [P, 2]), sb("rs_d", [P, 1]), sb("rsd_m", [P, 1])
        vn = sb("vn", [P, GW])
        u_in, soft = sb("u_in", [H, 2, P]), sb("soft", [H, 2, P])
        ig, nb, mx = sb("ig", [H, P]), sb("nb", [H, P]), sb("mx", [H, P])
        sp_, la = soft, u_in[:, 0, :]
        row, arg, bc = sb("row", [H, ROWS, P]), sb("arg", [H, 5, P]), [sb(f"bc{j}", [H, 2, P]) for j in range(2)]
        ends = [sb(f"ends{j}", [H, 2, NB]) for j in range(2)]
        col = [sb(f"col{j}", [P, ROWS, H]) for j in range(2)]
        qkb = sb("qkb", [DH, 2 * H, P])
        dec_arg = sb("dec_arg", [P, 2 * H, P])
        wt, gt = sb("wt", [P, H, P]), sb("gt", [P, H, P])
        ws_in = wt
        v1, v1w = sb("v1", [P, H, DH + 1]), sb("v1w", [P, H, DH + 1])
        xs_b = sb("xs_b", [P, 2 * GW])
        xdt, xwl, xsk = sb("xdt", [P, H, DH]), sb("xwl", [P, H, DH]), sb("xsk", [P, H, DH])
        to = sb("to", [P, GW])
        nums, den = sb("nums", [P, H, DH + 1]), sb("den", [P, H])
        fd = nums[:, :, 0:DH]
        hb, sq, sums = sb("hb", [P, H, DH]), sb("sq", [P, H, DH]), sb("sums", [P, H])
        ssb, rsb_m, rsb = sb("ssb", [P, H]), sb("rsb_m", [P, H]), sb("rsb", [P, H])
        yz, ssc, rsc_m, rsc = sb("yz", [P, GW]), sb("ssc", [P, 1]), sb("rsc_m", [P, 1]), sb("rsc", [P, 1])
        y = [sb(f"y_mix{j}", [P, D]) for j in range(2)]
        yt = sb("yt", [P, KD, P])
        prod = sb("prod2", [P, D])
        ss2, rs2_m, rs2 = sb("ss2", [P, 1]), sb("rs2_m", [P, 1]), sb("rs2", [P, 1])
        sc_ps, pr_ps = ps("sc_ps", [P, 1024]), ps("pr_ps", [P, 1024])
        b01, b23 = ps("b01", [P, 1024]), ps("b23", [P, 1024])
        DEC = 512 - 2 * H * NB

        names = """rows_turned qk_turned scores_done cols_turned pv_done bcast_done qkb_turned cb_done qk_done
            xsb_turned nums_done ys_done state_ps_done f_done y_turned out_done h2_turned
            load_done0 load_done1 tile_stored
            gelu_done tap0_done softplus_done xc_done rows_exp prob_done prob_kept gate_tanh qkb_kept dec_exp xsb_kept
            sq_c_done yt_kept sq2_done xn2_done h2_kept
            v1_copied v1w_done xd_done rstd_d_done dec_masked rstd_b_done rstd_c_done rstd_2_done xwl_done skip_done
            qk_kept rows_in conv_done max_done args_done rows_done cols_kept var_done vn_done ya_done dec_ready
            w_done g_done yb_centred yz_done x2_done y_ready states_done probs_turned
            f_read score_read out_read nums_read h2_half load_b0 load_b1
            dve_step act_step pool_step params_loaded w_out_loaded spatial_turned alog_exp setup_dve
            vall_loaded xres_loaded""".split()
        E = {n: sem("m_" + n) for n in names}
        s_load_a, s_load_b = [E["load_done0"], E["load_done1"]], [E["load_b0"], E["load_b1"]]
        s_final, s_final2, s_ones = sem("m_final_stored"), sem("m_sample_stored"), sem("m_ones")
        N_PARAMS = 16
        steps_of = {}

        def engines(scope):
            sample = scope["sample"]
            band, k_t, v_all = scope.get("band"), scope.get("k_t"), scope.get("v_all")
            q_z, score, prob_t = (scope.get(n) for n in ("q_z", "score", "prob_t"))
            prob = score
            nmax, total, inv = (scope.get(n) for n in ("nmax", "total", "inv"))
            cst, hst, m0 = scope["cst"], scope["hst"], scope["m0"]
            mask = scope["mask"]
            batch = NB if sample else 1

            def x_view(t, j):
                flat = xt[t.parity]
                if sample:
                    return flat[:, 0:KX * NB * (TS + 3)].rearrange("p (k b t) -> p k b t", k=KX, b=NB)[:, :, :, j:j + TS]
                return flat[:, 0:KX * (P + 3)].rearrange("p (k t) -> p k t", k=KX)[:, :, j:j + P]

            def chan(ap, k):
                a = ap[:, k, :]
                return a.rearrange("p (b t) -> p b t", b=NB) if sample else a

            def blocks(i):
                return (i + 1) if isinstance(i, int) and i < NPAST else NPAST + 1

            def later(t, n=1):
                return not (isinstance(t.i, int) and t.i < n)

            W1 = DH + 1
            heads = "p (h d) -> p h d"

            def tensor_iteration(pe, t1, t2, t3):
                T = nc.tensor
                if t1:
                    p, i = pt_a[t1.parity], t1.i
                    pe.wait_ge(s_load_a[t1.parity], t1.pair * 48 + 48)
                    if later(t1):
                        pe.wait_ge(E["rows_in"], t1.i * 1)
                        if not sample:
                            pe.wait_ge(E["prob_kept"], t1.i * H)
                    if later(t1, 2):
                        pe.wait_ge(E["f_read"], t1.i - 1)
                    for n, at in enumerate((IB, FB, DT)):
                        last = T.transpose(sc_ps[0:H, 640 + n * P:640 + (n + 1) * P], p[:, at - A0:at - A0 + H], c["ident"][:])
                    last.then_inc(E["rows_turned"], 1)
                    if not sample:
                        for a in range(4):
                            last = T.transpose(pr_ps[:, a * P:(a + 1) * P], p[:, a * P:(a + 1) * P], c["ident"][:])
                        last.then_inc(E["qk_turned"], 1)
                        nk = blocks(i)
                        first_key = (i - (nk - 1)) * P
                if t3:
                    pe.wait_ge(E["y_ready"], t3.done)
                    pe.wait_ge(E["states_done"], t3.done)
                    for k in range(KD):
                        last = T.transpose(b01[:, k * P:(k + 1) * P], y[t3.parity][:, k * P:(k + 1) * P], c["ident"][:])
                    last.then_inc(E["y_turned"], 1)
                    pe.wait_ge(E["yt_kept"], t3.done)
                if t2:
                    pb = pt_b[t2.parity]
                    pe.wait_ge(s_load_b[t2.parity], t2.pair * 16 + 16)
                    for n, at in enumerate((QB, KB)):
                        for h in range(H):
                            last = T.matmul(b01[0:DH, (n * H + h) * P:(n * H + h + 1) * P],
                                            pb[:, at - QB + h * DH:at - QB + (h + 1) * DH], c["ident"][:], start=True, stop=True)
                    last.then_inc(E["qkb_turned"], 1)

                def scores(h):
                    n1 = min(nk * P, 512)
                    if h:
                        pe.wait_ge(E["score_read"], t1.nth(h - 1, H))
                    ins = T.matmul(sc_ps[:, 0:n1], q_z[:, h, :], k_t[:, h // 2, bass.ds(first_key, n1)],
                                   start=True, stop=True)
                    if nk > 4:
                        ins = T.matmul(sc_ps[:, 512:640], q_z[:, h, :], k_t[:, h // 2, bass.ds(first_key + 512, P)],
                                       start=True, stop=True)
                    ins.then_inc(E["scores_done"], 1)

                def attend(h):
                    if not t1 or sample:
                        return
                    if 1 <= h < H - 1:
                        scores(h + 1)
                    pe.wait_ge(E["prob_done"], t1.nth(h, H))
                    if h == 0:
                        pe.wait_ge(E["cols_kept"], t1.done)
                    else:
                        pe.wait_ge(E["prob_kept"], t1.nth(h - 1, H))
                    for m in range(nk):
                        last = T.transpose(pr_ps[:, m * P:(m + 1) * P], prob[h % 2][:, m * P:(m + 1) * P], c["ident"][:])
                    last.then_inc(E["probs_turned"], 1)
                    pe.wait_ge(E["prob_kept"], t1.nth(h, H))
                    if h == 0:
                        pe.wait_ge(E["vall_loaded"], 16)
                        if later(t1):
                            pe.wait_ge(E["ya_done"], t1.i * 1)
                    for m in range(nk):
                        if isinstance(i, int):
                            v = v_all[:, i - (nk - 1) + m, h * DH:(h + 1) * DH]
                        else:
                            v = v_all[:, bass.ds(i + (m - (nk - 1)), 1), h * DH:(h + 1) * DH].rearrange("p o d -> p (o d)")
                        last = T.matmul(pr_ps[:, 768 + h * DH:768 + (h + 1) * DH], prob_t[h % 2][:, m * P:(m + 1) * P], v,
                                        start=(m == 0), stop=(m == nk - 1))
                    last.then_inc(E["pv_done"], 1)

                if t1 and not sample:
                    pe.wait_ge(E["qk_kept"], t1.nth(2, 3))
                    scores(0)
                if t3:
                    pe.wait_ge(E["w_out_loaded"], 16)
                    for half in range(2):
                        if half and t1 and not sample:
                            scores(1)
                        for k in range(KD):
                            last = T.matmul(b23[:, half * 512:(half + 1) * 512], yt[:, k, :],
                                            w_out[:, k, half * 512:(half + 1) * 512], start=(k == 0), stop=(k == KD - 1))
                    last.then_inc(E["out_done"], 1)
                elif t1 and not sample:
                    scores(1)
                if t2:
                    pe.wait_ge(E["qkb_kept"], t2.done)
                    for r in range(2):
                        for h in range(H):
                            last = T.matmul(b01[:, r * 512 + h * P:r * 512 + (h + 1) * P], c["pick"][:, h, :],
                                            bc[t2.parity][:, r, :], start=True, stop=True)
                    last.then_inc(E["bcast_done"], 1)
                if t1:
                    pe.wait_ge(E["rows_done"], t1.done)
                    for r in range(ROWS):
                        last = T.matmul(pr_ps[:, 640 + r * H:640 + (r + 1) * H], row[:, r, :], c["ident"][0:H, 0:H],
                                        start=True, stop=True)
                    last.then_inc(E["cols_turned"], 1)
                if t2:
                    if t3:
                        pe.wait_ge(E["out_read"], t3.done)
                    pe.wait_ge(E["xc_done"], t2.done)
                    for g in range(2):
                        last = T.matmul(b23[:, g * P:(g + 1) * P], xc[t2.parity][:, 2 + g, :], xc[t2.parity][:, 4 + g, :],
                                        start=True, stop=True)
                    if not sample:
                        T.matmul(b23[:, DEC:DEC + 2 * H], c["ones"][0:H, :], ends[t2.parity][:, :, 0:H], start=True, stop=True)
                    for n, rows in enumerate((DH, P)):
                        for h in range(H if sample else 0):
                            at = DEC + (n * H + h) * batch
                            last = T.matmul(b23[0:rows, at:at + batch], c["pick"][:, h, 0:rows], ends[t2.parity][:, n, 0:batch],
                                            start=True, stop=True)
                    for h in range(H):
                        last = T.matmul(b23[:, 512 + h * P:512 + (h + 1) * P], qkb[:, H + h, :], qkb[:, h, :], start=True, stop=True)
                    last.then_inc(E["qk_done"], 1)
                attend(0)
                attend(1)
                if t2:
                    pe.wait_ge(E["dec_ready"], t2.done)
                    for k in range(4):
                        last = T.transpose(b01[:, k * P:(k + 1) * P], xc[t2.parity][:, k, :], c["ident"][:])
                    last.then_inc(E["xsb_turned"], 1)
                if t3:
                    pe.wait_ge(E["xn2_done"], t3.done)
                    for k in range(4):
                        last = T.transpose(b01[:, 512 + k * P:512 + (k + 1) * P], prod[:, k * P:(k + 1) * P], c["ident"][:])
                    last.then_inc(E["h2_turned"], 1)
                attend(2)
                if t3:
                    pe.wait_ge(E["h2_half"], t3.nth(0, 2))
                    for k in range(4):
                        last = T.transpose(b01[:, 512 + k * P:512 + (k + 1) * P], prod[:, (4 + k) * P:(5 + k) * P], c["ident"][:])
                    last.then_inc(E["h2_turned"], 1)
                if t2:
                    pe.wait_ge(E["g_done"], t2.done)
                    pe.wait_ge(E["v1_copied"], t2.done)
                    pe.wait_ge(E["xsb_kept"], t2.done)
                    if later(t2):
                        pe.wait_ge(E["states_done"], t2.i * 1)
                    for h in range(H):
                        last = T.matmul(b01[:, h * W1:(h + 1) * W1], wt[:, h, :], v1[:, h, :], start=True, stop=True)
                    if not sample:
                        for h in range(H):
                            last = T.matmul(b23[:, h * W1:(h + 1) * W1], qkb[:, h, :], cst[:, h, :], start=True, stop=True)
                        last.then_inc(E["nums_done"], 1)
                    else:
                        for h in range(H):
                            if h:
                                pe.wait_ge(scope["n2_used"], h)
                            for half in range(2):
                                last = T.matmul(sc_ps[:, half * 512:half * 512 + 4 * W1].rearrange("p (b e) -> p b e", b=4),
                                                qkb[:, h, :], cst[:, h, 4 * half:4 * half + 4, :], start=True, stop=True)
                            last.then_inc(scope["n2_done"], 1)
                    if not sample:
                        if t1:
                            pe.wait_ge(E["score_read"], t1.nth(H - 1, H))
                        pe.wait_ge(E["vn_done"], t2.done)
                        for g in range(H):
                            last = T.matmul(sc_ps[:, 640 + g * DH:640 + (g + 1) * DH], scope["ws_t"][:, g, :],
                                            vn[:, g * DH:(g + 1) * DH], start=True, stop=True)
                        last.then_inc(E["f_done"], 1)
                    pe.wait_ge(E["xd_done"], t2.done)
                    for h in range(H):
                        last = T.matmul(b23[:, 512 + h * DH:512 + (h + 1) * DH], gt[:, h, :], xdt[:, h, :], start=True,
                                        stop=True)
                    if not sample:
                        for h in range(H):
                            last = T.matmul(b23[:, 768 + h * DH:768 + (h + 1) * DH], xc[t2.parity][:, 4 + h // 2, :],
                                            hst[:, h, :], start=True, stop=True)
                    last.then_inc(E["ys_done"], 1)
                attend(3)
                if t2:
                    kb = KB - QB
                    if not sample:
                        pe.wait_ge(E["v1w_done"], t2.done)
                        pe.wait_ge(E["xwl_done"], t2.done)
                        pe.wait_ge(E["nums_read"], t2.done)
                        if t3:
                            pe.wait_ge(E["h2_half"], t3.nth(1, 2))
                        for h in range(H):
                            T.matmul(b01[0:DH, 512 + 0 + h * DH:512 + (h + 1) * DH], pb[:, kb + h * DH:kb + (h + 1) * DH],
                                     v1w[:, h, 0:DH], start=True, stop=True)
                        for h in range(H):
                            T.matmul(b01[0:DH, 768 + h:768 + h + 1], pb[:, kb + h * DH:kb + (h + 1) * DH],
                                     v1w[:, h, DH:W1], start=True, stop=True)
                        for h in range(H):
                            last = T.matmul(b23[:, h * DH:(h + 1) * DH], xs_b[:, GW + h // 2 * P:GW + (h // 2 + 1) * P],
                                            xwl[:, h, :], start=True, stop=True)
                        last.then_inc(E["state_ps_done"], 1)
                    else:
                        for h in range(H):
                            pe.wait_ge(scope["n2_used"], H + h)
                            T.matmul(sc_ps[:, 0:512].rearrange("p (b e) -> p b e", b=NB), xc[t2.parity][:, 4 + h // 2, :],
                                     hst[:, h, :, :], start=True, stop=True).then_inc(scope["n2_done"], 1)
                        for h in range(H):
                            pe.wait_ge(scope["n2_used"], 2 * H + h)
                            pe.wait_ge(scope["vws_done"], h + 1)
                            for half in range(2):
                                last = T.matmul(sc_ps[0:DH, half * 512:half * 512 + 4 * W1], pb[:, kb + h * DH:kb + (h + 1) * DH],
                                                scope["vws"][h % 2][:, 4 * half * W1:(4 * half + 4) * W1], start=True, stop=True)
                            last.then_inc(scope["n2_done"], 1)
                        for h in range(H):
                            pe.wait_ge(scope["n2_used"], 3 * H + h)
                            pe.wait_ge(scope["vws_done"], H + h + 1)
                            T.matmul(sc_ps[:, 0:512], xs_b[:, GW + h // 2 * P:GW + (h // 2 + 1) * P],
                                     scope["vws"][h % 2][:, 0:512], start=True, stop=True).then_inc(scope["n2_done"], 1)
                        pe.wait_ge(E["vn_done"], t2.done)
                        pe.wait_ge(scope["n2_used"], 4 * H)
                        for g in range(H):
                            last = T.matmul(sc_ps[:, 640 + g * DH:640 + (g + 1) * DH], scope["ws_t"][:, g, :],
                                            vn[:, g * DH:(g + 1) * DH], start=True, stop=True)
                        last.then_inc(E["f_done"], 1)

            def scalar_iteration(act, step, t1, t2, t3):
                a = nc.scalar
                if t3:
                    act.wait_ge(E["y_turned"], t3.done)
                    if later(t3):
                        act.wait_ge(E["tile_stored"], t3.i * 32)
                    a.activation(yt[:], b01[:].rearrange("p (k t) -> p k t", k=KD), ACT.Copy).then_inc(E["yt_kept"], 1)
                if t1:
                    act.wait_ge(E["rows_in"], t1.done)
                    step(a.activation(soft[:], u_in[:], ACT.Abs))
                    step.settle()
                    step(a.activation(soft[:], soft[:], ACT.Exp, scale=-1.0))
                    step.settle()
                    a.activation(soft[:], soft[:], ACT.Ln, bias=1.0).then_inc(E["softplus_done"], 1)
                if t2:
                    act.wait_ge(E["qkb_turned"], t2.done)
                    a.activation(qkb[:], b01[0:DH, :].rearrange("p (a t) -> p a t", a=2 * H), ACT.Copy
                                 ).then_inc(E["qkb_kept"], 1)
                if t1:
                    act.wait_ge(E["args_done"], t1.done)
                    a.activation(row[:, 0:5, :], arg[:], ACT.Exp).then_inc(E["rows_exp"], 1)
                    w = blocks(t1.i) * P

                def probs(h):
                    if not t1 or sample:
                        return
                    act.wait_ge(E["max_done"], t1.nth(h, H))
                    if h == 0 and later(t1):
                        act.wait_ge(E["ya_done"], t1.i * 1)
                    a.activation(prob[h % 2][:, 0:w], score[h % 2][:, 0:w], ACT.Exp, bias=nmax[:, h:h + 1],
                                 accum_out=total[:, h:h + 1]).then_inc(E["prob_done"], 1)

                def keep_probs(h):
                    if not t1 or sample:
                        return
                    act.wait_ge(E["probs_turned"], t1.nth(h, H))
                    if h >= 2:
                        act.wait_ge(E["pv_done"], t1.nth(h - 2, H))
                    elif later(t1):
                        act.wait_ge(E["pv_done"], t1.i * H + (h - 1))
                    a.activation(prob_t[h % 2][:, 0:w], pr_ps[:, 0:w], ACT.Copy).then_inc(E["prob_kept"], 1)

                probs(0)
                if t1:
                    p, uv, sz = pt_a[t1.parity], uvs[t1.parity], szs[t1.parity]
                    act.wait_ge(s_load_a[t1.parity], t1.pair * 48 + 48)
                    if later(t1, 2):
                        act.wait_ge(E["y_ready"], t1.i - 1)
                    step(a.activation(uv[:], p[:, UD - A0:UD - A0 + 2 * GW], ACT.Gelu_apprx_tanh))
                    a.activation(sz[:], p[:, ZC - A0:ZC - A0 + GW], ACT.Silu).then_inc(E["gelu_done"], 1)
                    if sample:
                        act.wait_ge(scope["xt_ready"], 1)
                    if later(t1):
                        act.wait_ge(E["xc_done"], t1.i * 1)
                    for k in range(KX):
                        ins = a.activation(chan(acc, k), x_view(t1, 0)[:, k], ACT.Identity, scale=taps_c[:, 0, k:k + 1],
                                           bias=taps_c[:, 4, k:k + 1])
                    ins.then_inc(E["tap0_done"], 1)
                    act.wait_ge(E["conv_done"], t1.done)
                    if later(t1, 2):
                        act.wait_ge(E["ys_done"], t1.i - 1)
                    a.activation(xc[t1.parity][:], acc[:], ACT.Silu).then_inc(E["xc_done"], 1)
                keep_probs(0)
                if t2:
                    act.wait_ge(E["dec_ready"], t2.done)
                    a.activation(dec_arg[:], dec_arg[:], ACT.Exp).then_inc(E["dec_exp"], 1)
                probs(1)
                if t3:
                    act.wait_ge(E["x2_done"], t3.done)
                    a.activation(prod[:], xr[:], ACT.Square, accum_out=ss2[:]).then_inc(E["sq2_done"], 1)
                keep_probs(1)
                if t3:
                    act.wait_ge(E["rstd_2_done"], t3.done)
                    a.activation(prod[:], xr[:], ACT.Copy, scale=rs2[:, 0:1]).then_inc(E["xn2_done"], 1)
                probs(2)
                if t2:
                    act.wait_ge(E["xsb_turned"], t2.done)
                    if later(t2) and not sample:
                        act.wait_ge(E["state_ps_done"], t2.i * 1)
                    a.activation(xs_b[:], b01[:, 0:512], ACT.Copy).then_inc(E["xsb_kept"], 1)
                    act.wait_ge(s_load_b[t2.parity], t2.pair * 16 + 16)
                    if later(t2):
                        act.wait_ge(E["y_ready"], t2.i * 1)
                    a.activation(to[:], pt_b[t2.parity][:, OB - QB:OB - QB + GW], ACT.Tanh, scale=0.5
                                 ).then_inc(E["gate_tanh"], 1)

                def keep_h2(half):
                    if not t3 or sample:
                        return
                    act.wait_ge(E["h2_turned"], t3.nth(half, 2))
                    for k in range(4):
                        kk = half * 4 + k
                        ins = a.activation(yt[:, kk, :], b01[:, 512 + k * P:512 + (k + 1) * P], ACT.Identity,
                                           scale=keep["ffn_scale"][:, kk, 0:1], bias=keep["ffn_shift"][:, kk, 0:1])
                    ins.then_inc(E["h2_half"], 1)

                keep_h2(0)
                keep_probs(2)
                probs(3)
                keep_h2(1)
                keep_probs(3)
                if t2:
                    act.wait_ge(E["yz_done"], t2.done)
                    a.activation(xdt[:].rearrange("p h d -> p (h d)"), yz[:], ACT.Square, accum_out=ssc[:]
                                 ).then_inc(E["sq_c_done"], 1)

            def pool_iteration(pool, step, t1, t2, t3):
                g = nc.gpsimd

                def rstd(out, mid, square_sum, at, width, signal):
                    step(g.tensor_tensor(mid, square_sum, c["per_width"][:, at:at + width], ALU.mult))
                    step.settle()
                    step(g.tensor_tensor(mid, mid, c["eps"][:, 0:width], ALU.add))
                    step.settle()
                    g.tensor_tensor(out, mid, c["minus_half"][:, 0:width], ALU.pow).then_inc(E[signal], 1)

                if t2:
                    cl = col[t2.parity]
                    pool.wait_ge(s_load_b[t2.parity], t2.pair * 16 + 16)
                    pool.wait_ge(E["cols_kept"], t2.done)
                    if later(t2):
                        pool.wait_ge(E["ys_done"], t2.i * 1)
                        if not sample:
                            pool.wait_ge(E["state_ps_done"], t2.i * 1)
                    g.tensor_tensor(v1[:, :, 0:DH], pt_b[t2.parity][:, VB - QB:VB - QB + GW].rearrange(heads, h=H),
                                    c["ones"][:, 0:1].unsqueeze(2).to_broadcast([P, H, DH]), ALU.mult
                                    ).then_inc(E["v1_copied"], 1)
                    pool.wait_ge(E["v1_copied"], t2.done)
                    g.tensor_tensor(v1w[:], v1[:], spread(cl[:, R_WB, :], 2, W1), ALU.mult).then_inc(E["v1w_done"], 1)
                    pool.wait_ge(E["var_done"], t2.done)
                    step(g.tensor_tensor(rsd_m[:], mv[:, 1:2], c["eps"][:, 0:1], ALU.add))
                    step.settle()
                    g.tensor_tensor(rs_d[:], rsd_m[:], c["minus_half"][:, 0:1], ALU.pow).then_inc(E["rstd_d_done"], 1)
                    pool.wait_ge(E["dec_exp"], t2.done)
                    g.tensor_tensor(dec_arg[:], dec_arg[:], spread(mask[:], 1, 2 * H), ALU.mult).then_inc(E["dec_masked"], 1)
                if t3:
                    pool.wait_ge(E["sq2_done"], t3.done)
                    rstd(rs2[:], rs2_m[:], ss2[:], H + 1, 1, "rstd_2_done")
                if t2:
                    pool.wait_ge(E["xsb_kept"], t2.done)
                    if later(t2):
                        pool.wait_ge(E["sq_c_done"], t2.i * 1)
                    xs = xs_b[:, 0:GW].rearrange(heads, h=H)
                    g.tensor_tensor(xdt[:], xs, spread(cl[:, R_DT, :], 2, DH), ALU.mult).then_inc(E["xd_done"], 1)
                    g.tensor_tensor(xwl[:], xs, spread(cl[:, R_WC, :], 2, DH), ALU.mult).then_inc(E["xwl_done"], 1)
                    g.tensor_tensor(xsk[:], xs, spread(skip[:], 2, DH), ALU.mult).then_inc(E["skip_done"], 1)
                    pool.wait_ge(E["yb_centred"], t2.done)
                    rstd(rsb[:], rsb_m[:], ssb[:], 0, H, "rstd_b_done")
                    pool.wait_ge(E["sq_c_done"], t2.done)
                    rstd(rsc[:], rsc_m[:], ssc[:], H, 1, "rstd_c_done")

            def vector_iteration(dve, step, t1, t2, t3):
                v = nc.vector
                if t1:
                    dve.wait_ge(E["rows_turned"], t1.done)
                    step(v.tensor_scalar(u_in[:, 0, :], sc_ps[0:H, 640 + P:640 + 2 * P], row_par[:, 1:2], -1.0, ALU.add, ALU.mult))
                    step(v.tensor_scalar(ig[:], sc_ps[0:H, 640:640 + P], row_par[:, 0:1], None, ALU.add))
                    v.tensor_scalar(u_in[:, 1, :], sc_ps[0:H, 640 + 2 * P:640 + 3 * P], row_par[:, 2:3], None, ALU.add
                                    ).then_inc(E["rows_in"], 1)
                    if not sample:
                        dve.wait_ge(E["qk_turned"], t1.done)
                        qk = pr_ps[:, 0:512].rearrange("p (a t) -> p a t", a=4)
                        v.tensor_copy(q_z[0:64, 0:4:2, :], qk[0:64, 0:2, :]).then_inc(E["qk_kept"], 1)
                        v.tensor_copy(q_z[64:128, 1:4:2, :], qk[64:128, 0:2, :]).then_inc(E["qk_kept"], 1)
                        v.tensor_copy(k_t[:, :, bass.ds(t1.i * P, P)], qk[:, 2:4, :]).then_inc(E["qk_kept"], 1)
                def scores(h):
                    if not t1 or sample:
                        return
                    w = blocks(t1.i) * P
                    dve.wait_ge(E["scores_done"], t1.nth(h, H))
                    if h >= 2:
                        dve.wait_ge(E["probs_turned"], t1.nth(h - 2, H))
                    v.scalar_tensor_tensor(score[h % 2][:, 0:w], sc_ps[:, 0:w], DH ** -0.5,
                                           band[:, h, BAND - w:BAND], ALU.mult, ALU.add).then_inc(E["score_read"], 1)
                    dve.wait_ge(E["score_read"], t1.nth(h, H))
                    v.tensor_reduce(nmax[:, h:h + 1], score[h % 2][:, 0:w], AX, ALU.max, negate=True
                                    ).then_inc(E["max_done"], 1)

                if t1:
                    bcj = bc[t1.parity]
                    dve.wait_ge(E["softplus_done"], t1.done)
                    step(v.scalar_tensor_tensor(sp_[:], u_in[:], 0.0, soft[:], ALU.max, ALU.add))
                    step.settle()
                    step(v.tensor_scalar(la, sp_[:, 1, :], row_par[:, 4:5], None, ALU.mult))
                    step(v.tensor_copy(row[:, R_DT, :], sp_[:, 1, :]))
                    segments = [(b * TS, (b + 1) * TS) for b in range(NB)] if sample else [(0, P)]
                    for lo, hi in segments:
                        ins = v.tensor_tensor_scan(nb[:, lo:hi], c["ones"][0:H, lo:hi], sp_[:, 0, lo:hi], 0.0, ALU.mult, ALU.add)
                    step(ins)
                    step.settle()
                    for lo, hi in segments:
                        ins = v.tensor_tensor_scan(arg[:, 3, lo:hi], c["ones"][0:H, lo:hi], u_in[:, 0, lo:hi], 0.0, ALU.mult, ALU.add)
                    step(v.tensor_tensor(row[:, R_A, :], ig[:], nb[:], ALU.add))
                    step.settle()
                    for n, (lo, hi) in enumerate(segments):
                        ins = v.tensor_tensor_scan(mx[:, lo:hi], row[:, R_A, lo:hi], row[:, R_A, lo:hi], m0[:, n:n + 1],
                                                   ALU.max, ALU.max)
                    step(v.tensor_copy(bcj[:, 1, :], arg[:, 3, :]))
                    step.settle()
                    step(v.tensor_scalar(row[:, R_NCS, :], arg[:, 3, :], -1.0, None, ALU.mult))
                    step(v.tensor_tensor(arg[:, 1, :], nb[:], mx[:], ALU.subtract))
                    step(v.tensor_scalar(bcj[:, 0, :], mx[:], -1.0, None, ALU.mult))
                    if not sample:
                        step(v.tensor_scalar(arg[:, 0, :], mx[:], m0[:, 0:1], -1.0, ALU.subtract, ALU.mult))
                        step(v.tensor_scalar(arg[:, 2, :], row[:, R_A, :], mx[:, P - 1:P], None, ALU.subtract))
                        step(v.tensor_scalar(arg[:, 4, :], arg[:, 3, :], arg[:, 3, P - 1:P], -1.0, ALU.subtract, ALU.mult))
                        step.settle()
                        v.tensor_tensor(m0[:], mx[:, P - 1:P], nb[:, P - 1:P], ALU.subtract).then_inc(E["args_done"], 1)
                    else:
                        def streams(ap):
                            return ap.rearrange("h (b t) -> h b t", b=NB)

                        step(v.tensor_tensor(streams(arg[:, 0, :]), spread(m0[:], 2, TS), streams(mx[:]), ALU.subtract))
                        step(v.tensor_tensor(streams(arg[:, 2, :]), streams(row[:, R_A, :]), spread(mx[:, TS - 1:P:TS], 2, TS),
                                             ALU.subtract))
                        step(v.tensor_tensor(streams(arg[:, 4, :]), spread(arg[:, 3, TS - 1:P:TS], 2, TS),
                                             streams(arg[:, 3, :]), ALU.subtract))
                        step.settle()
                        v.tensor_tensor(m0[:], mx[:, TS - 1:P:TS], nb[:, TS - 1:P:TS], ALU.subtract).then_inc(E["args_done"], 1)
                scores(0)
                if t1:
                    dve.wait_ge(E["tap0_done"], t1.done)
                    for tap in range(1, 4):
                        for k in range(KX):
                            ins = v.scalar_tensor_tensor(chan(acc, k), x_view(t1, tap)[:, k], taps_c[:, tap, k:k + 1],
                                                         chan(acc, k), ALU.mult, ALU.add)
                        if tap < 3:
                            step(ins)
                            step.settle()
                    ins.then_inc(E["conv_done"], 1)
                scores(1)
                if t1:
                    dve.wait_ge(E["rows_exp"], t1.done)
                    for n, r in enumerate((R_INTER, R_CS)):
                        if sample:
                            step(v.tensor_copy(ends[t1.parity][:, n, :], row[:, r, TS - 1:P:TS]))
                        else:
                            step(v.tensor_scalar(ends[t1.parity][:, n, 0:H], c["ident"][0:H, 0:H], row[:, r, P - 1:P], None,
                                                 ALU.mult))
                    v.tensor_tensor(row[:, R_WC, :], row[:, R_WC, :], row[:, R_DT, :], ALU.mult).then_inc(E["rows_done"], 1)
                if t2:
                    step(v.bn_stats(stats[:], uvs[t2.parity][:, GW:2 * GW]))
                if t3:
                    dve.wait_ge(E["out_done"], t3.done)
                    dve.wait_ge(E["xres_loaded"], t3.i * 16 + 16)
                    if later(t3):
                        dve.wait_ge(E["h2_turned"], t3.i * 2)
                    v.tensor_tensor(prod[:], b23[:], keep["mix_gate"][:, 1 if sample else 0, :], ALU.mult
                                    ).then_inc(E["out_read"], 1)
                if t2:
                    dve.wait_ge(E["cols_kept"], t2.done)
                    dve.wait_ge(E["bcast_done"], t2.done)
                    if later(t2):
                        dve.wait_ge(E["g_done"], t2.i * 1)
                    for n, r in enumerate((R_A, R_NCS)):
                        for h in range(H):
                            at = n * 512 + h * P
                            ins = v.tensor_scalar(dec_arg[:, n * H + h, :], b01[:, at:at + P], col[t2.parity][:, r, h:h + 1], 0.0,
                                                  ALU.add, ALU.min)
                    ins.then_inc(E["dec_ready"], 1)
                if t1:
                    dve.wait_ge(E["cols_turned"], t1.done)
                    v.tensor_copy(col[t1.parity][:], pr_ps[:, 640:640 + ROWS * H].rearrange("p (r h) -> p r h", r=ROWS)
                                  ).then_inc(E["cols_kept"], 1)
                if t3:
                    dve.wait_ge(E["out_read"], t3.done)
                    v.tensor_tensor(xr[:], xr[:], prod[:], ALU.add).then_inc(E["x2_done"], 1)
                elif t2:
                    step.settle()
                if t2:
                    v.bn_aggr(mv[:], stats[:]).then_inc(E["var_done"], 1)
                if t3 and sample:
                    for half in range(2):
                        ks = slice(half * 4, half * 4 + 4)
                        dve.wait_ge(E["h2_turned"], t3.nth(half, 2))
                        h2 = yt[:, ks, :].rearrange("p k (b t) -> p k b t", b=NB)
                        step(v.tensor_tensor(h2, b01[:, 512:1024].rearrange("p (k b t) -> p k b t", k=4, b=NB),
                                             spread(keep["ffn_scale"][:, ks, 1:], 3, TS), ALU.mult))
                        step.settle()
                        v.tensor_tensor(h2, h2, spread(keep["ffn_shift"][:, ks, 1:], 3, TS), ALU.add
                                        ).then_inc(E["h2_half"], 1)
                scores(2)
                if t2:
                    uv, sz, cl, yj = uvs[t2.parity], szs[t2.parity], col[t2.parity], y[t2.parity]
                    dve.wait_ge(E["rstd_d_done"], t2.done)
                    if later(t2):
                        dve.wait_ge(E["f_done"], t2.i * 1)
                    step(v.tensor_scalar(vn[:], uv[:, GW:2 * GW], mv[:, 0:1], rs_d[:, 0:1], ALU.subtract, ALU.mult))
                    step.settle()
                    v.tensor_tensor(vn[:], vn[:], gd[:], ALU.mult).then_inc(E["vn_done"], 1)
                    dve.wait_ge(E["dec_masked"], t2.done)
                    dve.wait_ge(E["qk_done"], t2.done)
                    step(v.scalar_tensor_tensor(wt[:], b23[:, 512:1024].rearrange("p (h t) -> p h t", h=H), DH ** -0.5,
                                                dec_arg[:, 0:H, :], ALU.mult, ALU.mult))
                    for grp in range(2):
                        ins = v.tensor_tensor(gt[:, 2 * grp:2 * grp + 2, :], spread(b23[:, grp * P:(grp + 1) * P], 1, 2),
                                              dec_arg[:, H + 2 * grp:H + 2 * grp + 2, :], ALU.mult)
                    ins.then_inc(E["g_done"], 1)
                def mixer_d():
                    dve.wait_ge(E["f_done"], t2.done)
                    v.tensor_tensor(fd, sc_ps[:, 640:640 + GW].rearrange(heads, h=H),
                                    spread(scope["bs"][:], 2, DH), ALU.add).then_inc(E["f_read"], 1)
                    dve.wait_ge(E["f_read"], t2.done)
                    step(v.tensor_tensor(yj[:, 3 * GW:4 * GW].rearrange(heads, h=H), fd,
                                         uv[:, 0:GW].rearrange(heads, h=H), ALU.mult))

                scores(3)
                if t2:
                    if not sample:
                        dve.wait_ge(E["nums_done"], t2.done)
                        step(v.tensor_tensor(nums[:], b23[:, 0:H * W1].rearrange("p (h e) -> p h e", h=H),
                                             spread(cl[:, R_INTER, :], 2, W1), ALU.mult))
                    else:
                        wide = scope["wide"]
                        for h in range(H):
                            dve.wait_ge(scope["n2_done"], h + 1)
                            for half in range(2):
                                ins = v.tensor_tensor(wide[:, 4 * half:4 * half + 4, :],
                                                      sc_ps[:, half * 512:half * 512 + 4 * W1].rearrange("p (b e) -> p b e", b=4),
                                                      spread(c["stream"][:, 4 * half:4 * half + 4], 2, W1), ALU.mult)
                            ins.then_inc(scope["n2_used"], 1)
                            dve.wait_ge(scope["n2_used"], h + 1)
                            step(v.tensor_reduce(nums[:, h, :], wide[:].rearrange("p b e -> p e b"), AX, ALU.add))
                            step.settle()
                        step(v.tensor_tensor(nums[:], nums[:], spread(cl[:, R_INTER, :], 2, W1), ALU.mult))
                    step.settle()
                    v.tensor_tensor(nums[:], nums[:], b01[:, 0:H * W1].rearrange("p (h e) -> p h e", h=H), ALU.add
                                    ).then_inc(E["nums_read"], 1)
                    dve.wait_ge(E["nums_read"], t2.done)
                    dn = nums[:, :, DH]
                    step(v.scalar_tensor_tensor(den[:], dn, -1.0, dn, ALU.mult, ALU.max))
                    step.settle()
                    step(v.tensor_tensor(den[:], den[:], cl[:, R_FLOOR, :], ALU.max))
                    step.settle()
                    step(v.reciprocal(den[:], den[:]))
                    step.settle()
                    step(v.tensor_tensor(hb[:], nums[:, :, 0:DH], spread(den[:], 2, DH), ALU.mult))
                    step.settle()
                    step(v.tensor_reduce(sums[:], hb[:], AX, ALU.add))
                    step.settle()
                    step(v.tensor_scalar(sums[:], sums[:], 1.0 / DH, None, ALU.mult))
                    step.settle()
                    step(v.tensor_tensor(hb[:], hb[:], spread(sums[:], 2, DH), ALU.subtract))
                    step.settle()
                    step(v.tensor_tensor(sq[:], hb[:], hb[:], ALU.mult))
                    step.settle()
                    v.tensor_reduce(ssb[:], sq[:], AX, ALU.add).then_inc(E["yb_centred"], 1)
                    if not sample:
                        mixer_d()
                    dve.wait_ge(E["ys_done"], t2.done)
                    yz3 = yz[:].rearrange(heads, h=H)
                    if not sample:
                        step(v.tensor_tensor(yz3, b23[:, 768:1024].rearrange(heads, h=H),
                                             spread(cl[:, R_CS, :], 2, DH), ALU.mult))
                    else:
                        for h in range(H):
                            dve.wait_ge(scope["n2_done"], H + h + 1)
                            v.tensor_tensor(wide[:, :, 0:DH], sc_ps[:, 0:512].rearrange("p (b e) -> p b e", b=NB),
                                            spread(c["stream"][:], 2, DH), ALU.mult).then_inc(scope["n2_used"], 1)
                            dve.wait_ge(scope["n2_used"], H + h + 1)
                            step(v.tensor_reduce(yz3[:, h, :], wide[:, :, 0:DH].rearrange("p b e -> p e b"), AX, ALU.add))
                            step.settle()
                        step(v.tensor_tensor(yz3, yz3, spread(cl[:, R_CS, :], 2, DH), ALU.mult))
                    step.settle()
                    step(v.tensor_tensor(yz[:], yz[:], b23[:, 512:768], ALU.add))
                    dve.wait_ge(E["skip_done"], t2.done)
                    step.settle()
                    step(v.tensor_tensor(yz3, yz3, xsk[:], ALU.add))
                    step.settle()
                    v.tensor_tensor(yz[:], yz[:], sz[:], ALU.mult).then_inc(E["yz_done"], 1)
                    dve.wait_ge(E["rstd_b_done"], t2.done)
                    step(v.tensor_tensor(hb[:], hb[:], spread(rsb[:], 2, DH), ALU.mult))
                    dve.wait_ge(E["gate_tanh"], t2.done)
                    step.settle()
                    step(v.scalar_tensor_tensor(sq[:].rearrange("p h d -> p (h d)"), to[:], 1.0,
                                                hb[:].rearrange("p h d -> p (h d)"), ALU.add, ALU.mult))
                    step.settle()
                    step(v.tensor_tensor(yj[:, GW:2 * GW], sq[:].rearrange("p h d -> p (h d)"), gb[:], ALU.mult))
                if t1 and not sample:
                    dve.wait_ge(E["pv_done"], t1.nth(H - 1, H))
                    if later(t1, 2):
                        dve.wait_ge(E["y_turned"], t1.i - 1)
                    step(v.reciprocal(inv[:], total[:]))
                    step.settle()
                    v.tensor_tensor(y[t1.parity][:, 0:GW].rearrange(heads, h=H),
                                    pr_ps[:, 768:1024].rearrange(heads, h=H), spread(inv[:], 2, DH), ALU.mult
                                    ).then_inc(E["ya_done"], 1)
                elif t1:
                    step(v.tensor_copy(y[t1.parity][:, 0:GW], ya_sample[:]))
                if t2:
                    if not sample:
                        dve.wait_ge(E["state_ps_done"], t2.done)
                        step(v.tensor_tensor(cst[:], cst[:], spread(b23[0:DH, DEC:DEC + H], 2, W1), ALU.mult))
                        step(v.tensor_tensor(hst[:], hst[:], spread(b23[:, DEC + H:DEC + 2 * H], 2, DH), ALU.mult))
                        step.settle()
                        step(v.scalar_tensor_tensor(cst[:, :, 0:DH], b01[0:DH, 512:768].rearrange(heads, h=H),
                                                    DH ** -0.5, cst[:, :, 0:DH], ALU.mult, ALU.add))
                        step(v.scalar_tensor_tensor(cst[:, :, DH], b01[0:DH, 768:768 + H], DH ** -0.5, cst[:, :, DH],
                                                    ALU.mult, ALU.add))
                        v.tensor_tensor(hst[:], hst[:], b23[:, 0:256].rearrange("p (h e) -> p h e", h=H), ALU.add
                                        ).then_inc(E["states_done"], 1)
                    else:
                        vws = scope["vws"]

                        def weigh(n):
                            h = n % H
                            if n >= 2:
                                dve.wait_ge(scope["n2_done"], 2 * H + n - 1)
                            width, src = (W1, v1w) if n < H else (DH, xwl)
                            dst = vws[n % 2][:, 0:NB * width].rearrange("p (b e) -> p b e", b=NB)
                            v.tensor_tensor(dst, spread(src[:, h, :], 1, NB), spread(c["stream"][:], 2, width), ALU.mult
                                            ).then_inc(scope["vws_done"], 1)

                        dve.wait_ge(E["v1w_done"], t2.done)
                        dve.wait_ge(E["xwl_done"], t2.done)
                        weigh(0)
                        weigh(1)
                        for n in range(2 * H):
                            h = n % H
                            if n < H:
                                dec = spread(b23[0:DH, DEC + h * NB:DEC + (h + 1) * NB], 2, W1)
                                step(v.tensor_tensor(cst[:, h], cst[:, h], dec, ALU.mult))
                                dve.wait_ge(scope["n2_done"], 2 * H + n + 1)
                                step.settle()
                                for half in range(2):
                                    b4 = slice(4 * half, 4 * half + 4)
                                    ins = v.scalar_tensor_tensor(
                                        cst[:, h, b4, :],
                                        sc_ps[0:DH, half * 512:half * 512 + 4 * W1].rearrange("p (b e) -> p b e", b=4),
                                        DH ** -0.5, cst[:, h, b4, :], ALU.mult, ALU.add)
                                ins.then_inc(scope["n2_used"], 1)
                            else:
                                dec = spread(b23[:, DEC + (H + h) * NB:DEC + (H + h + 1) * NB], 2, DH)
                                step(v.tensor_tensor(hst[:, h], hst[:, h], dec, ALU.mult))
                                dve.wait_ge(scope["n2_done"], 2 * H + n + 1)
                                step.settle()
                                ins = v.tensor_tensor(hst[:, h], hst[:, h], sc_ps[:, 0:512].rearrange("p (b e) -> p b e", b=NB),
                                                      ALU.add)
                                ins.then_inc(scope["n2_used"], 1)
                            if n + 2 < 2 * H:
                                weigh(n + 2)
                        dve.wait_ge(scope["n2_used"], 4 * H)
                        v.tensor_copy(stats[:, 0:1], stats[:, 0:1]).then_inc(E["states_done"], 1)
                    if sample:
                        mixer_d()
                    dve.wait_ge(E["rstd_c_done"], t2.done)
                    step.settle()
                    v.scalar_tensor_tensor(yj[:, 2 * GW:3 * GW], yz[:], rsc[:, 0:1], gc[:], ALU.mult, ALU.mult
                                           ).then_inc(E["y_ready"], 1)

            return tensor_iteration, scalar_iteration, pool_iteration, vector_iteration

        def prompt_iterations(engine, iteration, steps=None):
            def run(n, front, middle, back):
                args = [Tile(*at) if at else None for at in (front, middle, back)]
                if steps:
                    iteration(engine, steps, *args)
                else:
                    iteration(engine, *args)

            def at(n):
                return (n // 2, n % 2) if 0 <= n < NT else None

            for n in range(NPAST):
                if steps:
                    steps.next()
                run(n, at(n), at(n - 1), at(n - 2))
            if steps:
                steps.next()
                first = steps.base
            with engine.Fori(NPAST // 2, NT // 2) as pair:
                if steps:
                    steps.base = pair * (2 * steps.per_tile) + (first - NPAST * steps.per_tile)
                    steps.count = 0
                run(None, (pair, 0), (pair - 1, 1), (pair - 1, 0))
                run(None, (pair, 1), (pair, 0), (pair - 1, 1))
                assert not steps or steps.count == 2 * steps.per_tile, (steps.count, steps.per_tile)
            if steps:
                steps.base, steps.count = first + (NT - NPAST) * steps.per_tile, 0
            for n in (NT, NT + 1):
                if steps:
                    steps.next()
                run(n, at(n), at(n - 1), at(n - 2))

        def sample_iterations(engine, iteration, steps=None):
            t = Tile(NT // 2, 0)
            for parts in ((t, None, None), (None, t, None), (None, None, t)):
                if steps:
                    steps.next()
                    iteration(engine, steps, *parts)
                else:
                    iteration(engine, *parts)

        with ExitStack() as pctx:
            psb, _ = new_pools(nc, pctx)
            scope = {
                "sample": False, "mask": c["tri"], "ws_t": ws_t, "bs": bs,
                "band": psb("band", [P, H, BAND]), "k_t": psb("k_t_p", [P, 2, SEQ]), "v_all": psb("v_all", [P, NT, GW]),
                "q_z": psb("q_z_p", [P, H, P]), "score": [psb(f"score{n}", [P, BAND]) for n in range(2)],
                "prob_t": [psb(f"prob_t{n}", [P, BAND]) for n in range(2)],
                "nmax": psb("nmax", [P, H]), "total": psb("total", [P, H]), "inv": psb("inv", [P, H]),
                "cst": psb("cst", [DH, H, DH + 1]), "hst": psb("hst", [P, H, DH]), "m0": psb("m0", [H, 1]),
            }
            band, cst, hst, m0 = (scope[n] for n in ("band", "cst", "hst", "m0"))
            ssm_out = prod[0:DH, 0:512]
            tensor_iteration, scalar_iteration, pool_iteration, vector_iteration = engines(scope)
            block = pctx.enter_context(nc.Block())

            @block.sync
            def _(sp):
                def load_a(i, j):
                    sp.dma_start(pt_a[j][:, 0:2 * GW], S["proj"][bass.ds(i * P, P), 0:2 * GW]).then_inc(s_load_a[j], 16)
                    sp.dma_start(pt_a[j][:, 2 * GW:], S["proj"][bass.ds(i * P, P), IB:PW]).then_inc(s_load_a[j], 16)
                    sp.dma_start(xt[j][:, 0:KX * (P + 3)].rearrange("p (k t) -> p k t", k=KX),
                                 S["xbc"][:, :, bass.ds(i * P, P + 3)]).then_inc(s_load_a[j], 16)

                def load_b(i, j):
                    sp.dma_start(pt_b[j][:], S["proj"][bass.ds(i * P, P), QB:IB]).then_inc(s_load_b[j], 16)

                def load_x(i):
                    sp.dma_start(xr[:], A["x_prompt"][0, bass.ds(i * P, P), :]).then_inc(E["xres_loaded"], 16)

                params = [(row_par[:, n:n + 1], A[name].rearrange("a h -> h a"))
                          for n, name in enumerate(("b_i_bias", "b_f_bias", "c_dt_bias", "c_a_log"))]
                params += [(skip[:], A["c_d_skip"][0].partition_broadcast(P)),
                           (gb[:], A["b_norm_g"][0].partition_broadcast(P)),
                           (gc[:], A["c_norm_g"][0].partition_broadcast(P)),
                           (gd[:], A["d_norm_g"][0].partition_broadcast(P)),
                           (bs[:], A["d_b_s"][0].rearrange("g t -> t g")),
                           (taps_c[:, 4, :], A["c_conv_b"][0].rearrange("(k p) -> p k", p=P)),
                           (ws_in[:], A["d_w_s"][0].rearrange("g t s -> t g s")),
                           (band[:], rel_tile(S, slice(0, P), slice(0, BAND)))]
                params += [(taps_c[:, n, :], A["c_conv_w"][0, n].rearrange("(k p) -> p k", p=P)) for n in range(4)]
                for dst, src in params:
                    sp.dma_start(dst, src, allow_slow_non_contiguous=True).then_inc(E["params_loaded"], 16)
                assert len(params) == N_PARAMS
                for i in range(2):
                    load_a(i, i)
                for i in range(2):
                    load_b(i, i)
                sp.dma_start(scope["v_all"][:], S["proj"][0:SEQ, VA:VA + GW].rearrange("(n p) d -> p n d", p=P)
                             ).then_inc(E["vall_loaded"], 16)
                load_x(0)
                sp.dma_start(w_out[:], A["w_out"][0].rearrange("(k p) n -> p k n", p=P)).then_inc(E["w_out_loaded"], 16)

                copies = [(O["p_a_k"][0, 0].rearrange("t h d -> t (h d)"), S["proj"][SEQ - HIST:SEQ, KA:KA + GW]),
                          (O["p_a_v"][0, 0].rearrange("t h d -> t (h d)"), S["proj"][SEQ - HIST:SEQ, VA:VA + GW]),
                          (O["s_a_k"][0].rearrange("b t h d -> (b t) (h d)"), S["proj"][SEQ:SEQ + P, KA:KA + GW]),
                          (O["s_a_v"][0].rearrange("b t h d -> (b t) (h d)"), S["proj"][SEQ:SEQ + P, VA:VA + GW])]
                for n in range(3):
                    copies.append((O["p_c_conv"][0, 0, n].rearrange("(k p) -> p k", p=P), S["xbc"][:, :, SEQ + n]))
                for dst, src in copies:
                    sp.dma_start(dst, src, allow_slow_non_contiguous=True).then_inc(s_final, 16)

                def iteration(front, middle, back, more=True):
                    if front:
                        sp.wait_ge(E["qk_turned"], front.done)
                        sp.wait_ge(E["gelu_done"], front.done)
                        sp.wait_ge(E["conv_done"], front.done)
                        load_a(front.i + 2, front.parity)
                    if back:
                        sp.wait_ge(E["h2_half"], back.nth(1, 2))
                        sp.dma_start(S["x2"][bass.ds(back.i * P, P), :], xr[:]).then_inc(E["tile_stored"], 16)
                        sp.dma_start(S["h2t"][:, :, bass.ds(back.i * P, P)], yt[:]).then_inc(E["tile_stored"], 16)
                        if more:
                            sp.wait_ge(E["tile_stored"], back.i * 32 + 32)
                            load_x(back.i + 1)
                    if middle:
                        sp.wait_ge(E["gate_tanh"], middle.done)
                        sp.wait_ge(E["state_ps_done"], middle.done)
                        load_b(middle.i + 2, middle.parity)

                def tile_at(n, end=NT):
                    return Tile(n // 2, n % 2) if 0 <= n < end else None

                for n in range(NPAST):
                    iteration(tile_at(n), tile_at(n - 1), tile_at(n - 2))
                with sp.Fori(NPAST // 2, NT // 2 - 1) as pair:
                    iteration(Tile(pair, 0), Tile(pair - 1, 1), Tile(pair - 1, 0))
                    iteration(Tile(pair, 1), Tile(pair, 0), Tile(pair - 1, 1))
                for n in range(NT - 2, NT + 2):
                    iteration(tile_at(n, NT - 2), tile_at(n - 1, NT - 2), tile_at(n - 2), more=n < NT + 1)
                sp.wait_ge(E["tile_stored"], 32 * NT)
                sp.wait_ge(E["setup_dve"], 9)
                finals = [(O["p_c_ssm"][0, 0].rearrange("h p n -> p h n"), ssm_out.rearrange("p (h n) -> p h n", h=H)),
                          (O["p_b_c"][0, 0].rearrange("h d e -> d h e"), cst[:, :, 0:DH]),
                          (O["p_b_n"][0, 0].rearrange("h d -> d h"), cst[:, :, DH]),
                          (O["p_b_m"][0].rearrange("a h -> h a"), m0[:])]
                for dst, src in finals:
                    sp.dma_start(dst, src, allow_slow_non_contiguous=True).then_inc(s_final, 16)
                sp.wait_ge(s_final, 16 * (len(copies) + len(finals)))

            @block.tensor
            def _(pe):
                pe.wait_ge(E["params_loaded"], 16 * N_PARAMS)
                for g in range(H):
                    last = nc.tensor.transpose(b01[:, g * P:(g + 1) * P], ws_in[:, g, :], c["ident"][:])
                last.then_inc(E["spatial_turned"], 1)
                pe.wait_ge(E["setup_dve"], 7)
                prompt_iterations(pe, tensor_iteration)
                pe.wait_ge(E["states_done"], NT)
                for h in range(H):
                    last = nc.tensor.transpose(pr_ps[0:DH, h * P:(h + 1) * P], hst[:, h, :], c["ident"][:])
                last.then_inc(E["spatial_turned"], 1)

            @block.scalar
            def _(act):
                step = Steps(act, E["act_step"])
                act.wait_ge(E["params_loaded"], 16 * N_PARAMS)
                nc.scalar.activation(row_par[:, 4:5], row_par[:, 3:4], ACT.Exp).then_inc(E["alog_exp"], 1)
                prompt_iterations(act, scalar_iteration, step)
                steps_of["act"] = step

            @block.gpsimd
            def _(pool):
                step = Steps(pool, E["pool_step"])
                nc.gpsimd.memset(v1[:, :, DH:DH + 1], 1.0).then_inc(s_ones, 1)
                nc.gpsimd.memset(scope["q_z"][:], 0.0).then_inc(s_ones, 1)
                pool.wait_ge(s_ones, 2)
                pool.wait_ge(E["params_loaded"], 16 * N_PARAMS)
                prompt_iterations(pool, pool_iteration, step)
                steps_of["pool"] = step

            @block.vector
            def _(dve):
                step = Steps(dve, E["dve_step"])
                v, ready = nc.vector, E["setup_dve"]
                dve.wait_ge(E["params_loaded"], 16 * N_PARAMS)
                v.memset(cst[:], 0.0).then_inc(ready, 1)
                v.memset(hst[:], 0.0).then_inc(ready, 1)
                v.memset(m0[:], 0.0).then_inc(ready, 1)
                v.memset(band[0:64, :, BAND - 64:BAND], NEG).then_inc(ready, 1)
                v.memset(band[64:128, :, 0:64], NEG).then_inc(ready, 1)
                v.tensor_scalar(gb[:], gb[:], 0.5, None, ALU.mult).then_inc(ready, 1)
                dve.wait_ge(E["spatial_turned"], 1)
                v.tensor_tensor(ws_t[:], b01[:, 0:512].rearrange("p (g t) -> p g t", g=H), spread(c["tri"][:], 1, H),
                                ALU.mult).then_inc(ready, 1)
                dve.wait_ge(E["alog_exp"], 1)
                v.tensor_scalar(row_par[:, 4:5], row_par[:, 4:5], -1.0, None, ALU.mult).then_inc(ready, 1)
                dve.wait_ge(ready, 8)
                dve.wait_ge(s_ones, 2)
                prompt_iterations(dve, vector_iteration, step)
                dve.wait_ge(E["spatial_turned"], 2)
                v.tensor_copy(ssm_out, pr_ps[0:DH, 0:512]).then_inc(ready, 1)
                steps_of["dve"] = step

        with ExitStack() as sctx:
            ssb_, _ = new_pools(nc, sctx)
            W1 = DH + 1
            scope = {
                "sample": True, "mask": c["tri_s"], "ws_t": ssb_("ws_t_s", [P, H, P]), "bs": ssb_("bs_s", [P, H]),
                "cst": ssb_("cst_s", [DH, H, NB, W1]), "hst": ssb_("hst_s", [P, H, NB, DH]), "m0": ssb_("m0_s", [H, NB]),
                "wide": ssb_("wide_m", [P, NB, W1]), "vws": [ssb_(f"vws{n}", [P, NB * W1]) for n in range(2)],
                "n2_done": sem("ms_wide_done"), "n2_used": sem("ms_wide_used"), "vws_done": sem("ms_vws_done"),
                "xt_ready": sem("ms_xt_ready"),
            }
            cst, hst, m0 = scope["cst"], scope["hst"], scope["m0"]
            ssm = ssb_("ssm_rows", [DH, NB * H, P])
            ws_rows, bs_rows = ssb_("ws_rows", [TS, H, TS]), ssb_("bs_rows", [TS, H])
            ws_wide, repeat = ssb_("ws_wide", [P, H, P]), ssb_("repeat", [TS, P])
            conv_rows, tails = ssb_("conv_rows", [3 * NB, XW]), ssb_("conv_tails", [P, KX, NB, 3])
            n_in = 3 + 2 * H
            s_in, s_ssm, s_t, s_k, s_wide = (sem("ms_in"), sem("ms_ssm_loaded"), sem("ms_turned"), sem("ms_kept"),
                                             sem("ms_spatial_spread"))
            s_repeat, s_rows, s_xt, s_tails = (sem("ms_repeat_made"), sem("ms_conv_rows_loaded"), sem("ms_xt_loaded"),
                                               sem("ms_conv_tails"))
            tensor_iteration, scalar_iteration, pool_iteration, vector_iteration = engines(scope)
            xt_view = xt[0][:].rearrange("p (k b t) -> p k b t", k=KX, b=NB)
            block = sctx.enter_context(nc.Block())

            @block.sync
            def _(sp):
                sp.dma_start(ssm[:], A["state_c_ssm"][0].rearrange("b h p n -> p (b h) n")).then_inc(s_ssm, 16)
                sp.dma_start(ws_rows[:], A["d_w_s"][0, :, 0:TS, 0:TS].rearrange("g t s -> t g s")).then_inc(s_in, 16)
                sp.dma_start(bs_rows[:], A["d_b_s"][0, :, 0:TS].rearrange("g t -> t g"), allow_slow_non_contiguous=True
                             ).then_inc(s_in, 16)
                sp.dma_start(conv_rows[:], A["state_c_conv"][0].rearrange("b j n -> (b j) n")).then_inc(s_rows, 16)
                for k in range(KX):
                    sp.dma_start(xt_view[:, k, :, 3:], S["xbc_s"][:, k, :].rearrange("p (b t) -> p b t", b=NB)
                                 ).then_inc(s_xt, 16)
                for h in range(H):
                    sp.dma_start(cst[:, h, :, 0:DH], A["state_b_c"][0, :, h].rearrange("b d e -> d b e")).then_inc(s_in, 16)
                    sp.dma_start(cst[:, h, :, DH], A["state_b_n"][0, :, h].rearrange("b d -> d b"),
                                 allow_slow_non_contiguous=True).then_inc(s_in, 16)
                sp.dma_start(m0[:], A["state_b_m"][0].rearrange("b h -> h b"), allow_slow_non_contiguous=True
                             ).then_inc(s_in, 16)
                third = (PW - IB) // 3
                for n in range(3):
                    sp.dma_start(pt_a[0][:, 2 * GW + n * third:2 * GW + (n + 1) * third],
                                 S["proj"][SEQ:SEQ + P, IB + n * third:IB + (n + 1) * third]).then_inc(s_load_a[0], 16)
                sp.dma_start(pt_b[0][:], S["proj"][SEQ:SEQ + P, QB:IB]).then_inc(s_load_b[0], 16)
                sp.dma_start(xr[:], A["x_sample"].rearrange("b t d -> (b t) d")).then_inc(E["xres_loaded"], 16)
                sp.wait_ge(s_tails, 2)
                sp.dma_start(O["s_c_conv"][0].rearrange("b j n -> (b j) n"), conv_rows[:]).then_inc(s_final2, 16)
                sp.wait_ge(E["h2_half"], 2 * (NT + 1))
                out = [(S["h2t"][:, :, SEQ:SEQ + P], yt[:]), (S["x2"][SEQ:SEQ + P, :], xr[:]),
                       (O["s_d_v"][0].rearrange("b t d -> (b t) d"), vn[:]),
                       (O["s_b_m"][0].rearrange("b h -> h b"), m0[:])]
                for h in range(H):
                    out.append((O["s_b_c"][0, :, h].rearrange("b d e -> d b e"), cst[:, h, :, 0:DH]))
                    out.append((O["s_b_n"][0, :, h].rearrange("b d -> d b"), cst[:, h, :, DH]))
                for dst, src in out:
                    sp.dma_start(dst, src, allow_slow_non_contiguous=True).then_inc(s_final2, 16)
                sp.wait_ge(s_k, 5 + NB)
                sp.dma_start(O["s_c_ssm"][0].rearrange("b h p n -> p (b h) n"), ssm[:]).then_inc(s_final2, 16)
                sp.wait_ge(s_final2, 16 * (len(out) + 2))

            @block.tensor
            def _(pe):
                pe.wait_ge(s_ssm, 16)
                for h in range(H):
                    if h >= 2:
                        pe.wait_ge(s_k, h - 1)
                    for b in range(NB):
                        last = nc.tensor.transpose(sc_ps[:, h % 2 * 512 + b * DH:h % 2 * 512 + (b + 1) * DH], ssm[:, b * H + h, :],
                                                   c["ident"][0:DH, 0:DH])
                    last.then_inc(s_t, 1)
                pe.wait_ge(s_in, 16 * n_in)
                pe.wait_ge(s_repeat, 1)
                nc.tensor.matmul(b23[:, 0:H * TS], repeat[:], ws_rows[:].rearrange("t g s -> t (g s)"), start=True, stop=True)
                nc.tensor.matmul(b23[:, H * TS:H * TS + H], repeat[:], bs_rows[:], start=True, stop=True).then_inc(s_t, 1)
                pe.wait_ge(s_rows, 16)
                for k in range(KX):
                    last = nc.tensor.transpose(b23[:, 512 + k * 3 * NB:512 + (k + 1) * 3 * NB],
                                               conv_rows[:, k * P:(k + 1) * P], c["ident"][0:3 * NB, 0:3 * NB])
                last.then_inc(s_t, 1)
                pe.wait_ge(s_tails, 1)
                for k in range(KX):
                    last = nc.tensor.transpose(pr_ps[0:3 * NB, k * P:(k + 1) * P],
                                               tails[:, k].rearrange("p b j -> p (b j)"), c["ident"][:])
                last.then_inc(s_t, 1)
                pe.wait_ge(s_wide, 2)
                for g in range(H):
                    last = nc.tensor.transpose(b01[:, g * P:(g + 1) * P], ws_wide[:, g, :], c["ident"][:])
                last.then_inc(s_t, 1)
                pe.wait_ge(s_k, 5)
                pe.wait_ge(s_tails, 2)
                sample_iterations(pe, tensor_iteration)
                for b in range(NB):
                    if b >= 2:
                        pe.wait_ge(s_k, 5 + b - 1)
                    for h in range(H):
                        last = nc.tensor.transpose(pr_ps[0:DH, b % 2 * 512 + h * P:b % 2 * 512 + (h + 1) * P],
                                                   hst[:, h, b, :], c["ident"][:])
                    last.then_inc(s_t, 1)

            @block.scalar
            def _(act):
                sample_iterations(act, scalar_iteration, steps_of["act"].on(act))

            @block.gpsimd
            def _(pool):
                sample_iterations(pool, pool_iteration, steps_of["pool"].on(pool))

            @block.vector
            def _(dve):
                v = nc.vector
                v.tensor_copy(repeat[:].rearrange("k (b t) -> k b t", b=NB), spread(c["ident"][0:TS, 0:TS], 1, NB)
                              ).then_inc(s_repeat, 1)
                for h in range(H):
                    dve.wait_ge(s_t, h + 1)
                    v.tensor_copy(hst[:, h], sc_ps[:, h % 2 * 512:h % 2 * 512 + 512].rearrange("p (b d) -> p b d", b=NB)).then_inc(s_k, 1)
                dve.wait_ge(s_t, H + 1)
                v.tensor_copy(ws_wide[:].rearrange("p g (b s) -> p g b s", b=NB),
                              spread(b23[:, 0:H * TS].rearrange("p (g s) -> p g s", g=H), 2, NB)).then_inc(s_wide, 1)
                v.tensor_copy(scope["bs"][:], b23[:, H * TS:H * TS + H]).then_inc(s_wide, 1)
                dve.wait_ge(s_xt, 16 * KX)
                v.tensor_copy(tails[:], xt_view[:, :, :, TS:TS + 3]).then_inc(s_tails, 1)
                dve.wait_ge(s_t, H + 2)
                v.tensor_copy(xt_view[:, :, :, 0:3], b23[:, 512:512 + KX * 3 * NB].rearrange("p (k b j) -> p k b j", k=KX, b=NB)
                              ).then_inc(scope["xt_ready"], 1)
                dve.wait_ge(scope["xt_ready"], 1)
                dve.wait_ge(s_t, H + 3)
                v.tensor_copy(conv_rows[:], pr_ps[0:3 * NB, 0:XW]).then_inc(s_tails, 1)
                dve.wait_ge(s_wide, 2)
                dve.wait_ge(s_t, H + 4)
                v.tensor_tensor(scope["ws_t"][:], b01[:, 0:512].rearrange("p (g t) -> p g t", g=H),
                                spread(c["tri_s"][:], 1, H), ALU.mult).then_inc(s_k, 1)
                dve.wait_ge(s_k, 5)
                sample_iterations(dve, vector_iteration, steps_of["dve"].on(dve))
                for b in range(NB):
                    dve.wait_ge(s_t, H + 5 + b)
                    v.tensor_copy(ssm[:, b * H:(b + 1) * H, :],
                                  pr_ps[0:DH, b % 2 * 512:b % 2 * 512 + 512].rearrange("p (h n) -> p h n", h=H)
                                  ).then_inc(s_k, 1)


def feed_forward(nc, sem, A, O, S, c, keep):
    with ExitStack() as ctx:
        sb, ps = new_pools(nc, ctx)
        spans = [(0, 768, [(0, 384), (384, 384)]), (768, 768, [(0, 384), (384, 384)]),
                 (1536, 512, [(0, 320), (320, 320)])]
        NSP, MAXT, HALF = len(spans), 768, 384
        NCH, NPASS = 2, 2
        TP = HALF // P
        LAST = NSP - 1
        h2_hi, h2_lo = sb("h2_hi", [P, KD, MAXT], F32R), sb("h2_lo", [P, KD, MAXT], F32R)
        h2_raw = sb("h2_raw", [P, MAXT])
        mid = sb("mid", [P, KF, MAXT])
        m_hi, m_lo = ([sb(f"mid_{n}{j}", [P, HALF], F32R) for j in range(2)] for n in ("hi", "lo"))
        raw = [sb(f"w_raw{j}", [P, D]) for j in range(2)]
        w_hi, w_lo = ([sb(f"w_{n}{j}", [P, D], F32R) for j in range(2)] for n in ("hi", "lo"))
        g_buf, g_s = sb("g_buf", [P, 2 + MAXT]), sb("g_s", [P, NB, 2 + TS])
        conv, gate_on = sb("conv", [P, MAXT]), sb("gate_on", [P, MAXT])
        taps, tap = sb("taps", [P, KF, 4]), sb("tap", [P, 4])
        tail = sb("tail", [P, KF, 18])
        hist = sb("hist", [P, KF, 16])
        xr = [sb(f"xr{j}", [P, D]) for j in range(2)]
        ffn_gate = sb("ffn_gate_in", [P, 2, D])
        y, prod = sb("y", [P, D]), [sb(f"prod{j}", [P, D]) for j in range(2)]
        g_fin = sb("g_fin", [P, D])
        ss, mean, rstd = sb("ff_ss", [P, 2]), sb("ff_mean", [P, 2]), sb("ff_rstd", [P, 2])
        h2_first = mid[:, KD:2 * KD, :]
        flat = mid[:].rearrange("p f t -> p (f t)")
        rows_in, rows_out = flat[0:16, 0:FF], flat[0:18, 0:FF]
        acc = ps("acc_ps", [P, 4, 2, 512])
        g_ps, u_ps = acc[:, 0], acc[:, 1]
        pair_of = [2, 3, 0, 1, 2, 3]

        s_par, s_hist, s_h2 = sem("ff_params"), sem("ff_history"), sem("h2_piece_loaded")
        s_h2f = [sem(f"h2_first_loaded{n}") for n in range(4)]
        s_h2hi, s_h2lo = sem("h2_hi_done"), sem("h2_lo_done")
        s_raw, s_hi, s_lo, s_used = ([sem(f"w_{n}{j}") for j in range(2)] for n in ("loaded", "hi_done", "lo_done", "used"))
        s_mhi, s_mlo = sem("mid_hi_done"), sem("mid_lo_done")
        s_xr = [sem(f"xr_loaded{j}") for j in range(2)]
        s_ht, s_hk, s_gk, s_mid = sem("hist_turned"), sem("hist_kept"), sem("g_kept"), sem("mid_done")
        s_conv, s_on = sem("ff_conv_done"), sem("gate_on_done")
        s_x3, s_ss, s_mean, s_rstd, s_y = sem("x3_done"), sem("ff_squares"), sem("ff_mean"), sem("ff_rstd"), sem("y_done")
        s_read = sem("down_read")
        s_dve, s_store, s_tail, s_tk = sem("ff_dve"), sem("y_stored"), sem("tail_turned"), sem("tail_kept")
        s_tout = sem("tail_stored")

        wg = A["f_w_gate"][0].rearrange("(k p) (f c) -> f p k c", p=P, c=P)
        wu = A["f_w_up"][0].rearrange("(k p) (f c) -> f p k c", p=P, c=P)
        wd = A["f_w_down"][0].rearrange("(f p) n -> f p n", p=P)
        n_tiles = [sum(w for _, w in ch) // P for _, _, ch in spans]
        first_tile = [sum(n_tiles[:s]) for s in range(NSP)]
        SLOT = KF + NPASS * KF // 2

        def unit(s, f):
            return f + s * SLOT

        def down_unit(s, a, q):
            return q + (s * SLOT + KF + a * KF // 2)

        def tiles_of(s, a):
            return list(range(first_tile[s] + a * TP, min(first_tile[s] + (a + 1) * TP, first_tile[s] + n_tiles[s])))

        def before(s, a):
            if a is None:
                return tiles_of(s - 1, 1) if s else []
            return tiles_of(s, 0) if a == 1 else []

        def at_f(ap, f):
            return ap[:, f] if isinstance(f, int) else ap[:, bass.ds(f, 1)].rearrange("p o n -> p (o n)")

        def pieces(s, a):
            return a == 0 and s < LAST

        def static_until(s, a):
            if pieces(s, a):
                return 1, 1 + KD
            return 3, KF // 2 - 1

        block = ctx.enter_context(nc.Block())

        @block.sync
        def _(sp):
            def load_gu(s, f, first=False):
                for j, w in enumerate((wg, wu)):
                    if not first:
                        sp.wait_ge(s_lo[j], unit(s, f))
                    sp.dma_start(raw[j][:].rearrange("p (k c) -> p k c", k=KD), w[f] if isinstance(f, int) else
                                 w[bass.ds(f, 1)].rearrange("o p k c -> (o p) k c")).then_inc(s_raw[j], 16)

            def load_dn(s, a, q, j):
                f = q * 2 + j
                sp.wait_ge(s_lo[j], down_unit(s, a, q))
                sp.dma_start(raw[j][:], wd[f] if isinstance(f, int) else
                             wd[bass.ds(f, 1)].rearrange("o p n -> (o p) n")).then_inc(s_raw[j], 16)

            def load_xr(i):
                sp.dma_start(xr[i % 2][:], S["x2"][i * P:(i + 1) * P, :]).then_inc(s_xr[i % 2], 16)

            def load_piece(s, k):
                t0, n = spans[s + 1][0], sum(w for _, w in spans[s + 1][2])
                sp.wait_ge(s_h2lo, k + KD * (s + 1))
                src = S["h2t"][:, bass.ds(k, 1), t0:t0 + n].rearrange("p o t -> p (o t)")
                sp.dma_start(h2_raw[:, 0:n], src).then_inc(s_h2, 16)

            def store(i):
                sp.wait_ge(s_y, i + 1)
                dst = O["y_prompt"][0, i * P:(i + 1) * P, :] if i < NT else O["y_sample"].rearrange("b t d -> (b t) d")
                sp.dma_start(dst, y[:]).then_inc(s_store, 16)
                if i + 2 <= NT:
                    load_xr(i + 2)

            for n in range(4):
                sp.dma_start(h2_first[:, 2 * n:2 * n + 2, :], S["h2t"][:, 2 * n:2 * n + 2, 0:MAXT]).then_inc(s_h2f[n], 16)
                if n == 0:
                    load_gu(0, 0, first=True)
            sp.dma_start(rows_in, A["state_ffn_conv"][0].rearrange("b j n -> (b j) n")).then_inc(s_hist, 16)
            for j in range(3):
                sp.dma_start(taps[:, :, j], A["f_conv_w"][0, j].rearrange("(f p) -> p f", p=P),
                             allow_slow_non_contiguous=True).then_inc(s_par, 16)
            sp.dma_start(taps[:, :, 3], A["f_conv_b"][0].rearrange("(f p) -> p f", p=P),
                         allow_slow_non_contiguous=True).then_inc(s_par, 16)
            sp.dma_start(g_fin[:], A["g_final"].partition_broadcast(P)).then_inc(s_par, 16)
            sp.dma_start(ffn_gate[:], S["ffn_gate"]).then_inc(s_par, 16)
            load_xr(0)
            load_xr(1)
            for s in range(NSP):
                for f in range(6):
                    if s or f:
                        load_gu(s, f)
                    if f >= 3 and f - 3 < len(before(s, None)):
                        store(before(s, None)[f - 3])
                with sp.Fori(3, KF // 2) as q:
                    load_gu(s, q * 2)
                    load_gu(s, q * 2 + 1)
                for a in range(NPASS):
                    lo, hi = static_until(s, a)
                    for f in range(2 * lo):
                        load_dn(s, a, f // 2, f % 2)
                        if f >= 3 and f - 3 < len(before(s, a)):
                            store(before(s, a)[f - 3])
                    with sp.Fori(lo, hi) as q:
                        load_dn(s, a, q, 0)
                        load_dn(s, a, q, 1)
                        if pieces(s, a):
                            load_piece(s, q - 1)
                    for f in range(2 * hi, KF):
                        load_dn(s, a, f // 2, f % 2)
            for i in tiles_of(LAST, 1):
                store(i)
            sp.wait_ge(s_tk, 6)
            sp.dma_start(O["s_ffn_conv"][0].rearrange("b j n -> (b j) n"), rows_out[0:16]).then_inc(s_tout, 16)
            sp.dma_start(O["p_ffn_conv"][0, 0], rows_out[16:18]).then_inc(s_tout, 16)
            sp.wait_ge(s_tout, 32)
            sp.wait_ge(s_store, 16 * (NT + 1))

        @block.tensor
        def _(pe):
            t = nc.tensor

            def gate_or_up(s, out, j, pieces_wait):
                for b, (at, width) in enumerate(spans[s][2]):
                    for k in range(KD):
                        if pieces_wait and b == 0:
                            pe.wait_ge(s_h2lo, KD * s + k + 1)
                        hi, lo = w_hi[j][:, k * P:(k + 1) * P], w_lo[j][:, k * P:(k + 1) * P]
                        dst, cols = out[:, b, 0:width], slice(at, at + width)
                        t.matmul(dst, hi, h2_hi[:, k, cols], start=(k == 0), stop=False)
                        t.matmul(dst, hi, h2_lo[:, k, cols], start=False, stop=False)
                        last = t.matmul(dst, lo, h2_hi[:, k, cols], start=False, stop=(k == KD - 1))
                return last

            def step(s, q, j):
                f = q * 2 + j
                n_th = f + s * KF
                start = isinstance(f, int) and f == 0
                pe.wait_ge(s_lo[0], unit(s, f) + 1)
                if not (start and s == 0):
                    pe.wait_ge(s_gk, n_th)
                if start and s:
                    pe.wait_ge(s_read, first_tile[s - 1] + 3)
                gate_or_up(s, g_ps, 0, start).then_inc(s_used[0], 1)
                pe.wait_ge(s_lo[1], unit(s, f) + 1)
                if not (start and s == 0):
                    pe.wait_ge(s_mid, n_th)
                if start and s:
                    pe.wait_ge(s_read, first_tile[s - 1] + 4)
                gate_or_up(s, u_ps, 1, False).then_inc(s_used[1], 1)

            def down_step(s, a, q, j):
                f = q * 2 + j
                start, stop = (isinstance(f, int) and f == e for e in (0, KF - 1))
                pe.wait_ge(s_mlo, f + ((s * NPASS + a) * KF + 1))
                for n, i in enumerate(tiles_of(s, a)):
                    k = i - first_tile[s]
                    pair = pair_of[k]
                    if start:
                        if pair == 0:
                            pe.wait_ge(s_gk, (s + 1) * KF)
                        elif pair == 1:
                            pe.wait_ge(s_mid, (s + 1) * KF)
                        elif a == 1:
                            pe.wait_ge(s_read, first_tile[s] + pair - 1)
                        elif s:
                            pe.wait_ge(s_read, first_tile[s - 1] + pair + 3)
                        elif pair == 3:
                            pe.wait_ge(s_hk, 1)
                    cols = slice(n * P, (n + 1) * P)
                    for lhs, rhs, begin in ((m_hi, w_hi, start), (m_hi, w_lo, False), (m_lo, w_hi, False)):
                        for half in range(2):
                            last = t.matmul(acc[:, pair, half, :], lhs[j][:, cols], rhs[j][:, half * 512:(half + 1) * 512],
                                            start=begin, stop=(stop and lhs is m_lo))
                last.then_inc(s_used[j], 1)

            def turn_tail(r, ready):
                if ready:
                    pe.wait_ge(*ready)
                for f in range(4 * r, min(4 * r + 4, KF)):
                    last = t.transpose(acc[0:18, (0, 3)[r % 4 // 2], r % 2, f % 4 * P:(f % 4 + 1) * P], tail[:, f, :],
                                       c["ident"][:])
                last.then_inc(s_tail, 1)

            pe.wait_ge(s_hist, 16)
            for f in range(KF):
                last = t.transpose(acc[:, 3, 0, f * 16:(f + 1) * 16], rows_in[:, f * P:(f + 1) * P], c["ident"][0:16, 0:16])
            last.then_inc(s_ht, 1)
            for s in range(NSP):
                for f in range(6):
                    step(s, f // 2, f % 2)
                with pe.Fori(3, KF // 2) as q:
                    step(s, q, 0)
                    step(s, q, 1)
                for a in range(NPASS):
                    lo, hi = static_until(s, a)
                    for f in range(2 * lo):
                        down_step(s, a, f // 2, f % 2)
                    if s == LAST and a == 1:
                        for r in range(4):
                            turn_tail(r, (s_read, first_tile[s] + 3))
                    with pe.Fori(lo, hi) as q:
                        down_step(s, a, q, 0)
                        down_step(s, a, q, 1)
                    if s == LAST and a == 1:
                        for r in range(4, 6):
                            turn_tail(r, (s_tk, r - 3))
                    for f in range(2 * hi, KF):
                        down_step(s, a, f // 2, f % 2)

        @block.scalar
        def _(act):
            a_ = nc.scalar

            def split(j, n):
                act.wait_ge(s_raw[j], n * 16 + 16)
                if not (isinstance(n, int) and n == 0):
                    act.wait_ge(s_used[j], n)
                a_.activation(w_hi[j][:], raw[j][:], ACT.Copy).then_inc(s_hi[j], 1)

            def keep_g(s, f):
                n_th = f + s * KF
                act.wait_ge(s_used[0], unit(s, f) + 1)
                if not (isinstance(n_th, int) and n_th == 0):
                    act.wait_ge(s_conv, n_th)
                for b, (at, width) in enumerate(spans[s][2]):
                    prompt = min(width, spans[s][1] - at)
                    last = a_.activation(g_buf[:, 2 + at:2 + at + prompt], g_ps[:, b, 0:prompt], ACT.Copy)
                    if prompt < width:
                        last = a_.activation(g_s[:, :, 2:],
                                             g_ps[:, b, prompt:width].rearrange("p (n t) -> p n t", n=NB), ACT.Copy)
                last.then_inc(s_gk, 1)
                act.wait_ge(s_conv, n_th + 1)
                if not (isinstance(n_th, int) and n_th == 0):
                    act.wait_ge(s_mid, n_th)
                width = sum(w for _, w in spans[s][2])
                a_.activation(gate_on[:, 0:width], conv[:, 0:width], ACT.Silu).then_inc(s_on, 1)

            def step(s, f, last=None):
                split(0, unit(s, f))
                if last is not None:
                    keep_g(s, last)
                split(1, unit(s, f))

            def down_step(s, a, q, j):
                f = q * 2 + j
                split(j, down_unit(s, a, q))
                width = len(tiles_of(s, a)) * P
                a_.activation(m_hi[j][:, 0:width], at_f(mid, f)[:, a * HALF:a * HALF + width], ACT.Copy
                              ).then_inc(s_mhi, 1)

            def squares(i):
                act.wait_ge(s_x3, i + 1)
                a_.activation(prod[i % 2][:], xr[i % 2][:], ACT.Square, accum_out=ss[:, i % 2:i % 2 + 1]).then_inc(s_ss, 1)

            def tile_part(k, tiles):
                if 1 <= k <= len(tiles):
                    squares(tiles[k - 1])

            for k in range(KD):
                act.wait_ge(s_h2f[k // 2], 16)
                a_.activation(h2_hi[:, k, :], h2_first[:, k, :], ACT.Copy).then_inc(s_h2hi, 1)
                if k == 0:
                    split(0, 0)
            for s in range(NSP):
                for f in range(6):
                    if s == 0 and f == 0:
                        split(1, 0)
                    else:
                        step(s, f, f - 1 if f else None)
                    tile_part(f, before(s, None))
                with act.Fori(3, KF // 2) as q:
                    step(s, q * 2, q * 2 - 1)
                    step(s, q * 2 + 1, q * 2)
                for a in range(NPASS):
                    lo, hi = static_until(s, a)
                    for f in range(2 * lo):
                        down_step(s, a, f // 2, f % 2)
                        if a == 0 and f == 0:
                            keep_g(s, KF - 1)
                        tile_part(f, before(s, a))
                    with act.Fori(lo, hi) as q:
                        down_step(s, a, q, 0)
                        down_step(s, a, q, 1)
                        if pieces(s, a):
                            n = sum(w for _, w in spans[s + 1][2])
                            act.wait_ge(s_h2, (q - 1) * 16 + (KD * 16 * s + 16))
                            a_.activation(at_f(h2_hi, q - 1)[:, 0:n], h2_raw[:, 0:n], ACT.Copy).then_inc(s_h2hi, 1)
                    for f in range(2 * hi, KF):
                        down_step(s, a, f // 2, f % 2)
            for k in range(3):
                tile_part(k, tiles_of(LAST, 1))

        @block.gpsimd
        def _(pool):
            for i in range(NT + 1):
                j = i % 2
                pool.wait_ge(s_ss, i + 1)
                nc.gpsimd.tensor_scalar(mean[:, j:j + 1], ss[:, j:j + 1], 1.0 / D, EPS, ALU.mult, ALU.add
                                        ).then_inc(s_mean, 1)
                pool.wait_ge(s_mean, i + 1)
                nc.gpsimd.tensor_tensor(rstd[:, j:j + 1], mean[:, j:j + 1], c["minus_half"][:, 0:1], ALU.pow
                                        ).then_inc(s_rstd, 1)

        @block.vector
        def _(dve):
            v = nc.vector
            own = Steps(dve, s_dve)

            def split(j, n):
                dve.wait_ge(s_hi[j], n + 1)
                v.tensor_tensor(w_lo[j][:], raw[j][:], w_hi[j][:], ALU.subtract).then_inc(s_lo[j], 1)

            def convolve(s, f):
                n, sample = spans[s][1], s == LAST
                own(v.tensor_copy(tap[:], at_f(taps, f)))
                if s:
                    own(v.tensor_copy(g_buf[:, 0:2], at_f(tail, f)[:, 16:18]))
                if sample:
                    own(v.tensor_copy(g_s[:, :, 0:2], at_f(hist, f).rearrange("p (b j) -> p b j", b=NB)))
                own.settle()
                dve.wait_ge(s_gk, f + (s * KF + 1))
                gs = g_s[:]
                cs = conv[:, n:n + P].rearrange("p (b t) -> p b t", b=NB) if sample else None
                own(v.tensor_scalar(conv[:, 0:n], g_buf[:, 0:n], tap[:, 0:1], tap[:, 3:4], ALU.mult, ALU.add))
                if sample:
                    own(v.tensor_scalar(cs, gs[:, :, 0:TS], tap[:, 0:1], tap[:, 3:4], ALU.mult, ALU.add))
                own.settle()
                own(v.scalar_tensor_tensor(conv[:, 0:n], g_buf[:, 1:n + 1], tap[:, 1:2], conv[:, 0:n],
                                           ALU.mult, ALU.add))
                if sample:
                    v.scalar_tensor_tensor(cs, gs[:, :, 1:TS + 1], tap[:, 1:2], cs, ALU.mult, ALU.add)
                    v.tensor_copy(at_f(tail, f)[:, 0:16].rearrange("p (b j) -> p b j", b=NB), gs[:, :, TS:TS + 2])
                own(v.tensor_copy(at_f(tail, f)[:, 16:18], g_buf[:, n:n + 2]))
                own.settle()
                if sample:
                    v.scalar_tensor_tensor(cs, gs[:, :, 2:TS + 2], tap[:, 2:3], cs, ALU.mult, ALU.add)
                v.scalar_tensor_tensor(conv[:, 0:n], g_buf[:, 2:n + 2], tap[:, 2:3], conv[:, 0:n],
                                       ALU.mult, ALU.add).then_inc(s_conv, 1)

            def multiply(s, f):
                dve.wait_ge(s_on, f + (s * KF + 1))
                dve.wait_ge(s_used[1], unit(s, f) + 1)
                for b, (at, w) in enumerate(spans[s][2]):
                    last = v.tensor_tensor(at_f(mid, f)[:, at:at + w], gate_on[:, at:at + w], u_ps[:, b, 0:w], ALU.mult)
                last.then_inc(s_mid, 1)

            def step(s, f, last=None):
                split(0, unit(s, f))
                if last is not None:
                    convolve(s, last)
                    multiply(s, last)
                split(1, unit(s, f))

            def down_step(s, a, q, j):
                f = q * 2 + j
                split(j, down_unit(s, a, q))
                width = len(tiles_of(s, a)) * P
                dve.wait_ge(s_mhi, f + ((s * NPASS + a) * KF + 1))
                v.tensor_tensor(m_lo[j][:, 0:width], at_f(mid, f)[:, a * HALF:a * HALF + width], m_hi[j][:, 0:width],
                                ALU.subtract).then_inc(s_mlo, 1)

            def gated(i):
                s = max(n for n in range(NSP) if first_tile[n] <= i)
                a = (i - first_tile[s]) // TP
                dve.wait_ge(s_used[1], down_unit(s, a, KF // 2 - 1) + 1)
                if i >= 2:
                    dve.wait_ge(s_ss, i - 1)
                v.tensor_tensor(prod[i % 2][:], acc[:, pair_of[i - first_tile[s]]].rearrange("p a n -> p (a n)"),
                                ffn_gate[:, 1 if i == NT else 0, :], ALU.mult).then_inc(s_read, 1)

            def residual(i):
                dve.wait_ge(s_read, i + 1)
                dve.wait_ge(s_xr[i % 2], 16 * (i // 2 + 1))
                v.tensor_tensor(xr[i % 2][:], xr[i % 2][:], prod[i % 2][:], ALU.add).then_inc(s_x3, 1)

            def finish(i):
                dve.wait_ge(s_rstd, i + 1)
                if i:
                    dve.wait_ge(s_store, 16 * i)
                v.scalar_tensor_tensor(y[:], xr[i % 2][:], rstd[:, i % 2:i % 2 + 1], g_fin[:], ALU.mult, ALU.mult
                                       ).then_inc(s_y, 1)

            def tile_part(k, tiles):
                if k == 0:
                    for i in tiles[:2]:
                        gated(i)
                if 1 <= k <= len(tiles):
                    residual(tiles[k - 1])
                if k == 2 and len(tiles) > 2:
                    gated(tiles[2])
                if 2 <= k <= len(tiles) + 1:
                    finish(tiles[k - 2])

            def keep_tail(r):
                dve.wait_ge(s_tail, r + 1)
                w = min(4, KF - 4 * r) * P
                v.tensor_copy(rows_out[:, r * 512:r * 512 + w], acc[0:18, (0, 3)[r % 4 // 2], r % 2, 0:w]).then_inc(s_tk, 1)

            dve.wait_ge(s_ht, 1)
            v.tensor_copy(hist[:], acc[:, 3, 0, 0:KF * 16].rearrange("p (f n) -> p f n", f=KF)).then_inc(s_hk, 1)
            own(v.memset(g_buf[:, 0:2], 0.0))
            for k in range(KD):
                dve.wait_ge(s_h2hi, k + 1)
                v.tensor_tensor(h2_lo[:, k, :], h2_first[:, k, :], h2_hi[:, k, :], ALU.subtract).then_inc(s_h2lo, 1)
                if k == 0:
                    split(0, 0)
            dve.wait_ge(s_par, 16 * 6)
            for s in range(NSP):
                for f in range(6):
                    if s == 0 and f == 0:
                        split(1, 0)
                    else:
                        step(s, f, f - 1 if f else None)
                    tile_part(f, before(s, None))
                PER = 2 * (4 + (s > 0) + 2 * (s == LAST))
                with dve.Fori(3, KF // 2) as q:
                    own.enter(q, 3, PER)
                    step(s, q * 2, q * 2 - 1)
                    step(s, q * 2 + 1, q * 2)
                own.leave(KF // 2 - 3, PER)
                for a in range(NPASS):
                    lo, hi = static_until(s, a)
                    for f in range(2 * lo):
                        down_step(s, a, f // 2, f % 2)
                        if a == 0 and f == 0:
                            convolve(s, KF - 1)
                            multiply(s, KF - 1)
                        tile_part(f, before(s, a))
                    if s == LAST and a == 1:
                        for r in range(4):
                            keep_tail(r)
                    with dve.Fori(lo, hi) as q:
                        down_step(s, a, q, 0)
                        down_step(s, a, q, 1)
                        if pieces(s, a):
                            n = sum(w for _, w in spans[s + 1][2])
                            dve.wait_ge(s_h2hi, q + KD * (s + 1))
                            v.tensor_tensor(at_f(h2_lo, q - 1)[:, 0:n], h2_raw[:, 0:n], at_f(h2_hi, q - 1)[:, 0:n],
                                            ALU.subtract).then_inc(s_h2lo, 1)
                    if s == LAST and a == 1:
                        for r in range(4, 6):
                            keep_tail(r)
                    for f in range(2 * hi, KF):
                        down_step(s, a, f // 2, f % 2)
            for k in range(4):
                tile_part(k, tiles_of(LAST, 1))


def bass_hybrid_chunk_streaming_encoder_step_kernel(nc, A, O):
    with ExitStack() as ctx:
        sb, _ = new_pools(nc, ctx)
        sem = Semaphores(nc)
        S = {name: nc.dram_tensor("scratch_" + name, shape, F32, kind="Internal").ap() for name, shape in {
            "proj": (SEQ + P, PW), "xbc": (P, KX, SEQ + 3), "xbc_s": (P, KX, P), "h2t": (P, KD, SEQ + P),
            "x2": (SEQ + P, D), "ffn_gate": (P, 2, D), "rel_row": (H, 768), "rel": (H, P, 768)}.items()}
        c, const_program = make_constants(nc, sb, sem)
        sem.constants_cut = sem["const_cut"]
        keep = {name: sb(name, [P, KD, 1 + NB]) for name in ("mix_scale", "mix_shift", "ffn_scale", "ffn_shift")}
        with ExitStack() as first:
            sb1, _ = new_pools(nc, first)
            keep["mix_gate"] = sb1("mix_gate", [P, 2, D])
            ya_sample = sb1("ya_sample", [P, GW])
            rel_bias_rows(nc, sem, A, S)
            with ExitStack() as second:
                sb2, _ = new_pools(nc, second)
                w_in_sb = sb2("w_in_sb", [P, KD * WIN + 520])
                modulation(nc, sem, A, S, c, const_program, keep, w_in_sb)
                projection(nc, sem, A, S, c, keep, w_in_sb)
            sem.give_back()
            sample_attention(nc, sem, A, S, c, ya_sample)
            mixers(nc, sem, A, O, S, c, keep, ya_sample)
        sem.give_back()
        feed_forward(nc, sem, A, O, S, c, keep)


class Semaphores:

    def __init__(self, nc):
        self.nc, self.made, self.group = nc, {}, []

    def give_back(self):
        self.nc.clear_and_free_semaphores(self.group)
        self.nc.all_engine_barrier()
        self.group = []

    def __call__(self, name):
        assert name not in self.made, name
        self.made[name] = self.nc.alloc_semaphore(name=name)
        self.group.append(self.made[name])
        return self.made[name]

    def __getitem__(self, name):
        return self.made[name]


_INS = ["x_prompt", "x_sample", "c_prompt", "c_sample", "cache_a_k", "cache_a_v", "state_b_c", "state_b_n", "state_b_m",
        "state_c_ssm", "state_c_conv", "state_ffn_conv", "w_ada", "b_ada", "g_norm_mix", "g_norm_ffn", "w_in", "w_out",
        "a_rel_bias", "b_i_bias", "b_f_bias", "b_norm_g", "c_conv_w", "c_conv_b", "c_dt_bias", "c_a_log", "c_d_skip",
        "c_norm_g", "d_norm_g", "d_w_s", "d_b_s", "f_w_gate", "f_w_up", "f_conv_w", "f_conv_b", "f_w_down", "g_final"]
_OUTS = {
    "y_prompt": (1, SEQ, D), "y_sample": (NB, TS, D), "p_a_k": (1, 1, HIST, H, DH), "p_a_v": (1, 1, HIST, H, DH),
    "p_b_c": (1, 1, H, DH, DH), "p_b_n": (1, 1, H, DH), "p_b_m": (1, 1, H), "p_c_ssm": (1, 1, H, DH, NSTATE),
    "p_c_conv": (1, 1, 3, XW), "p_ffn_conv": (1, 1, 2, FF), "s_a_k": (1, NB, TS, H, DH), "s_a_v": (1, NB, TS, H, DH),
    "s_b_c": (1, NB, H, DH, DH), "s_b_n": (1, NB, H, DH), "s_b_m": (1, NB, H), "s_c_ssm": (1, NB, H, DH, NSTATE),
    "s_c_conv": (1, NB, 3, XW), "s_ffn_conv": (1, NB, 2, FF), "s_d_v": (1, NB, TS, GW)}


def kernel(**inputs):
    import numpy as _np
    import concourse.bacc as _bacc
    from concourse.bass_utils import run_bass_kernel_spmd as _run

    nc = _bacc.Bacc("TRN2", target_bir_lowering=False, num_devices=1)
    arrays, A = {}, {}
    for name in _INS:
        a = _np.ascontiguousarray(inputs[name])
        if name == "a_rel_bias":
            name = "a_rel_bias_reversed"
            a = _np.ascontiguousarray(a[:, :, ::-1])
        arrays[f"in_{name}"] = a
        A[name] = nc.dram_tensor(f"in_{name}", a.shape, F32, kind="ExternalInput").ap()
    O = {name: nc.dram_tensor(f"out_{name}", shape, F32, kind="ExternalOutput").ap() for name, shape in _OUTS.items()}
    bass_hybrid_chunk_streaming_encoder_step_kernel(nc, A, O)
    r = _run(nc, [arrays], core_ids=[0])
    return tuple(r.results[0][f"out_{name}"] for name in _OUTS)
```
